# Optimizing a Trainium2 kernel written in Bass

```python
import math
import jax, jax.numpy as jnp
from jax import lax
import numpy as np

D_MODEL = 1024
BATCH = 1
SEQ = 512
DEPTH = 1

HG_HEADS = 8
HG_DK = 128
HG_DV = D_MODEL // HG_HEADS
HG_CHUNK = 32

NSA_HEADS = 8
NSA_GROUPS = 2
NSA_REP = NSA_HEADS // NSA_GROUPS
NSA_DK = 128
NSA_DV = 128
CMP_BLOCK = 32
CMP_STRIDE = 16
CMP_HIDDEN = 128
SLC_BLOCK = 64
SLC_TOPK = 16
WINDOW = 512
Q_BLOCK = 64
FORCE_SCORE = 1e4

REL_BUCKETS = 32
REL_MAX_DIST = 128

N_GROUPS = 4
EXP_PER_GROUP = 8
N_EXPERTS = N_GROUPS * EXP_PER_GROUP
TOPK_IN_GROUP = 2
D_EXPERT = D_MODEL // 2
MOE_BLOCK = 128

ALPHA = (2 * DEPTH) ** 0.25
BETA = (8 * DEPTH) ** -0.25

SPLITS = (HG_HEADS * HG_DK, HG_HEADS * HG_DK, HG_HEADS * HG_DV, HG_HEADS * HG_DV,
          NSA_HEADS * NSA_DK,
          NSA_GROUPS * NSA_DK, NSA_GROUPS * NSA_DV,
          NSA_GROUPS * NSA_DK, NSA_GROUPS * NSA_DV,
          NSA_GROUPS * NSA_DK, NSA_GROUPS * NSA_DV,
          3 * NSA_HEADS, D_MODEL, D_MODEL)
D_IN = sum(SPLITS)


def _layer_norm(x, eps=1e-5):
    xf = x.astype(jnp.float32)
    mu = jnp.mean(xf, axis=-1, keepdims=True)
    var = jnp.mean(jnp.square(xf - mu), axis=-1, keepdims=True)
    return ((xf - mu) * lax.rsqrt(var + eps)).astype(x.dtype)

def _rms_norm(x, eps=1e-6):
    xf = x.astype(jnp.float32)
    return (xf * lax.rsqrt(jnp.mean(jnp.square(xf), axis=-1, keepdims=True) + eps)).astype(x.dtype)

def _masked_softmax(logits, mask):
    lf = jnp.where(mask, logits.astype(jnp.float32), -1e30)
    p = jax.nn.softmax(lf, axis=-1)
    return jnp.where(mask, p, 0.0)

def _rel_bucket(dist):
    n = jnp.maximum(dist, 0)
    max_exact = REL_BUCKETS // 2
    nf = jnp.maximum(n, 1).astype(jnp.float32)
    large = max_exact + (jnp.log(nf / max_exact) / math.log(REL_MAX_DIST / max_exact)
                         * (REL_BUCKETS - max_exact)).astype(jnp.int32)
    large = jnp.minimum(large, REL_BUCKETS - 1)
    return jnp.where(n < max_exact, n, large)

def _hgrn2(q, f_raw, v, lb):
    B, T = q.shape[:2]
    N = T // HG_CHUNK
    lb = lb.reshape(HG_HEADS, HG_DK).astype(q.dtype)
    f = lb + (1 - lb) * jax.nn.sigmoid(f_raw)
    log_f = jnp.log(f)
    k = 1 - f

    def chunks(a):
        return a.reshape(B, N, HG_CHUNK, HG_HEADS, a.shape[-1]).transpose(1, 0, 3, 2, 4)

    qc, kc, vc, lfc = chunks(q), chunks(k), chunks(v), chunks(log_f)
    b = jnp.cumsum(lfc, axis=3)
    b_last = b[:, :, :, -1:, :]
    q_in = qc * jnp.exp(b)
    k_in = kc * jnp.exp(-b)
    k_end = kc * jnp.exp(b_last - b)
    causal = jnp.tril(jnp.ones((HG_CHUNK, HG_CHUNK), dtype=bool))
    att = jnp.einsum('nbhid,nbhjd->nbhij', q_in, k_in)
    att = jnp.where(causal, att, 0)
    o_intra = jnp.einsum('nbhij,nbhje->nbhie', att, vc)
    upd = jnp.einsum('nbhcd,nbhce->nbhde', k_end, vc)
    decay = jnp.exp(b_last[:, :, :, 0, :])

    def step(S, xs):
        q_n, dec_n, u_n = xs
        o_n = jnp.einsum('bhcd,bhde->bhce', q_n, S)
        S = dec_n[..., None] * S + u_n
        return S, o_n

    S0 = jnp.zeros((B, HG_HEADS, HG_DK, HG_DV), q.dtype)
    _, o_inter = lax.scan(step, S0, (q_in, decay, upd))
    o = o_intra + o_inter
    return o.transpose(1, 0, 3, 2, 4).reshape(B, T, HG_HEADS, HG_DV)

def _compress(kv, pos, w1, b1, w2):
    B, G, T, d = kv.shape
    r = CMP_BLOCK // CMP_STRIDE
    ns = T // CMP_STRIDE
    sub = kv.reshape(B, G, ns, CMP_STRIDE, d)
    blocks = jnp.concatenate([sub[:, :, j:ns - r + 1 + j] for j in range(r)], axis=3)
    blocks = (blocks + pos).reshape(B, G, ns - r + 1, CMP_BLOCK * d)
    return jax.nn.silu(blocks @ w1 + b1) @ w2

def _nsa(q, kc, vc, ks, vs, kw, vw, gate_raw, rel_bias,
         pos_k, w1_k, b1_k, w2_k, pos_v, w1_v, b1_v, w2_v):
    B, T = q.shape[:2]
    G, R = NSA_GROUPS, NSA_REP
    NQB = T // Q_BLOCK
    NSLC = T // SLC_BLOCK
    NSEL = min(SLC_TOPK, NSLC)
    scale = NSA_DK ** -0.5
    to_g = lambda a: a.transpose(0, 2, 1, 3)

    k_cmp = _compress(to_g(kc), pos_k, w1_k, b1_k, w2_k)
    v_cmp = _compress(to_g(vc), pos_v, w1_v, b1_v, w2_v)
    NC = k_cmp.shape[2]
    cmp_end = jnp.arange(NC) * CMP_STRIDE + CMP_BLOCK - 1
    cs = np.arange(NC) * CMP_STRIDE
    ss = np.arange(NSLC) * SLC_BLOCK
    overlap = jnp.asarray(((cs[:, None] < ss[None, :] + SLC_BLOCK)
                           & (cs[:, None] + CMP_BLOCK > ss[None, :])).astype(np.float32))

    k_slc = to_g(ks).reshape(B, G, NSLC, SLC_BLOCK, NSA_DK)
    v_slc = to_g(vs).reshape(B, G, NSLC, SLC_BLOCK, NSA_DV)
    pad = ((0, 0), (0, 0), (WINDOW, 0), (0, 0))
    k_win = jnp.pad(to_g(kw), pad)
    v_win = jnp.pad(to_g(vw), pad)
    table = rel_bias.reshape(G, R, REL_BUCKETS)
    g_ix = jnp.arange(G)[None, :, None, None, None]
    r_ix = jnp.arange(R)[None, None, :, None, None]
    blk_start = jnp.arange(NSLC) * SLC_BLOCK
    j_ix = jnp.arange(NSLC)

    q_blocks = q.reshape(B, NQB, Q_BLOCK, G, R, NSA_DK).transpose(1, 0, 3, 4, 2, 5)
    gate_blocks = jax.nn.sigmoid(gate_raw).reshape(B, NQB, Q_BLOCK, G, R, 3).transpose(1, 0, 3, 4, 2, 5)
    gather = jax.vmap(jax.vmap(lambda blk, ix: blk[ix]))

    def block_fn(args):
        qb, q_blk, g_blk = args
        t = qb * Q_BLOCK + jnp.arange(Q_BLOCK)
        dist_c = t[:, None] - cmp_end[None, :]
        s_c = jnp.einsum('bgrqd,bgnd->bgrqn', q_blk, k_cmp) * scale + table[:, :, _rel_bucket(dist_c)]
        p_c = _masked_softmax(s_c, dist_c >= 0)
        o_c = jnp.einsum('bgrqn,bgnd->bgrqd', p_c.astype(v_cmp.dtype), v_cmp)
        imp = jnp.einsum('bgqn,nj->bgqj', p_c.sum(axis=2), overlap)
        cur = t // SLC_BLOCK
        forced = (j_ix[None, :] == 0) | (j_ix[None, :] == cur[:, None]) | (j_ix[None, :] == cur[:, None] - 1)
        valid = blk_start[None, :] <= t[:, None]
        score = jnp.where(valid, jnp.where(forced, FORCE_SCORE, imp), -1.0)
        _, idx = lax.top_k(score, NSEL)
        k_sel = gather(k_slc, idx).reshape(B, G, Q_BLOCK, NSEL * SLC_BLOCK, NSA_DK)
        v_sel = gather(v_slc, idx).reshape(B, G, Q_BLOCK, NSEL * SLC_BLOCK, NSA_DV)
        s_pos = (idx[..., None] * SLC_BLOCK + jnp.arange(SLC_BLOCK)).reshape(B, G, Q_BLOCK, NSEL * SLC_BLOCK)
        dist_s = t[None, None, :, None] - s_pos
        s_s = (jnp.einsum('bgrqd,bgqkd->bgrqk', q_blk, k_sel) * scale
               + table[g_ix, r_ix, _rel_bucket(dist_s)[:, :, None]])
        p_s = _masked_softmax(s_s, (dist_s >= 0)[:, :, None])
        o_s = jnp.einsum('bgrqk,bgqkd->bgrqd', p_s.astype(v_sel.dtype), v_sel)
        k_w = lax.dynamic_slice_in_dim(k_win, qb * Q_BLOCK, WINDOW + Q_BLOCK, axis=2)
        v_w = lax.dynamic_slice_in_dim(v_win, qb * Q_BLOCK, WINDOW + Q_BLOCK, axis=2)
        pos_w = qb * Q_BLOCK - WINDOW + jnp.arange(WINDOW + Q_BLOCK)
        dist_w = t[:, None] - pos_w[None, :]
        mask_w = (dist_w >= 0) & (dist_w < WINDOW) & (pos_w[None, :] >= 0)
        s_w = jnp.einsum('bgrqd,bgkd->bgrqk', q_blk, k_w) * scale + table[:, :, _rel_bucket(dist_w)]
        p_w = _masked_softmax(s_w, mask_w)
        o_w = jnp.einsum('bgrqk,bgkd->bgrqd', p_w.astype(v_w.dtype), v_w)
        return g_blk[..., 0:1] * o_c + g_blk[..., 1:2] * o_s + g_blk[..., 2:3] * o_w

    o = lax.map(block_fn, (jnp.arange(NQB), q_blocks, gate_blocks))
    return o.transpose(1, 0, 4, 2, 3, 5).reshape(B, T, NSA_HEADS * NSA_DV)

def _hier_moe(h, w_grp, b_grp, w_exp, b_exp, w1, w3, w2):
    B, T, D = h.shape
    x = h.reshape(-1, D)
    NT = x.shape[0]
    grp_prob = jax.nn.softmax((x @ w_grp + b_grp).astype(jnp.float32), axis=-1)
    grp_p, grp_idx = lax.top_k(grp_prob, 1)
    exp_logits = (x @ w_exp + b_exp).astype(jnp.float32).reshape(NT, N_GROUPS, EXP_PER_GROUP)
    in_grp = exp_logits[jnp.arange(NT), grp_idx[:, 0]]
    top_l, top_i = lax.top_k(in_grp, TOPK_IN_GROUP)
    comb = grp_p * jax.nn.softmax(top_l, axis=-1)
    expert = grp_idx * EXP_PER_GROUP + top_i

    A = NT * TOPK_IN_GROUP
    e_flat = expert.reshape(-1)
    tok_flat = jnp.repeat(jnp.arange(NT), TOPK_IN_GROUP)
    order = jnp.argsort(e_flat)
    e_s, tok_s, w_s = e_flat[order], tok_flat[order], comb.reshape(-1)[order]
    counts = jnp.bincount(e_flat, length=N_EXPERTS)
    starts = jnp.cumsum(counts) - counts
    padded = (counts + MOE_BLOCK - 1) // MOE_BLOCK * MOE_BLOCK
    pend = jnp.cumsum(padded)
    pstarts = pend - padded
    dest = pstarts[e_s] + jnp.arange(A) - starts[e_s]
    n_blocks = -(-A // MOE_BLOCK) + N_EXPERTS
    x_pad = jnp.zeros((n_blocks * MOE_BLOCK, D), x.dtype).at[dest].set(x[tok_s])
    block_expert = jnp.minimum(jnp.searchsorted(pend, jnp.arange(n_blocks) * MOE_BLOCK, side='right'),
                               N_EXPERTS - 1)

    def expert_block(args):
        xb, e = args
        return (jax.nn.silu(xb @ w1[e]) * (xb @ w3[e])) @ w2[e]

    y_pad = lax.map(expert_block, (x_pad.reshape(n_blocks, MOE_BLOCK, D), block_expert)).reshape(-1, D)
    y = y_pad[dest] * w_s[:, None].astype(x.dtype)
    out = jnp.zeros_like(x).at[tok_s].add(y)
    return out.reshape(B, T, D)

def first_inputs(seed: int = 0) -> dict:
    key = jax.random.key(seed)
    ks = iter(jax.random.split(key, 40))
    nrm = lambda shape, s: jax.random.normal(next(ks), shape, jnp.float32) * s
    L, D = DEPTH, D_MODEL
    return {
        'x': nrm((BATCH, SEQ, D), 1.0),
        'c': nrm((BATCH, D), 1.0),
        'ada_w': nrm((L, D, 6 * D), 0.1 * D ** -0.5),
        'ada_b': nrm((L, 6 * D), 0.02),
        'w_in': nrm((L, D, D_IN), D ** -0.5),
        'b_in': nrm((L, D_IN), 0.02),
        'hg_lb_logits': nrm((DEPTH + 1, HG_HEADS * HG_DK), 0.1),
        'hg_norm_w': 1.0 + nrm((L, HG_HEADS * HG_DV), 0.05),
        'cmp_pos_k': nrm((L, CMP_BLOCK, NSA_DK), 0.1),
        'cmp_w1_k': nrm((L, CMP_BLOCK * NSA_DK, CMP_HIDDEN), (CMP_BLOCK * NSA_DK) ** -0.5),
        'cmp_b1_k': nrm((L, CMP_HIDDEN), 0.02),
        'cmp_w2_k': nrm((L, CMP_HIDDEN, NSA_DK), CMP_HIDDEN ** -0.5),
        'cmp_pos_v': nrm((L, CMP_BLOCK, NSA_DV), 0.1),
        'cmp_w1_v': nrm((L, CMP_BLOCK * NSA_DV, CMP_HIDDEN), (CMP_BLOCK * NSA_DV) ** -0.5),
        'cmp_b1_v': nrm((L, CMP_HIDDEN), 0.02),
        'cmp_w2_v': nrm((L, CMP_HIDDEN, NSA_DV), CMP_HIDDEN ** -0.5),
        'rel_bias': nrm((NSA_HEADS, REL_BUCKETS), 0.5),
        'w_br_hg': nrm((L, HG_HEADS * HG_DV, D), BETA * (HG_HEADS * HG_DV) ** -0.5),
        'w_br_nsa': nrm((L, NSA_HEADS * NSA_DV, D), BETA * (NSA_HEADS * NSA_DV) ** -0.5),
        'w_out': nrm((L, D, D), BETA * D ** -0.5),
        'ln1_g': 1.0 + nrm((L, D), 0.05),
        'ln1_b': nrm((L, D), 0.02),
        'router_grp_w': nrm((L, D, N_GROUPS), D ** -0.5),
        'router_grp_b': nrm((L, N_GROUPS), 0.01),
        'router_exp_w': nrm((L, D, N_EXPERTS), D ** -0.5),
        'router_exp_b': nrm((L, N_EXPERTS), 0.01),
        'exp_w1': nrm((L, N_EXPERTS, D, D_EXPERT), D ** -0.5),
        'exp_w3': nrm((L, N_EXPERTS, D, D_EXPERT), D ** -0.5),
        'exp_w2': nrm((L, N_EXPERTS, D_EXPERT, D), BETA * D_EXPERT ** -0.5),
        'ln2_g': 1.0 + nrm((L, D), 0.05),
        'ln2_b': nrm((L, D), 0.02),
    }

def first_block(x, c, ada_w, ada_b, w_in, b_in, hg_lb_logits, hg_norm_w,
              cmp_pos_k, cmp_w1_k, cmp_b1_k, cmp_w2_k, cmp_pos_v, cmp_w1_v, cmp_b1_v, cmp_w2_v,
              rel_bias, w_br_hg, w_br_nsa, w_out, ln1_g, ln1_b,
              router_grp_w, router_grp_b, router_exp_w, router_exp_b,
              exp_w1, exp_w3, exp_w2, ln2_g, ln2_b):
    B, T, D = x.shape
    split_idx = [int(v) for v in np.cumsum(SPLITS)[:-1]]
    lb_all = jnp.cumsum(jax.nn.softmax(hg_lb_logits.astype(jnp.float32), axis=0), axis=0)
    c_act = jax.nn.silu(c)
    for l in range(DEPTH):
        mod = c_act @ ada_w[l] + ada_b[l]
        sh1, sc1, g1, sh2, sc2, g2 = jnp.split(mod, 6, axis=-1)

        h = _layer_norm(x) * (1 + sc1[:, None]) + sh1[:, None]
        proj = h @ w_in[l] + b_in[l]
        (hq, hf, hi, hg, nq, kc, vc, ks, vs, kw, vw, ngate, mg_h, mg_n) = jnp.split(proj, split_idx, axis=-1)
        o_h = _hgrn2(hq.reshape(B, T, HG_HEADS, HG_DK), hf.reshape(B, T, HG_HEADS, HG_DK),
                     hi.reshape(B, T, HG_HEADS, HG_DV), lb_all[l])
        o_h = (_rms_norm(o_h) * hg_norm_w[l].reshape(HG_HEADS, HG_DV)
               * jax.nn.sigmoid(hg.reshape(B, T, HG_HEADS, HG_DV))).reshape(B, T, HG_HEADS * HG_DV)
        gsz = (B, T, NSA_GROUPS, NSA_DK)
        o_n = _nsa(nq.reshape(B, T, NSA_HEADS, NSA_DK),
                   kc.reshape(gsz), vc.reshape(gsz), ks.reshape(gsz), vs.reshape(gsz),
                   kw.reshape(gsz), vw.reshape(gsz),
                   ngate.reshape(B, T, NSA_HEADS, 3), rel_bias,
                   cmp_pos_k[l], cmp_w1_k[l], cmp_b1_k[l], cmp_w2_k[l],
                   cmp_pos_v[l], cmp_w1_v[l], cmp_b1_v[l], cmp_w2_v[l])
        merged = jax.nn.sigmoid(mg_h) * (o_h @ w_br_hg[l]) + jax.nn.sigmoid(mg_n) * (o_n @ w_br_nsa[l])
        y = (1 + g1[:, None]) * (merged @ w_out[l])
        x = _layer_norm(ALPHA * x + y) * ln1_g[l] + ln1_b[l]

        h = _layer_norm(x) * (1 + sc2[:, None]) + sh2[:, None]
        y = (1 + g2[:, None]) * _hier_moe(h, router_grp_w[l], router_grp_b[l], router_exp_w[l],
                                          router_exp_b[l], exp_w1[l], exp_w3[l], exp_w2[l])
        x = _layer_norm(ALPHA * x + y) * ln2_g[l] + ln2_b[l]
    return x


ATTN_HEADS = 8
HEAD_DIM = 64
ATTN_WIDTH = ATTN_HEADS * HEAD_DIM
Q_BLOCK_2 = 128
POOL_WINDOWS = (2, 4, 8, 16)
POOL_GROUPS = len(POOL_WINDOWS)
POOL_WIDTH = D_MODEL - ATTN_WIDTH
POOL_GROUP_DIM = POOL_WIDTH // POOL_GROUPS
IN_WIDTH = 3 * ATTN_WIDTH + ATTN_HEADS + POOL_WIDTH
N_EXPERT_GROUPS = 4
EXPERTS_PER_GROUP = 8
TOP_K_EXPERT = 2
D_EXPERT_2 = 256
N_MOD = 6
EPS = 1e-6
NEG_INF = -1e30
FGATE_BIAS_INIT = 3.0


def rmsnorm(x, g):
    xf = x.astype(jnp.float32)
    y = xf * lax.rsqrt(jnp.mean(xf * xf, axis=-1, keepdims=True) + EPS)
    return (y * g.astype(jnp.float32)).astype(x.dtype)

def modulate(h, shift, scale):
    return h * (1.0 + scale[:, None, :]) + shift[:, None, :]

def forgetting_attention(q, k, v, log_f):
    B, S, H, dh = q.shape
    nb = S // Q_BLOCK_2
    qh = q.transpose(0, 2, 1, 3)
    kh = k.transpose(0, 2, 1, 3)
    vh = v.transpose(0, 2, 1, 3)
    F = jnp.cumsum(log_f, axis=1).transpose(0, 2, 1)
    q_blocks = qh.reshape(B, H, nb, Q_BLOCK_2, dh).transpose(2, 0, 1, 3, 4)
    fq_blocks = F.reshape(B, H, nb, Q_BLOCK_2).transpose(2, 0, 1, 3)
    starts = jnp.arange(nb, dtype=jnp.int32) * Q_BLOCK_2
    key_pos = jnp.arange(S, dtype=jnp.int32)
    scale = 1.0 / math.sqrt(dh)

    def one_block(args):
        qb, fqb, start = args
        s = jnp.einsum('bhqd,bhkd->bhqk', qb, kh).astype(jnp.float32) * scale
        s = s + fqb[..., None] - F[:, :, None, :]
        qpos = start + jnp.arange(Q_BLOCK_2, dtype=jnp.int32)
        causal = key_pos[None, :] <= qpos[:, None]
        s = jnp.where(causal[None, None], s, NEG_INF)
        p = jax.nn.softmax(s, axis=-1).astype(vh.dtype)
        return jnp.einsum('bhqk,bhkd->bhqd', p, vh)

    out = lax.map(one_block, (q_blocks, fq_blocks, starts))
    return out.transpose(1, 0, 3, 2, 4).reshape(B, S, H * dh)

def trailing_mean(cs, w):
    S = cs.shape[1]
    prev = jnp.pad(cs[:, :S - w], ((0, 0), (w, 0), (0, 0)))
    cnt = jnp.minimum(jnp.arange(1, S + 1), w).astype(jnp.float32)
    return (cs - prev) / cnt[None, :, None]

def multiscale_pool(u, w_pool, pool_scale):
    B, S, _ = u.shape
    ug = u.reshape(B, S, POOL_GROUPS, POOL_GROUP_DIM)
    cs = jnp.cumsum(ug.astype(jnp.float32), axis=1)
    pooled = jnp.stack(
        [trailing_mean(cs[:, :, g, :], w) for g, w in enumerate(POOL_WINDOWS)], axis=2)
    diff = (pooled - ug.astype(jnp.float32)).astype(u.dtype)
    mixed = jnp.einsum('bsgc,gcd->bsgd', diff, w_pool)
    return mixed.reshape(B, S, POOL_WIDTH) * pool_scale

def hierarchical_moe(h, w_rg, b_rg, w_re, b_re, w_gate, w_up, w_down):
    lg = jnp.matmul(h, w_rg).astype(jnp.float32) + b_rg
    pg = jax.nn.softmax(lg, axis=-1)
    top_p, top_g = lax.top_k(pg, 1)
    le = jnp.einsum('td,gde->tge', h, w_re).astype(jnp.float32) + b_re
    le_sel = jnp.take_along_axis(le, top_g[:, :, None], axis=1)[:, 0]
    ev, ei = lax.top_k(le_sel, TOP_K_EXPERT)
    ew = jax.nn.softmax(ev, axis=-1)
    e_comb = jnp.sum(jax.nn.one_hot(ei, EXPERTS_PER_GROUP, dtype=jnp.float32) * ew[..., None], axis=1)
    g_comb = jax.nn.one_hot(top_g[:, 0], N_EXPERT_GROUPS, dtype=jnp.float32) * top_p
    comb = (g_comb[:, :, None] * e_comb[:, None, :]).astype(h.dtype)
    y = jnp.zeros_like(h)
    for g in range(N_EXPERT_GROUPS):
        a = jnp.einsum('td,edf->tef', h, w_gate[g])
        b = jnp.einsum('td,edf->tef', h, w_up[g])
        act = jax.nn.silu(a) * b * comb[:, g, :, None]
        y = y + jnp.einsum('tef,efd->td', act, w_down[g])
    return y

def second_inputs(seed: int = 0) -> dict:
    key = jax.random.key(seed)
    ks = jax.random.split(key, 20)
    f32 = jnp.float32
    D, L = D_MODEL, DEPTH
    G, E, F = N_EXPERT_GROUPS, EXPERTS_PER_GROUP, D_EXPERT_2

    def nrm(k, shape, scale):
        return jax.random.normal(k, shape, f32) * scale

    return {
        "x": nrm(ks[0], (BATCH, SEQ, D), 1.0),
        "c": nrm(ks[1], (BATCH, D), 1.0),
        "norm_mix_g": 1.0 + nrm(ks[2], (L, D), 0.02),
        "norm_ffn_g": 1.0 + nrm(ks[3], (L, D), 0.02),
        "norm_final_g": 1.0 + nrm(ks[4], (D,), 0.02),
        "w_ada": nrm(ks[5], (L, D, N_MOD * D), 0.5 * D ** -0.5),
        "b_ada": nrm(ks[6], (L, N_MOD * D), 0.02),
        "w_in": nrm(ks[7], (L, D, IN_WIDTH), D ** -0.5),
        "b_fgate": FGATE_BIAS_INIT + nrm(ks[8], (L, ATTN_HEADS), 0.1),
        "w_pool": nrm(ks[9], (L, POOL_GROUPS, POOL_GROUP_DIM, POOL_GROUP_DIM), POOL_GROUP_DIM ** -0.5),
        "pool_scale": 1.0 + nrm(ks[10], (L, POOL_WIDTH), 0.1),
        "w_out": nrm(ks[11], (L, D, D), D ** -0.5),
        "w_router_group": nrm(ks[12], (L, D, G), D ** -0.5),
        "b_router_group": nrm(ks[13], (L, G), 0.01),
        "w_router_expert": nrm(ks[14], (L, G, D, E), D ** -0.5),
        "b_router_expert": nrm(ks[15], (L, G, E), 0.01),
        "w_expert_gate": nrm(ks[16], (L, G, E, D, F), D ** -0.5),
        "w_expert_up": nrm(ks[17], (L, G, E, D, F), D ** -0.5),
        "w_expert_down": nrm(ks[18], (L, G, E, F, D), F ** -0.5),
    }

def second_block(x, c, norm_mix_g, norm_ffn_g, norm_final_g, w_ada, b_ada, w_in, b_fgate,
              w_pool, pool_scale, w_out, w_router_group, b_router_group, w_router_expert,
              b_router_expert, w_expert_gate, w_expert_up, w_expert_down):
    B, S, D = x.shape
    split_pts = [ATTN_WIDTH, 2 * ATTN_WIDTH, 3 * ATTN_WIDTH, 3 * ATTN_WIDTH + ATTN_HEADS]
    c_act = jax.nn.silu(c)
    for l in range(DEPTH):
        mod = jnp.matmul(c_act, w_ada[l]) + b_ada[l]
        sh_m, sc_m, gt_m, sh_f, sc_f, gt_f = jnp.split(mod, N_MOD, axis=-1)

        h = modulate(rmsnorm(x, norm_mix_g[l]), sh_m, sc_m)
        proj = jnp.matmul(h, w_in[l])
        q, k, v, f_logit, u = jnp.split(proj, split_pts, axis=-1)
        q = q.reshape(B, S, ATTN_HEADS, HEAD_DIM)
        k = k.reshape(B, S, ATTN_HEADS, HEAD_DIM)
        v = v.reshape(B, S, ATTN_HEADS, HEAD_DIM)
        log_f = jax.nn.log_sigmoid(f_logit.astype(jnp.float32) + b_fgate[l].astype(jnp.float32))
        attn_out = forgetting_attention(q, k, v, log_f)
        pool_out = multiscale_pool(u, w_pool[l], pool_scale[l])
        mix = jnp.matmul(jnp.concatenate([attn_out, pool_out.astype(attn_out.dtype)], axis=-1), w_out[l])
        x = x + gt_m[:, None, :] * mix

        h = modulate(rmsnorm(x, norm_ffn_g[l]), sh_f, sc_f)
        ffn = hierarchical_moe(h.reshape(B * S, D), w_router_group[l], b_router_group[l],
                               w_router_expert[l], b_router_expert[l], w_expert_gate[l],
                               w_expert_up[l], w_expert_down[l])
        x = x + gt_f[:, None, :] * ffn.reshape(B, S, D)
    return rmsnorm(x, norm_final_g)


def setup_inputs(seed=0):
    out = dict(first_inputs(seed))
    for name, value in second_inputs(seed + 1).items():
        if name != "x":
            out[name + "_2"] = value
    return out


def reference(
    x, c, ada_w, ada_b, w_in, b_in, hg_lb_logits, hg_norm_w, cmp_pos_k, cmp_w1_k, cmp_b1_k,
    cmp_w2_k, cmp_pos_v, cmp_w1_v, cmp_b1_v, cmp_w2_v, rel_bias, w_br_hg, w_br_nsa, w_out,
    ln1_g, ln1_b, router_grp_w, router_grp_b, router_exp_w, router_exp_b, exp_w1, exp_w3,
    exp_w2, ln2_g, ln2_b, c_2, norm_mix_g_2, norm_ffn_g_2, norm_final_g_2, w_ada_2, b_ada_2,
    w_in_2, b_fgate_2, w_pool_2, pool_scale_2, w_out_2, w_router_group_2, b_router_group_2,
    w_router_expert_2, b_router_expert_2, w_expert_gate_2, w_expert_up_2, w_expert_down_2,
):
    x = first_block(
        x, c, ada_w, ada_b, w_in, b_in, hg_lb_logits, hg_norm_w, cmp_pos_k, cmp_w1_k, cmp_b1_k,
        cmp_w2_k, cmp_pos_v, cmp_w1_v, cmp_b1_v, cmp_w2_v, rel_bias, w_br_hg, w_br_nsa, w_out,
        ln1_g, ln1_b, router_grp_w, router_grp_b, router_exp_w, router_exp_b, exp_w1, exp_w3,
        exp_w2, ln2_g, ln2_b,
    )
    return second_block(
        x, c_2, norm_mix_g_2, norm_ffn_g_2, norm_final_g_2, w_ada_2, b_ada_2, w_in_2, b_fgate_2,
        w_pool_2, pool_scale_2, w_out_2, w_router_group_2, b_router_group_2, w_router_expert_2,
        b_router_expert_2, w_expert_gate_2, w_expert_up_2, w_expert_down_2,
    )


_drawn_inputs = setup_inputs


def setup_inputs(seed=0):
    import zlib

    import numpy as np

    out = dict(_drawn_inputs(seed))
    spreads = {}
    factors = {'b_in': 5.132,
     'hg_lb_logits': 3.791,
     'hg_norm_w': 4.41,
     'cmp_pos_k': 8.0,
     'cmp_w1_k': 3.522,
     'cmp_b1_k': 8.0,
     'cmp_w2_k': 3.661,
     'cmp_pos_v': 5.787,
     'cmp_b1_v': 8.0,
     'rel_bias': 2.907,
     'router_grp_b': 8.0,
     'router_exp_b': 5.01,
     'norm_mix_g_2': 8.0,
     'norm_ffn_g_2': 5.503,
     'norm_final_g_2': 2.893,
     'b_fgate_2': 8.0,
     'b_router_group_2': 8.0,
     'b_router_expert_2': 8.0}
    for name, (base, spread) in spreads.items():
        noise = np.random.default_rng([zlib.crc32(name.encode()), seed]).standard_normal(out[name].shape)
        drawn = base * np.exp(spread * noise) if base else spread * noise
        out[name] = __import__('jax').numpy.asarray(drawn.astype(out[name].dtype))
    for name, factor in factors.items():
        out[name] = (out[name] * factor).astype(out[name].dtype)
    return out
```

```python
from contextlib import ExitStack

import concourse.bass as bass
import numpy as np
from concourse import mybir

F32 = mybir.dt.float32
I32 = mybir.dt.int32
ALU = mybir.AluOpType
ACT = mybir.ActivationFunctionType
AX = mybir.AxisListType

P = 128
SEQ = 512
D = 1024
TC = SEQ // P
KC = D // P
HEADS = 8

HG_CHUNK = 32
N_CHUNK = SEQ // HG_CHUNK
QC = P // HG_CHUNK
GROUPS = 2
REP = HEADS // GROUPS
CMP_BLOCK = 32
CMP_STRIDE = 16
N_CMP = SEQ // CMP_STRIDE - 1
BUCKETS = 32
MAX_DIST = 128
ALPHA = 2 ** 0.25
ATT_SCALE = P ** -0.5
NEG = -1e30

N_GRP = 4
PER_GRP = 8
N_EXP = N_GRP * PER_GRP
SLOTS = 64
PAIRS = N_EXP // 2
F1 = 512
F2 = 256

DH2 = 64
POOL_WINDOWS = (2, 4, 8, 16)

BT0 = SEQ - P
BTW = BT0 + SEQ
BT_ROW = 1024


def pack_columns():
    return [("c", 8), ("ada_b", 48), ("b_in", 52), ("b_mg", 16), ("lb0", 8), ("lb1", 8), ("hg_norm_w", 8),
            ("cmp_b1_k", 1), ("cmp_b1_v", 1), ("cmp_pos_k", 32), ("cmp_pos_v", 32),
            ("ln1_g", 8), ("ln1_b", 8), ("ln2_g", 8), ("ln2_b", 8),
            ("c_2", 8), ("b_ada_2", 48), ("norm_mix_g_2", 8), ("norm_ffn_g_2", 8), ("norm_final_g_2", 8),
            ("pool_scale_2", 4)]


def pack_rows():
    return [("b_gate", 24), ("router_b", 36), ("router_b_2", 36), ("b_fgate_2", 8)]


def pack_consts():
    p = np.arange(P)[:, None]
    j = np.arange(P)[None, :]
    w = np.arange(BTW)[None, :]
    ident = (p == j)
    before = (p < j)
    ones = np.ones((P, P))
    hg_causal = (p // HG_CHUNK == j // HG_CHUNK) & (p <= j)
    chunk_of = (p // HG_CHUNK == np.arange(QC)[None, :])
    half = (p // DH2 == np.arange(2)[None, :])
    slot = np.broadcast_to(np.arange(SLOTS)[None, :], (P, SLOTS))
    chunk_cont = np.broadcast_to((np.arange(SEQ) % HG_CHUNK != 0)[None, :], (P, SEQ))
    upto = (p <= w - BT0)
    causal2 = np.where(w[:, :SEQ] - BT0 > p, NEG, 0.0)
    inv = np.array([[1.0 / min(t + 1, k) for t in range(16)] for k in POOL_WINDOWS]).reshape(1, -1)
    pool_inv = np.broadcast_to(inv, (P, inv.size))
    first = np.broadcast_to(np.arange(N_EXP, 0, -1)[None, :], (P, N_EXP))
    t = (np.arange(TC)[None, :, None] * P + p[:, :, None])
    cmp_ok = (t - (np.arange(N_CMP) * CMP_STRIDE + CMP_BLOCK - 1)[None, None, :] >= 0).reshape(P, -1)
    return [(n, np.asarray(a, np.float32)) for n, a in (
        ("ident", ident), ("before", before), ("ones", ones), ("hg_causal", hg_causal), ("chunk_of", chunk_of),
        ("half", half), ("slot", slot), ("chunk_cont", chunk_cont), ("upto", upto), ("causal2", causal2),
        ("pool_inv", pool_inv), ("first", first), ("cmp_ok", cmp_ok))]


def bucket_rows():
    import math
    dist = SEQ - 1 - np.arange(BT_ROW)
    n = np.maximum(dist, 0)
    half = BUCKETS // 2
    nf = np.maximum(n, 1).astype(np.float32)
    large = half + (np.log(nf / np.float32(half)) / np.float32(math.log(MAX_DIST / half)) * np.float32(BUCKETS - half)).astype(np.int32)
    b = np.where(n < half, n, np.minimum(large, BUCKETS - 1))
    out = np.zeros((BUCKETS + 1, BT_ROW), np.float32)
    out[b, np.arange(BT_ROW)] = dist >= 0
    out[BUCKETS] = dist < 0
    return out


def offsets(spec):
    at, out = 0, {}
    for name, n in spec:
        out[name] = (at, n)
        at += n
    return out, at


class Kit:

    def __init__(self, nc, inputs, out):
        self.nc, self.i, self.out = nc, inputs, out
        self.owned, self.zeroed = [], []
        self.col_at, self.n_cols = offsets(pack_columns())
        self.row_at, self.n_rows = offsets(pack_rows())
        self.const_at, self.n_consts = offsets([(n, a.shape[1]) for n, a in pack_consts()])

    def sb(self, ctx, name, shape, dt=F32):
        return ctx.enter_context(self.nc.sbuf_tensor(name, shape, dt))

    def banks(self, ctx, name, n):
        return [ctx.enter_context(self.nc.psum_tensor(f"{name}{j}", [P, 512], F32)) for j in range(n)]

    def sem(self, ctx, name):
        if not any(owner is ctx for owner, _ in self.owned):
            self.owned.append((ctx, []))
            ctx.callback(self.stage_over, ctx)
        handle = self.nc.alloc_semaphore(name=name)
        next(sems for owner, sems in self.owned if owner is ctx).append(handle)
        return handle

    def stage_over(self, ctx):
        mine = next(pair for pair in self.owned if pair[0] is ctx)
        self.owned.remove(mine)
        for s in self.zeroed:
            self.nc.release_semaphore(s)
        numbers = sorted(s.num for s in mine[1])
        start = numbers[0]
        for a, b in zip(numbers, numbers[1:] + [None]):
            if b != a + 1:
                self.nc.gpsimd.sem_clear(range(start, a + 1))
                start = b
        self.zeroed = mine[1]

    def col(self, name, j=0, n=1):
        a = self.col_at[name][0] + j
        return self.cols[:, a:a + n]

    def row(self, name):
        a, n = self.row_at[name]
        return self.rows[:, a:a + n]

    def const(self, name, a=0, b=None):
        at, n = self.const_at[name]
        return self.consts[:, at + a:at + (n if b is None else b)]


def load_constants(k):
    nc = k.nc
    with ExitStack() as ctx:
        loaded = k.sem(ctx, "const_loaded")
        with nc.Block() as block:
            @block.sync
            def _(sp):
                sp.dma_start(k.consts[:], k.i["consts"]).then_inc(loaded, 16)
                sp.dma_start(k.cols[:], k.i["cols"]).then_inc(loaded, 16)
                sp.dma_start(k.rows[:], k.i["rows"].partition_broadcast(P)).then_inc(loaded, 16)
                sp.dma_start(k.x[:], k.i["x"].rearrange("(c p) d -> p c d", p=P)).then_inc(loaded, 16)
                sp.wait_ge(loaded, 64)


def modulation(k, tag, weights, act, bias, mod):
    nc = k.nc
    NBUF, BLK = 3, 512
    rounds = 6 * D // BLK // NBUF
    per = BLK // P
    w_v = weights.rearrange("(k p) n -> p k n", p=P)
    with ExitStack() as ctx:
        buf = [k.sb(ctx, f"{tag}_w{r}", [P, KC, BLK]) for r in range(NBUF)]
        sig = k.sb(ctx, f"{tag}_sig", [P, KC])
        c_act = k.sb(ctx, f"{tag}_cact", [P, KC])
        ps, = k.banks(ctx, f"{tag}_ps", 1)
        w_loaded = [k.sem(ctx, f"{tag}_w_loaded{r}") for r in range(NBUF)]
        w_used = k.sem(ctx, f"{tag}_w_used")
        sig_ready = k.sem(ctx, f"{tag}_sig_ready")
        act_ready = k.sem(ctx, f"{tag}_act_ready")
        mod_kept = k.sem(ctx, f"{tag}_mod_kept")

        with nc.Block() as block:
            @block.sync
            def _(sp):
                for r in range(NBUF):
                    sp.dma_start(buf[r][:], w_v[:, :, r * BLK:(r + 1) * BLK]).then_inc(w_loaded[r], 16)
                with sp.Fori(1, rounds) as it:
                    for r in range(NBUF):
                        sp.wait_ge(w_used, it * NBUF + (r - NBUF + 1))
                        sp.dma_start(buf[r][:], w_v[:, :, bass.ts(it * NBUF + r, BLK)]).then_inc(w_loaded[r], 16)

            @block.scalar
            def _(act_e):
                act_e.activation(sig[:], act, ACT.Sigmoid).then_inc(sig_ready, 1)

            @block.tensor
            def _(pe):
                pe.wait_ge(act_ready, 1)
                with pe.Fori(0, rounds) as it:
                    for r in range(NBUF):
                        pe.wait_ge(w_loaded[r], it * 16 + 16)
                        if r == 0:
                            pe.wait_ge(mod_kept, it + 1)
                        for j in range(per):
                            for kc in range(KC):
                                last = pe.matmul(ps[:, r * P + j:r * P + j + 1],
                                                 buf[r][:, kc, j * P:(j + 1) * P], c_act[:, kc:kc + 1],
                                                 start=(kc == 0), stop=(kc == KC - 1))
                        last.then_inc(w_used, 1)

            @block.vector
            def _(dve):
                dve.wait_ge(sig_ready, 1)
                dve.tensor_tensor(c_act[:], act, sig[:], ALU.mult).then_inc(act_ready, 1)
                dve.drain().then_inc(mod_kept, 1)
                with dve.Fori(0, rounds) as it:
                    dve.wait_ge(w_used, it * NBUF + NBUF)
                    out = bass.ds(it * (NBUF * per), NBUF * per)
                    dve.tensor_tensor(mod[:, out].rearrange("p (r j) -> p r j", j=per),
                                      ps[:, 0:NBUF * P].rearrange("p (r j) -> p r j", j=P)[:, :, 0:per],
                                      bias[:, out].rearrange("p (r j) -> p r j", j=per), ALU.add).then_inc(mod_kept, 1)


def normalize(k, tag, eps, root_mean_square=False, gain=None, shift=None, out=None):
    nc = k.nc
    out = k.xn if out is None else out
    with ExitStack() as ctx:
        stats = k.sb(ctx, f"{tag}_stats", [P, TC, 2, 6])
        mv = k.sb(ctx, f"{tag}_mv", [P, TC, 2])
        var = k.sb(ctx, f"{tag}_var", [P, TC])
        dev = k.sb(ctx, f"{tag}_dev", [P, TC])
        rstd = k.sb(ctx, f"{tag}_rstd", [P, TC])
        var_ready = k.sem(ctx, f"{tag}_var_ready")
        dev_ready = k.sem(ctx, f"{tag}_dev_ready")
        scaled = k.sem(ctx, f"{tag}_scaled")
        gained = k.sem(ctx, f"{tag}_gained")
        with nc.Block() as block:
            @block.vector
            def _(dve):
                for c in range(TC):
                    for h in range(2):
                        dve.bn_stats(stats[:, c, h, :], k.x[:, c, h * 512:(h + 1) * 512])
                dve.drain()
                for c in range(TC):
                    dve.bn_aggr(mv[:, c, :], stats[:, c, :, :])
                dve.drain()
                if root_mean_square:
                    dve.tensor_tensor(var[:], mv[:, :, 0], mv[:, :, 0], ALU.mult)
                    dve.drain()
                    dve.tensor_tensor(var[:], var[:], mv[:, :, 1], ALU.add)
                    dve.drain()
                    dve.tensor_scalar(var[:], var[:], eps, None, ALU.add).then_inc(var_ready, 1)
                else:
                    dve.tensor_scalar(var[:], mv[:, :, 1], eps, None, ALU.add).then_inc(var_ready, 1)
                dve.wait_ge(dev_ready, 1)
                dve.reciprocal(rstd[:], dev[:])
                dve.drain()
                for c in range(TC):
                    if root_mean_square:
                        dve.tensor_scalar(out[:, c, :], k.x[:, c, :], rstd[:, c:c + 1], None, ALU.mult).then_inc(scaled, 1)
                    else:
                        dve.tensor_scalar(out[:, c, :], k.x[:, c, :], mv[:, c, 0:1], rstd[:, c:c + 1],
                                          ALU.subtract, ALU.mult).then_inc(scaled, 1)
                if gain is not None:
                    for c in (0, 1):
                        dve.wait_ge(scaled, c + 1)
                        dve.tensor_tensor(out[:, c, :], out[:, c, :], gain, ALU.mult)
                    dve.drain()
                    if shift is not None:
                        for c in (0, 1):
                            dve.tensor_tensor(out[:, c, :], out[:, c, :], shift, ALU.add)

            @block.scalar
            def _(act):
                act.wait_ge(var_ready, 1)
                act.activation(dev[:], var[:], ACT.Sqrt).then_inc(dev_ready, 1)

            @block.gpsimd
            def _(pool):
                if gain is not None:
                    for c in (2, 3):
                        pool.wait_ge(scaled, c + 1)
                        pool.tensor_tensor(out[:, c, :], out[:, c, :], gain, ALU.mult).then_inc(gained, 1)
                    if shift is not None:
                        for c in (2, 3):
                            pool.wait_ge(gained, c - 1)
                            pool.tensor_tensor(out[:, c, :], out[:, c, :], shift, ALU.add)


def transposed(k, tag, scale, shift):
    nc = k.nc
    with ExitStack() as ctx:
        ps = k.banks(ctx, f"{tag}_ps", 2)
        turned = k.sem(ctx, f"{tag}_turned")
        kept = k.sem(ctx, f"{tag}_kept")
        with nc.Block() as block:
            @block.tensor
            def _(pe):
                for kc in range(KC):
                    if kc >= 2:
                        pe.wait_ge(kept, kc - 1)
                    for c in range(TC):
                        last = pe.transpose(ps[kc % 2][:, c * P:(c + 1) * P], k.xn[:, c, kc * P:(kc + 1) * P],
                                            k.const("ident"))
                    last.then_inc(turned, 1)

            @block.scalar
            def _(act):
                for kc in range(KC):
                    act.wait_ge(turned, kc + 1)
                    act.activation(k.hT[:, kc, :], ps[kc % 2][:, :], ACT.Identity, scale=scale[:, kc:kc + 1],
                                   bias=shift[:, kc:kc + 1]).then_inc(kept, 1)


def broadcast_rows(k, tag, jobs):
    nc = k.nc
    with ExitStack() as ctx:
        ps = k.banks(ctx, f"{tag}_ps", 2)
        turned = k.sem(ctx, f"{tag}_turned")
        kept = k.sem(ctx, f"{tag}_kept")
        steps = [(cols, out, plus, j) for cols, out, plus in jobs for j in range(0, cols.shape[1], 4)]
        with nc.Block() as block:
            @block.tensor
            def _(pe):
                for n, (cols, out, plus, j) in enumerate(steps):
                    if n >= 2:
                        pe.wait_ge(kept, n - 1)
                    for q in range(min(4, cols.shape[1] - j)):
                        last = pe.transpose(ps[n % 2][:, q * P:(q + 1) * P],
                                            cols[:, j + q:j + q + 1].broadcast_to([P, P]), k.const("ident"))
                    last.then_inc(turned, 1)

            @block.vector
            def _(dve):
                for n, (cols, out, plus, j) in enumerate(steps):
                    dve.wait_ge(turned, n + 1)
                    width = min(4, cols.shape[1] - j) * P
                    dve.tensor_scalar(out[:, j * P:j * P + width], ps[n % 2][:, 0:width], float(plus), None,
                                      ALU.add).then_inc(kept, 1)


def persistent(k, ctx):
    k.consts = k.sb(ctx, "consts", [P, k.n_consts])
    k.cols = k.sb(ctx, "cols", [P, k.n_cols])
    k.rows = k.sb(ctx, "rows", [P, k.n_rows])
    k.x = k.sb(ctx, "x", [P, TC, D])
    k.xn = k.sb(ctx, "xn", [P, TC, D])
    k.hT = k.sb(ctx, "hT", [P, KC, SEQ])
    k.mod = k.sb(ctx, "mod", [P, 6 * KC])
    k.scale1 = k.sb(ctx, "scale1", [P, KC])


def recurrence(k, ohT):
    nc = k.nc
    w_hg = k.i["w_hg"]
    raw = k.xn[:].rearrange("p c (h e) -> p c h e", e=P)
    with ExitStack() as ctx:
        w = [k.sb(ctx, f"hg_w{s}", [P, KC, P]) for s in range(4)]
        q = k.sb(ctx, "hg_q", [P, SEQ])
        sigf = k.sb(ctx, "hg_sigf", [P, SEQ])
        fg = k.sb(ctx, "hg_fg", [P, SEQ])
        key = k.sb(ctx, "hg_key", [P, SEQ])
        logf = k.sb(ctx, "hg_logf", [P, SEQ])
        b = k.sb(ctx, "hg_b", [P, SEQ])
        left = k.sb(ctx, "hg_left", [P, SEQ])
        eb = k.sb(ctx, "hg_eb", [P, SEQ])
        enb = k.sb(ctx, "hg_enb", [P, SEQ])
        eleft = k.sb(ctx, "hg_eleft", [P, SEQ])
        q_in = k.sb(ctx, "hg_q_in", [P, SEQ])
        k_in = k.sb(ctx, "hg_k_in", [P, SEQ])
        k_end = k.sb(ctx, "hg_k_end", [P, SEQ])
        k_tok = k.sb(ctx, "hg_k_tok", [P, TC, P])
        v_tok = k.sb(ctx, "hg_v_tok", [P, TC, P])
        v_parts = k.sb(ctx, "hg_v_parts", [P, TC, QC, P])
        att = k.sb(ctx, "hg_att", [P, TC, P])
        state = k.sb(ctx, "hg_state", [P, N_CHUNK, P])
        gate = k.sb(ctx, "hg_gate", [P, HEADS, SEQ])
        junk = k.sb(ctx, "hg_junk", [P, TC, P])
        squares = k.sb(ctx, "hg_squares", [P, HEADS, TC])
        rstd = k.sb(ctx, "hg_rstd", [P, HEADS, TC])
        lb = k.sb(ctx, "hg_lb", [P, HEADS])
        one_lb = k.sb(ctx, "hg_one_lb", [P, HEADS])
        v_bias = k.sb(ctx, "hg_v_bias", [P, D])
        lower_bound_layer(k, lb)
        broadcast_rows(k, "hg_vb", [(k.col("b_in", 16, 8), v_bias[:, :], 0.0)])

        proj = k.banks(ctx, "hg_proj", 2)
        upd = k.banks(ctx, "hg_upd", 4)
        tr_out, = k.banks(ctx, "hg_tr_out", 1)
        score, = k.banks(ctx, "hg_score", 1)

        names = ("loaded_q loaded_f loaded_g loaded_v used_q used_f used_g used_v "
                 "q_kept f_kept g_kept v_kept fg_ready key_ready logf_ready b_ready left_ready eb_ready enb_ready eleft_ready "
                 "qin_ready kin_ready kend_ready keys_turned ktok_kept scores_done att_ready "
                 "v_parts_ready updates_done chain_done outputs_done raw_kept").split()
        S = {n: k.sem(ctx, "hg_" + n) for n in names}
        slices = "qfgv"

        with nc.Block() as block:
            @block.sync
            def _(sp):
                for s, a in enumerate(slices):
                    sp.dma_start(w[s][:], w_hg[0, s]).then_inc(S["loaded_" + a], 16)
                with sp.Fori(1, HEADS) as n:
                    for s, a in enumerate(slices):
                        sp.wait_ge(S["used_" + a], n)
                        sp.dma_start(w[s][:], w_hg[n, s]).then_inc(S["loaded_" + a], 16)

            @block.tensor
            def _(pe):
                def feature_major(s, a, bank, n):
                    pe.wait_ge(S["loaded_" + a], n * 16 + 16)
                    for kc in range(KC):
                        last = pe.matmul(proj[bank][:, :], w[s][:, kc, :], k.hT[:, kc, :],
                                         start=(kc == 0), stop=(kc == KC - 1))
                    last.then_inc(S["used_" + a], 1)

                def project_qf(n, first):
                    if not first:
                        pe.wait_ge(S["g_kept"], n)
                    feature_major(0, "q", 0, n)
                    if not first:
                        pe.wait_ge(S["v_kept"], n)
                    feature_major(1, "f", 1, n)

                def project_gv(n):
                    pe.wait_ge(S["q_kept"], n + 1)
                    feature_major(2, "g", 0, n)
                    pe.wait_ge(S["f_kept"], n + 1)
                    pe.wait_ge(S["loaded_v"], n * 16 + 16)
                    for c in range(TC):
                        for kc in range(KC):
                            last = pe.matmul(proj[1][:, c * P:(c + 1) * P], k.hT[:, kc, c * P:(c + 1) * P],
                                             w[3][:, kc, :], start=(kc == 0), stop=(kc == KC - 1))
                    last.then_inc(S["used_v"], 1)

                def scores_and_updates(n, first):
                    pe.wait_ge(S["kend_ready"], n + 1)
                    if not first:
                        pe.wait_ge(S["raw_kept"], n)
                    for c in range(TC):
                        last = pe.transpose(tr_out[:, c * P:(c + 1) * P], k_end[:, c * P:(c + 1) * P], k.const("ident"))
                    last.then_inc(S["keys_turned"], 1)
                    pe.wait_ge(S["qin_ready"], n + 1)
                    pe.wait_ge(S["kin_ready"], n + 1)
                    for c in range(TC):
                        last = pe.matmul(score[:, c * P:(c + 1) * P], k_in[:, c * P:(c + 1) * P],
                                         q_in[:, c * P:(c + 1) * P], start=True, stop=True)
                    last.then_inc(S["scores_done"], 1)
                    pe.wait_ge(S["ktok_kept"], n + 1)
                    pe.wait_ge(S["v_parts_ready"], n + 1)
                    if not first:
                        pe.wait_ge(S["chain_done"], n)
                    for c in range(TC):
                        last = pe.matmul(upd[c][:, :], k_tok[:, c, :], v_parts[:, c, :, :], start=True, stop=True)
                    last.then_inc(S["updates_done"], 1)

                def outputs(n):
                    pe.wait_ge(S["att_ready"], n + 1)
                    pe.wait_ge(S["chain_done"], n + 1)
                    for c in range(TC):
                        last = pe.matmul(tr_out[:, c * P:(c + 1) * P], att[:, c, :], v_tok[:, c, :],
                                         start=True, stop=False, skip_group_check=True)
                        for r in range(QC):
                            ch = c * QC + r
                            if ch:
                                last = pe.matmul(tr_out[r * HG_CHUNK:(r + 1) * HG_CHUNK, c * P:(c + 1) * P],
                                                 q_in[:, ch * HG_CHUNK:(ch + 1) * HG_CHUNK], state[:, ch, :],
                                                 start=False, stop=True, skip_group_check=True)
                    last.then_inc(S["outputs_done"], 1)

                project_qf(0, True)
                project_gv(0)
                project_qf(1, False)
                scores_and_updates(0, True)
                project_gv(1)
                outputs(0)
                with pe.Fori(1, HEADS - 1) as n:
                    project_qf(n + 1, False)
                    scores_and_updates(n, False)
                    project_gv(n + 1)
                    outputs(n)
                scores_and_updates(HEADS - 1, False)
                outputs(HEADS - 1)

            @block.scalar
            def _(act):
                def keep_qf(n, first):
                    act.wait_ge(S["used_q"], n + 1)
                    if not first:
                        act.wait_ge(S["qin_ready"], n)
                    act.activation(q[:], proj[0][:, :], ACT.Identity, bias=k.col("b_in", 0, 8)[:, bass.ds(n, 1)]).then_inc(S["q_kept"], 1)
                    act.wait_ge(S["used_f"], n + 1)
                    act.activation(sigf[:], proj[1][:, :], ACT.Sigmoid, bias=k.col("b_in", 8, 8)[:, bass.ds(n, 1)]).then_inc(S["f_kept"], 1)

                def keep_gate(n):
                    act.wait_ge(S["used_g"], n + 1)
                    act.activation(gate[:, n, :], proj[0][:, :], ACT.Sigmoid, bias=k.col("b_in", 24, 8)[:, bass.ds(n, 1)]).then_inc(S["g_kept"], 1)

                def keep_keys(n):
                    act.wait_ge(S["keys_turned"], n + 1)
                    act.activation(k_tok[:], tr_out[:, :], ACT.Copy).then_inc(S["ktok_kept"], 1)

                def log_decay(n):
                    act.wait_ge(S["fg_ready"], n + 1)
                    act.activation(logf[:], fg[:], ACT.Ln).then_inc(S["logf_ready"], 1)

                def decays(n, first):
                    act.wait_ge(S["b_ready"], n + 1)
                    if not first:
                        act.wait_ge(S["chain_done"], n)
                        act.wait_ge(S["qin_ready"], n)
                        act.wait_ge(S["kin_ready"], n)
                        act.wait_ge(S["kend_ready"], n)
                    act.activation(eb[:], b[:], ACT.Exp).then_inc(S["eb_ready"], 1)
                    act.activation(enb[:], b[:], ACT.Exp, scale=-1.0).then_inc(S["enb_ready"], 1)
                    act.wait_ge(S["left_ready"], n + 1)
                    act.activation(eleft[:], left[:], ACT.Exp).then_inc(S["eleft_ready"], 1)

                def keep_outputs(n):
                    act.wait_ge(S["outputs_done"], n + 1)
                    for c in range(TC):
                        act.activation(junk[:, c, :], tr_out[:, c * P:(c + 1) * P], ACT.Square, accum_out=squares[:, n, c:c + 1])
                    act.activation(raw[:, :, n, :], tr_out[:, :].rearrange("p (c e) -> p c e", e=P), ACT.Copy).then_inc(S["raw_kept"], 1)
                    act.drain()

                keep_qf(0, True)
                keep_gate(0)
                log_decay(0)
                decays(0, True)
                with act.Fori(0, HEADS - 1) as n:
                    keep_qf(n + 1, False)
                    keep_keys(n)
                    keep_gate(n + 1)
                    log_decay(n + 1)
                    decays(n + 1, False)
                    keep_outputs(n)
                keep_keys(HEADS - 1)
                keep_outputs(HEADS - 1)

            @block.vector
            def _(dve):
                def forget(n, first):
                    dve.wait_ge(S["f_kept"], n + 1)
                    if not first:
                        dve.wait_ge(S["logf_ready"], n)
                        dve.wait_ge(S["kend_ready"], n)
                    dve.tensor_scalar(fg[:], sigf[:], one_lb[:, bass.ds(n, 1)], lb[:, bass.ds(n, 1)],
                                      ALU.mult, ALU.add).then_inc(S["fg_ready"], 1)
                    dve.wait_ge(S["fg_ready"], n + 1)
                    dve.tensor_scalar(key[:], fg[:], -1.0, 1.0, ALU.mult, ALU.add).then_inc(S["key_ready"], 1)

                def running(n):
                    dve.wait_ge(S["logf_ready"], n + 1)
                    dve.tensor_tensor_scan(b[:], k.const("chunk_cont"), logf[:], 0.0, ALU.mult, ALU.add).then_inc(S["b_ready"], 1)
                    dve.wait_ge(S["b_ready"], n + 1)
                    b_v = b[:].rearrange("p (n j) -> p n j", j=HG_CHUNK)
                    dve.tensor_tensor(left[:].rearrange("p (n j) -> p n j", j=HG_CHUNK),
                                      b_v[:, :, HG_CHUNK - 1:HG_CHUNK].broadcast_to([P, N_CHUNK, HG_CHUNK]), b_v,
                                      ALU.subtract).then_inc(S["left_ready"], 1)

                def masked_scores(n):
                    dve.wait_ge(S["scores_done"], n + 1)
                    dve.tensor_tensor(att[:], score[:, :].rearrange("p (c i) -> p c i", i=P),
                                      k.const("hg_causal").unsqueeze(1).broadcast_to([P, TC, P]), ALU.mult).then_inc(S["att_ready"], 1)

                def chain(n):
                    dve.wait_ge(S["updates_done"], n + 1)
                    dve.tensor_copy(state[:, 1, :], upd[0][:, 0:P])
                    for ch in range(1, N_CHUNK - 1):
                        dve.drain()
                        end = (ch + 1) * HG_CHUNK - 1
                        last = dve.scalar_tensor_tensor(out=state[:, ch + 1, :], in0=state[:, ch, :], scalar=eb[:, end:end + 1],
                                                        in1=upd[ch // QC][:, (ch % QC) * P:(ch % QC + 1) * P],
                                                        op0=ALU.mult, op1=ALU.add)
                    last.then_inc(S["chain_done"], 1)

                def keep_values(n, first):
                    dve.wait_ge(S["used_v"], n + 1)
                    if not first:
                        dve.wait_ge(S["outputs_done"], n)
                    dve.tensor_tensor(v_tok[:], proj[1][:, :].rearrange("p (c e) -> p c e", e=P),
                                      v_bias[:, bass.ts(n, P)].unsqueeze(1).broadcast_to([P, TC, P]), ALU.add).then_inc(S["v_kept"], 1)
                    dve.wait_ge(S["v_kept"], n + 1)
                    for r in range(QC):
                        last = dve.tensor_scalar(v_parts[:, :, r, :], v_tok[:], k.const("chunk_of")[:, r:r + 1], None, ALU.mult)
                    last.then_inc(S["v_parts_ready"], 1)

                def decayed(n, first):
                    dve.wait_ge(S["eb_ready"], n + 1)
                    dve.tensor_tensor(q_in[:], q[:], eb[:], ALU.mult).then_inc(S["qin_ready"], 1)
                    dve.wait_ge(S["enb_ready"], n + 1)
                    dve.tensor_tensor(k_in[:], key[:], enb[:], ALU.mult).then_inc(S["kin_ready"], 1)

                dve.tensor_scalar(one_lb[:], lb[:], -1.0, 1.0, ALU.mult, ALU.add)
                dve.drain()
                forget(0, True)
                running(0)
                keep_values(0, True)
                decayed(0, True)
                with dve.Fori(0, HEADS - 1) as n:
                    forget(n + 1, False)
                    masked_scores(n)
                    chain(n)
                    running(n + 1)
                    keep_values(n + 1, False)
                    decayed(n + 1, False)
                masked_scores(HEADS - 1)
                chain(HEADS - 1)

            @block.gpsimd
            def _(pool):
                def key_to_end(n, first):
                    pool.wait_ge(S["eleft_ready"], n + 1)
                    pool.wait_ge(S["key_ready"], n + 1)
                    if not first:
                        pool.wait_ge(S["keys_turned"], n)
                    pool.tensor_tensor(k_end[:], key[:], eleft[:], ALU.mult).then_inc(S["kend_ready"], 1)

                key_to_end(0, True)
                with pool.Fori(1, HEADS) as n:
                    key_to_end(n, False)

        normalize_heads(k, raw, squares, rstd, gate, ohT, [score])


def lower_bound_layer(k, lb):
    nc = k.nc
    with ExitStack() as ctx:
        top = k.sb(ctx, "lb_top", [P, HEADS])
        e = k.sb(ctx, "lb_e", [P, 2, HEADS])
        total = k.sb(ctx, "lb_total", [P, HEADS])
        shifted = k.sem(ctx, "lb_shifted")
        risen = k.sem(ctx, "lb_risen")
        with nc.Block() as block:
            @block.vector
            def _(dve):
                dve.tensor_tensor(top[:], k.col("lb0", 0, 8), k.col("lb1", 0, 8), ALU.max)
                dve.drain()
                dve.tensor_tensor(e[:, 0, :], k.col("lb0", 0, 8), top[:], ALU.subtract)
                dve.tensor_tensor(e[:, 1, :], k.col("lb1", 0, 8), top[:], ALU.subtract).then_inc(shifted, 1)
                dve.wait_ge(risen, 1)
                dve.tensor_tensor(total[:], e[:, 0, :], e[:, 1, :], ALU.add)
                dve.drain()
                dve.reciprocal(total[:], total[:])
                dve.drain()
                dve.tensor_tensor(lb[:], e[:, 0, :], total[:], ALU.mult)

            @block.scalar
            def _(act):
                act.wait_ge(shifted, 1)
                act.activation(e[:], e[:], ACT.Exp).then_inc(risen, 1)


def normalize_heads(k, raw, squares, rstd, gate, ohT, ps):
    nc = k.nc
    with ExitStack() as ctx:
        dev = k.sb(ctx, "hn_dev", [P, HEADS, TC])
        var_ready = k.sem(ctx, "hn_var_ready")
        dev_ready = k.sem(ctx, "hn_dev_ready")
        scaled = k.sem(ctx, "hn_scaled")
        rstd_ready = k.sem(ctx, "hn_rstd_ready")
        turned = k.sem(ctx, "hn_turned")
        kept = k.sem(ctx, "hn_kept")
        with nc.Block() as block:
            @block.vector
            def _(dve):
                dve.tensor_scalar(squares[:], squares[:], 1.0 / P, 1e-6, ALU.mult, ALU.add).then_inc(var_ready, 1)
                dve.wait_ge(dev_ready, 1)
                dve.reciprocal(rstd[:], dev[:]).then_inc(rstd_ready, 1)
                with dve.Fori(0, HEADS) as h:
                    dve.wait_ge(turned, h + 1)
                    dve.scalar_tensor_tensor(out=ohT[:, h, :], in0=ps[0][:, :], scalar=k.col("hg_norm_w", 0, 8)[:, bass.ds(h, 1)],
                                             in1=gate[:, h, :], op0=ALU.mult, op1=ALU.mult).then_inc(kept, 1)

            @block.scalar
            def _(act):
                act.wait_ge(var_ready, 1)
                act.activation(dev[:], squares[:], ACT.Sqrt).then_inc(dev_ready, 1)
                act.wait_ge(rstd_ready, 1)
                for h in range(HEADS):
                    for c in range(TC):
                        last = act.activation(raw[:, c, h, :], raw[:, c, h, :], ACT.Copy, scale=rstd[:, h, c:c + 1])
                    last.then_inc(scaled, 1)

            @block.tensor
            def _(pe):
                for h in range(HEADS):
                    pe.wait_ge(scaled, h + 1)
                    if h >= 1:
                        pe.wait_ge(kept, h)
                    for c in range(TC):
                        last = pe.transpose(ps[0][:, c * P:(c + 1) * P], raw[:, c, h, :], k.const("ident"))
                    last.then_inc(turned, 1)


def key_values(k, kvT, v_tok, gates, k_cmp, v_cmp, Tables):
    nc = k.nc
    w_kv, w_v, w_cmp = k.i["w_kv"], k.i["w_v"], k.i["w_cmp"]
    NV = 2 * GROUPS * P + 3 * HEADS
    with ExitStack() as ctx:
        w = [k.sb(ctx, f"kv_w{s}", [P, KC, P]) for s in range(2)]
        wv = k.sb(ctx, "kv_wv", [P, KC, NV])
        v_bias = k.sb(ctx, "kv_v_bias", [P, 4 * P])
        broadcast_rows(k, "kv_vb", [(k.col("b_in", 46, 2), v_bias[:, 0:256], 0.0), (k.col("b_in", 50, 2), v_bias[:, 256:512], 0.0)])
        ps = k.banks(ctx, "kv_ps", 2)
        psv = k.banks(ctx, "kv_psv", 2)
        psg, = k.banks(ctx, "kv_psg", 1)
        w_loaded = [k.sem(ctx, f"kv_w_loaded{s}") for s in range(2)]
        wv_loaded = k.sem(ctx, "kv_wv_loaded")
        projected = k.sem(ctx, "kv_projected")
        kept = k.sem(ctx, "kv_kept")
        v_projected = k.sem(ctx, "kv_v_projected")
        v_kept = k.sem(ctx, "kv_v_kept")
        g_projected = k.sem(ctx, "kv_g_projected")
        g_kept = k.sem(ctx, "kv_g_kept")
        with nc.Block() as block:
            @block.sync
            def _(sp):
                for s in range(2):
                    sp.dma_start(w[s][:], w_kv[s]).then_inc(w_loaded[s], 16)
                sp.dma_start(wv[:], w_v.rearrange("(k p) n -> p k n", p=P)).then_inc(wv_loaded, 16)
                with sp.Fori(1, 4) as it:
                    for s in range(2):
                        sp.wait_ge(projected, it * 2 + (s - 1))
                        sp.dma_start(w[s][:], w_kv[it * 2 + s]).then_inc(w_loaded[s], 16)

            @block.tensor
            def _(pe):
                def feature_major(it, s, first):
                    pe.wait_ge(w_loaded[s], it * 16 + 16)
                    if not first:
                        pe.wait_ge(kept, it * 2 + (s - 1))
                    for kc in range(KC):
                        last = pe.matmul(ps[s][:, :], w[s][:, kc, :], k.hT[:, kc, :], start=(kc == 0), stop=(kc == KC - 1))
                    last.then_inc(projected, 1)

                for s in range(2):
                    feature_major(0, s, True)
                with pe.Fori(1, 4) as it:
                    for s in range(2):
                        feature_major(it, s, False)
                pe.wait_ge(wv_loaded, 16)
                for c in range(TC):
                    if c >= 2:
                        pe.wait_ge(v_kept, c - 1)
                    for kc in range(KC):
                        last = pe.matmul(psv[c % 2][:, :], k.hT[:, kc, c * P:(c + 1) * P], wv[:, kc, 0:4 * P],
                                         start=(kc == 0), stop=(kc == KC - 1))
                    last.then_inc(v_projected, 1)
                for c in range(TC):
                    for kc in range(KC):
                        last = pe.matmul(psg[:, c * 24:(c + 1) * 24], k.hT[:, kc, c * P:(c + 1) * P], wv[:, kc, 4 * P:NV],
                                         start=(kc == 0), stop=(kc == KC - 1))
                last.then_inc(g_projected, 1)

            @block.scalar
            def _(act):
                for j, at in enumerate((40, 41, 42, 43, 44, 45, 48, 49)):
                    act.wait_ge(projected, j + 1)
                    act.activation(kvT[:, j, :], ps[j % 2][:, :], ACT.Identity, bias=k.col("b_in", at)).then_inc(kept, 1)
                act.wait_ge(g_kept, 1)
                act.activation(gates[:], gates[:], ACT.Sigmoid)

            @block.vector
            def _(dve):
                for c in range(TC):
                    dve.wait_ge(v_projected, c + 1)
                    dve.tensor_tensor(v_tok[:, c, :], psv[c % 2][:, :], v_bias[:], ALU.add).then_inc(v_kept, 1)
                dve.wait_ge(g_projected, 1)
                dve.tensor_tensor(gates[:], psg[:, 0:TC * 24].rearrange("p (c n) -> p c n", n=24),
                                  k.row("b_gate").unsqueeze(1).broadcast_to([P, TC, 24]), ALU.add).then_inc(g_kept, 1)

    NB = GROUPS * N_CMP
    with ExitStack() as ctx:
        w1 = [k.sb(ctx, f"cmp_w1_{s}", [P, CMP_BLOCK, P]) for s in range(2)]
        w2 = k.sb(ctx, "cmp_w2", [P, 2, P])
        bias = k.sb(ctx, "cmp_bias", [P, 2])
        pre = k.sb(ctx, "cmp_pre", [P, 2, NB])
        sig = k.sb(ctx, "cmp_sig", [P, 2, NB])
        ps, psp, psk, psv = k.banks(ctx, "cmp_ps", 4)
        loaded = [k.sem(ctx, f"cmp_loaded{s}") for s in range(2)]
        w2_loaded = k.sem(ctx, "cmp_w2_loaded")
        hidden_done = k.sem(ctx, "cmp_hidden_done")
        pre_ready = k.sem(ctx, "cmp_pre_ready")
        sig_ready = k.sem(ctx, "cmp_sig_ready")
        act_ready = k.sem(ctx, "cmp_act_ready")
        out_done = k.sem(ctx, "cmp_out_done")
        with nc.Block() as block:
            @block.sync
            def _(sp):
                for s in range(2):
                    sp.dma_start(w1[s][:], w_cmp[s].rearrange("(l d) h -> d l h", d=P)).then_inc(loaded[s], 16)
                sp.dma_start(w2[:], k.i["w_cmp2"].rearrange("s h d -> h s d")).then_inc(w2_loaded, 16)

            @block.tensor
            def _(pe):
                for s, pos in enumerate(("cmp_pos_k", "cmp_pos_v")):
                    pe.wait_ge(loaded[s], 16)
                    for l in range(CMP_BLOCK):
                        pe.matmul(ps[:, s * NB:(s + 1) * NB], w1[s][:, l, :],
                                  kvT[:, GROUPS * s:GROUPS * s + GROUPS, l:l + CMP_STRIDE * (N_CMP - 1) + 1:CMP_STRIDE],
                                  start=(l == 0), stop=(l == CMP_BLOCK - 1))
                        last = pe.matmul(psp[:, s:s + 1], w1[s][:, l, :], k.col(pos, l), start=(l == 0), stop=(l == CMP_BLOCK - 1))
                    last.then_inc(hidden_done, 1)
                pe.wait_ge(act_ready, 1)
                pe.wait_ge(w2_loaded, 16)
                pe.matmul(psk[:, 0:NB], w2[:, 0, :], pre[:, 0, :], start=True, stop=True)
                for g in range(GROUPS):
                    last = pe.matmul(psv[0:N_CMP, g * P:(g + 1) * P], pre[:, 1, g * N_CMP:(g + 1) * N_CMP], w2[:, 1, :],
                                     start=True, stop=True)
                last.then_inc(out_done, 1)

            @block.vector
            def _(dve):
                dve.memset(v_cmp[:], 0.0)
                for s, b1 in enumerate(("cmp_b1_k", "cmp_b1_v")):
                    dve.wait_ge(hidden_done, 2)
                    dve.tensor_scalar(bias[:, s:s + 1], psp[:, s:s + 1], k.col(b1), None, ALU.add)
                    dve.drain()
                    dve.tensor_scalar(pre[:, s, :], ps[:, s * NB:(s + 1) * NB], bias[:, s:s + 1], None, ALU.add).then_inc(pre_ready, 1)
                dve.wait_ge(sig_ready, 1)
                dve.tensor_tensor(pre[:], pre[:], sig[:], ALU.mult).then_inc(act_ready, 1)
                dve.wait_ge(out_done, 1)
                dve.tensor_copy(k_cmp[:], psk[:, 0:NB])
                dve.tensor_copy(v_cmp[0:N_CMP], psv[0:N_CMP, 0:GROUPS * P].rearrange("p (g e) -> p g e", e=P))

            @block.scalar
            def _(act):
                act.wait_ge(pre_ready, 2)
                act.activation(sig[:], pre[:], ACT.Sigmoid).then_inc(sig_ready, 1)

    with ExitStack() as ctx:
        onehot = k.sb(ctx, "bias_onehot", [BUCKETS + 1, BT_ROW])
        rel = k.sb(ctx, "bias_rel", [BUCKETS + 1, HEADS])
        r_sb = k.sb(ctx, "bias_r", [HEADS, BT_ROW])
        ps = k.banks(ctx, "bias_ps", 2)
        loaded = k.sem(ctx, "bias_loaded")
        neg_set = k.sem(ctx, "bias_neg_set")
        made = k.sem(ctx, "bias_made")
        kept = k.sem(ctx, "bias_kept")
        spread = k.sem(ctx, "bias_spread")
        with nc.Block() as block:
            @block.sync
            def _(sp):
                sp.dma_start(onehot[:], k.i["buckets"]).then_inc(loaded, 16)
                sp.wait_ge(neg_set, 1)
                sp.dma_start(rel[0:BUCKETS, :], k.i["rel_bias"]).then_inc(loaded, 16)
                sp.wait_ge(kept, 2)
                for h in range(HEADS):
                    sp.dma_start(Tables[h], r_sb[h:h + 1, :].unsqueeze(1).broadcast_to([1, P, BT_ROW])).then_inc(spread, 16)
                sp.wait_ge(spread, 16 * HEADS)

            @block.tensor
            def _(pe):
                pe.wait_ge(loaded, 32)
                for j in range(2):
                    pe.matmul(ps[j][0:HEADS, :], rel[:], onehot[:, j * 512:(j + 1) * 512], start=True, stop=True).then_inc(made, 1)

            @block.vector
            def _(dve):
                dve.memset(rel[:], NEG).then_inc(neg_set, 1)
                for j in range(2):
                    dve.wait_ge(made, j + 1)
                    dve.tensor_copy(r_sb[:, j * 512:(j + 1) * 512], ps[j][0:HEADS, :]).then_inc(kept, 1)


def sparse_attention(k, onT):
    nc = k.nc
    UNITS = [(br, c) for br in range(2) for c in range(TC)]
    NU = len(UNITS) + 1
    with ExitStack() as ctx:
        kvT = k.sb(ctx, "at_kvT", [P, 8, SEQ])
        v_tok = k.sb(ctx, "at_v_tok", [P, TC, 512])
        gates = k.sb(ctx, "at_gates", [P, TC, 24])
        k_cmp = k.sb(ctx, "at_k_cmp", [P, GROUPS * N_CMP])
        v_cmp = k.sb(ctx, "at_v_cmp", [P, GROUPS, P])
        spread = nc.dram_tensor("bias_spread_rows", [HEADS, P, BT_ROW], F32).ap()
        key_values(k, kvT, v_tok, gates, k_cmp, v_cmp, spread)

        wq = [k.sb(ctx, f"at_wq{s}", [P, KC, P]) for s in range(2)]
        q = [k.sb(ctx, f"at_q{s}", [P, SEQ]) for s in range(2)]
        q_bias = k.sb(ctx, "at_q_bias", [P, HEADS])
        table = [k.sb(ctx, f"at_table{s}", [P, BTW]) for s in range(2)]
        values = k.sb(ctx, "at_values", [P, 2, TC, P])
        cvalues = k.sb(ctx, "at_cvalues", [P, P])
        NP = 4
        p = [k.sb(ctx, f"at_p{s}", [P, SEQ]) for s in range(NP)]
        top = k.sb(ctx, "at_top", [P, NU, TC])
        ntop = k.sb(ctx, "at_ntop", [P, NU, TC])
        total = k.sb(ctx, "at_total", [P, NU, TC])
        factor = k.sb(ctx, "at_factor", [P, NU, TC])
        pT = [k.sb(ctx, f"at_pT{s}", [P, SEQ]) for s in range(2)]
        cpT = k.sb(ctx, "at_cpT", [P, SEQ])
        spare = k.sb(ctx, "at_spare", [P, 2])

        sc = k.banks(ctx, "at_sc", 3)
        tr = k.banks(ctx, "at_tr", 2)
        o_ps, = k.banks(ctx, "at_o", 1)
        proj, = k.banks(ctx, "at_proj", 1)

        names = ("wq_loaded0 wq_loaded1 table_loaded0 table_loaded1 q_projected q_kept bias_ready "
                 "scored logits_ready exp_ready factor_ready p_ready turned pT_ready mixed o_kept values_ready cleared").split()
        S = {n: k.sem(ctx, "at_" + n) for n in names}

        def pairs(eng, head):
            head(0, 0, 0)
            head(1, 1, 0)
            with eng.Fori(1, HEADS // 2 - 1) as it:
                head(it * 2, 0, it - 1)
                head(it * 2 + 1, 1, it - 1)
            head(HEADS - 2, 0, GROUPS - 1)
            head(HEADS - 1, 1, GROUPS - 1)

        def loads(h, s):
            return 16 * (h // 2 + 1) if isinstance(h, int) else (h - s) * 8 + 16

        def after_first(h):
            return not isinstance(h, int) or h > 0

        with nc.Block() as block:
            @block.sync
            def _(sp):
                def load_head(h, s, g):
                    if not isinstance(h, int) or h >= 2:
                        sp.wait_ge(S["q_projected"], h - 1)
                    sp.dma_start(wq[s][:], k.i["w_nq"][h]).then_inc(S[f"wq_loaded{s}"], 16)
                    if not isinstance(h, int) or h >= 2:
                        sp.wait_ge(S["logits_ready"], (h - 1) * NU)
                    view = spread[h].rearrange("p m -> (p m)")[P - 1:P - 1 + P * (BT_ROW - 1)]
                    view = view.rearrange("(p m) -> p m", m=BT_ROW - 1)[:, 0:BTW]
                    sp.dma_start(table[s][:], view).then_inc(S[f"table_loaded{s}"], 16)

                pairs(sp, load_head)

            @block.tensor
            def _(pe):
                def project(h, s):
                    pe.wait_ge(S[f"wq_loaded{s}"], loads(h, s))
                    if after_first(h):
                        pe.wait_ge(S["q_kept"], h)
                    for kc in range(KC):
                        last = pe.matmul(proj[:, :], wq[s][:, kc, :], k.hT[:, kc, :], start=(kc == 0), stop=(kc == KC - 1))
                    last.then_inc(S["q_projected"], 1)

                def scores(h, s, g, u):
                    if u >= 3 or after_first(h):
                        pe.wait_ge(S["logits_ready"], h * NU + (u - 2))
                    if u == 0:
                        pe.wait_ge(S["q_kept"], h + 1)
                    if u < len(UNITS):
                        br, c = UNITS[u]
                        keys = kvT[:, 4 + GROUPS * br:4 + GROUPS * (br + 1), :]
                        last = pe.matmul(sc[u % 3][:, 0:(c + 1) * P], q[s][:, c * P:(c + 1) * P],
                                         keys[:, g, 0:(c + 1) * P], start=True, stop=True)
                    else:
                        for c in range(TC):
                            last = pe.matmul(sc[u % 3][:, c * N_CMP:(c + 1) * N_CMP], q[s][:, c * P:(c + 1) * P],
                                             k_cmp[:, bass.ts(g, N_CMP)], start=True, stop=True)
                    last.then_inc(S["scored"], 1)

                def turn(h, u):
                    pe.wait_ge(S["p_ready"], h * NU + (u + 1))
                    if u >= 2 or after_first(h):
                        pe.wait_ge(S["pT_ready"], h * NU + (u - 1))
                    if u < len(UNITS):
                        for kk in range(UNITS[u][1] + 1):
                            last = pe.transpose(tr[u % 2][:, kk * P:(kk + 1) * P], p[u % NP][:, kk * P:(kk + 1) * P], k.const("ident"))
                    else:
                        for c in range(TC):
                            last = pe.transpose(tr[u % 2][0:N_CMP, c * P:(c + 1) * P],
                                                p[u % NP][:, c * N_CMP:(c + 1) * N_CMP], k.const("ident"))
                    last.then_inc(S["turned"], 1)

                def mix(h, u):
                    pe.wait_ge(S["pT_ready"], h * NU + (u + 1))
                    if u == 0:
                        pe.wait_ge(S["values_ready"], h + 1)
                        if after_first(h):
                            pe.wait_ge(S["o_kept"], h)
                    if u < len(UNITS):
                        br, c = UNITS[u]
                        for kk in range(c + 1):
                            last = pe.matmul(o_ps[:, c * P:(c + 1) * P], values[:, br, kk, :], pT[u % 2][:, kk * P:(kk + 1) * P],
                                             start=(u == 0), stop=False, skip_group_check=True)
                    else:
                        last = pe.matmul(o_ps[:, :], cvalues[:], cpT[:], start=False, stop=True, skip_group_check=True)
                    last.then_inc(S["mixed"], 1)

                def head(h, s, g):
                    for u in range(3):
                        scores(h, s, g, u)
                    if not (isinstance(h, int) and h == HEADS - 1):
                        project(h + 1, 1 - s)
                    for u in range(NU):
                        turn(h, u)
                        if u + 3 < NU:
                            scores(h, s, g, u + 3)
                        if u >= 1:
                            mix(h, u - 1)
                    mix(h, NU - 1)

                project(0, 0)
                pairs(pe, head)

            @block.scalar
            def _(act):
                act.activation(q_bias[:], k.col("b_in", 32, 8), ACT.Copy, scale=ATT_SCALE).then_inc(S["bias_ready"], 1)
                act.wait_ge(S["bias_ready"], 1)

                def keep_q(h, s):
                    act.wait_ge(S["q_projected"], h + 1)
                    act.activation(q[s][:], proj[:, :], ACT.Identity, bias=q_bias[:, bass.ds(h, 1)], scale=ATT_SCALE).then_inc(S["q_kept"], 1)

                def weights(h, u):
                    act.wait_ge(S["logits_ready"], h * NU + (u + 1))
                    if u < len(UNITS):
                        n = (UNITS[u][1] + 1) * P
                        act.activation(p[u % NP][:, 0:n], p[u % NP][:, 0:n], ACT.Exp, bias=ntop[:, u, 0:1],
                                       accum_out=total[:, u, 0:1]).then_inc(S["exp_ready"], 1)
                    else:
                        for c in range(TC):
                            last = act.activation(p[u % NP][:, c * N_CMP:(c + 1) * N_CMP], p[u % NP][:, c * N_CMP:(c + 1) * N_CMP],
                                                  ACT.Exp, bias=ntop[:, u, c:c + 1], accum_out=total[:, u, c:c + 1])
                        last.then_inc(S["exp_ready"], 1)

                def keep_turned(h, u):
                    act.wait_ge(S["turned"], h * NU + (u + 1))
                    if u < len(UNITS):
                        if u >= 2 or after_first(h):
                            act.wait_ge(S["mixed"], h * NU + (u - 1))
                        n = (UNITS[u][1] + 1) * P
                        act.activation(pT[u % 2][:, 0:n], tr[u % 2][:, 0:n], ACT.Copy).then_inc(S["pT_ready"], 1)
                    else:
                        if after_first(h):
                            act.wait_ge(S["mixed"], h * NU)
                        else:
                            act.wait_ge(S["cleared"], 1)
                        act.activation(cpT[0:N_CMP, :], tr[u % 2][0:N_CMP, :], ACT.Copy).then_inc(S["pT_ready"], 1)

                def head(h, s, g):
                    for u in range(NU + 2):
                        if u < NU:
                            weights(h, u)
                        if u == 2 and not (isinstance(h, int) and h == HEADS - 1):
                            keep_q(h + 1, 1 - s)
                        if u >= 2:
                            keep_turned(h, u - 2)

                keep_q(0, 0)
                pairs(act, head)

            @block.vector
            def _(dve):
                dve.memset(cpT[:], 0.0).then_inc(S["cleared"], 1)

                def logits(h, s, u):
                    if u == 0:
                        dve.wait_ge(S[f"table_loaded{s}"], loads(h, s))
                    dve.wait_ge(S["scored"], h * NU + (u + 1))
                    if u >= NP or after_first(h):
                        dve.wait_ge(S["turned"], h * NU + (u - NP + 1 if u >= NP else 0))
                    dve.memset(spare[:, 0:1], 0.0)
                    buf, bank = p[u % NP], sc[u % 3]
                    if u < len(UNITS):
                        n = (UNITS[u][1] + 1) * P
                        dve.tensor_tensor_reduce(buf[:, 0:n], bank[:, 0:n], table[s][:, BT0 + P - n:BT0 + P], 1.0, NEG * 10,
                                                 ALU.add, ALU.max, top[:, u, 0:1])
                        dve.drain()
                        dve.tensor_scalar(ntop[:, u, 0:1], top[:, u, 0:1], -1.0, None, ALU.mult).then_inc(S["logits_ready"], 1)
                    else:
                        for c in range(TC):
                            at = BT0 + CMP_BLOCK - 1 - c * P
                            dve.tensor_tensor_reduce(buf[:, c * N_CMP:(c + 1) * N_CMP], bank[:, c * N_CMP:(c + 1) * N_CMP],
                                                     table[s][:, at:at + CMP_STRIDE * (N_CMP - 1) + 1:CMP_STRIDE], 1.0, NEG * 10,
                                                     ALU.add, ALU.max, top[:, u, c:c + 1])
                        dve.drain()
                        dve.tensor_scalar(ntop[:, u, :], top[:, u, :], -1.0, None, ALU.mult).then_inc(S["logits_ready"], 1)

                def normalized(h, u):
                    dve.wait_ge(S["exp_ready"], h * NU + (u + 1))
                    nr = 1 if u < len(UNITS) else TC
                    dve.reciprocal(factor[:, u, 0:nr], total[:, u, 0:nr])
                    dve.drain()
                    buf = p[u % NP]
                    if u < len(UNITS):
                        br, c = UNITS[u]
                        n = (c + 1) * P
                        dve.tensor_scalar(buf[:, 0:n], buf[:, 0:n], factor[:, u, 0:1], gates[:, c, bass.ds(h * 3 + (1 + br), 1)],
                                          ALU.mult, ALU.mult).then_inc(S["p_ready"], 1)
                    else:
                        for c in range(TC):
                            blk = buf[:, c * N_CMP:(c + 1) * N_CMP]
                            dve.tensor_scalar(blk, blk, factor[:, u, c:c + 1], gates[:, c, bass.ds(h * 3, 1)], ALU.mult, ALU.mult)
                        dve.drain()
                        blk = buf[:, 0:TC * N_CMP]
                        dve.tensor_tensor(blk, blk, k.const("cmp_ok"), ALU.mult).then_inc(S["p_ready"], 1)

                def head(h, s, g):
                    for u in range(NU + 1):
                        if u < NU:
                            logits(h, s, u)
                        if u >= 1:
                            normalized(h, u - 1)
                    dve.wait_ge(S["mixed"], h * NU + NU)
                    dve.tensor_copy(onT[:, h, :], o_ps[:, :]).then_inc(S["o_kept"], 1)

                pairs(dve, head)

            @block.gpsimd
            def _(pool):
                def stage_values(h, s, g):
                    if after_first(h):
                        pool.wait_ge(S["mixed"], h * NU)
                        pool.tensor_tensor(spare[:, 1:2], k.const("ones", 0, 1), k.const("ones", 0, 1), ALU.add)
                    v_v = v_tok[:].rearrange("p c (b e) -> p c b e", e=P)
                    for br in range(2):
                        pool.tensor_copy(values[:, br, :, :], v_v[:, :, 2 * br:2 * br + 2, :][:, :, g, :])
                    pool.tensor_copy(cvalues[:], v_cmp[:, g, :]).then_inc(S["values_ready"], 1)

                pairs(pool, stage_values)


def merge_branches(k, ohT, onT, mergedT):
    nc = k.nc
    with ExitStack() as ctx:
        w = [k.sb(ctx, f"mg_w{s}", [P, KC, P]) for s in range(4)]
        sig = [k.sb(ctx, f"mg_sig{s}", [P, SEQ]) for s in range(2)]
        part = [k.sb(ctx, f"mg_part{s}", [P, SEQ]) for s in range(2)]
        ps = k.banks(ctx, "mg_ps", 4)
        loaded = [k.sem(ctx, f"mg_loaded{s}") for s in range(4)]
        done = [k.sem(ctx, f"mg_done{s}") for s in range(4)]
        sig_ready = [k.sem(ctx, f"mg_sig_ready{s}") for s in range(2)]
        part_ready = [k.sem(ctx, f"mg_part_ready{s}") for s in range(2)]
        sources = (k.hT, k.hT, ohT, onT)
        with nc.Block() as block:
            @block.sync
            def _(sp):
                for s in range(4):
                    sp.dma_start(w[s][:], k.i["w_merge"][0, s]).then_inc(loaded[s], 16)
                with sp.Fori(1, KC) as j:
                    for s in range(4):
                        sp.wait_ge(done[s], j)
                        sp.dma_start(w[s][:], k.i["w_merge"][j, s]).then_inc(loaded[s], 16)

            @block.tensor
            def _(pe):
                def step(j, first):
                    for s in range(4):
                        pe.wait_ge(loaded[s], j * 16 + 16)
                        if not first:
                            pe.wait_ge(sig_ready[s] if s < 2 else part_ready[s - 2], j)
                        for kc in range(KC):
                            last = pe.matmul(ps[s][:, :], w[s][:, kc, :], sources[s][:, kc, :], start=(kc == 0), stop=(kc == KC - 1))
                        last.then_inc(done[s], 1)

                step(0, True)
                with pe.Fori(1, KC) as j:
                    step(j, False)

            @block.scalar
            def _(act):
                def step(j, first):
                    for s in range(2):
                        act.wait_ge(done[s], j + 1)
                        if not first:
                            act.wait_ge(part_ready[s], j)
                        act.activation(sig[s][:], ps[s][:, :], ACT.Sigmoid, bias=k.col("b_mg", 8 * s, 8)[:, bass.ds(j, 1)]).then_inc(sig_ready[s], 1)

                step(0, True)
                with act.Fori(1, KC) as j:
                    step(j, False)

            @block.vector
            def _(dve):
                with dve.Fori(0, KC) as j:
                    for s in range(2):
                        dve.wait_ge(done[2 + s], j + 1)
                        dve.wait_ge(sig_ready[s], j + 1)
                        dve.tensor_tensor(part[s][:], sig[s][:], ps[2 + s][:, :], ALU.mult).then_inc(part_ready[s], 1)
                    dve.drain()
                    dve.tensor_tensor(mergedT[:, j, :], part[0][:], part[1][:], ALU.add)
                    dve.drain()


def project_out(k, tag, weights, source, gain, residual):
    nc = k.nc
    HALF = 512
    with ExitStack() as ctx:
        w = [k.sb(ctx, f"{tag}_w{s}", [P, KC, HALF]) for s in range(2)]
        part = [k.sb(ctx, f"{tag}_part{s}", [P, HALF]) for s in range(2)]
        ps = k.banks(ctx, f"{tag}_ps", 2)
        loaded = [k.sem(ctx, f"{tag}_loaded{s}") for s in range(2)]
        done = k.sem(ctx, f"{tag}_done")
        kept = k.sem(ctx, f"{tag}_kept")
        w_v = weights.rearrange("(k p) n -> p k n", p=P)
        units = [(h, c) for h in range(2) for c in range(TC)]
        with nc.Block() as block:
            @block.sync
            def _(sp):
                for h in range(2):
                    sp.dma_start(w[h][:], w_v[:, :, h * HALF:(h + 1) * HALF]).then_inc(loaded[h], 16)

            @block.tensor
            def _(pe):
                for n, (h, c) in enumerate(units):
                    if c == 0:
                        pe.wait_ge(loaded[h], 16)
                    if n >= 2:
                        pe.wait_ge(kept, n - 1)
                    for kc in range(KC):
                        last = pe.matmul(ps[n % 2][:, :], source[:, kc, c * P:(c + 1) * P], w[h][:, kc, :],
                                         start=(kc == 0), stop=(kc == KC - 1))
                    last.then_inc(done, 1)

            @block.vector
            def _(dve):
                for n, (h, c) in enumerate(units):
                    cut = slice(h * HALF, (h + 1) * HALF)
                    dve.wait_ge(done, n + 1)
                    dve.tensor_tensor(part[n % 2][:], ps[n % 2][:, :], gain[:, cut], ALU.mult).then_inc(kept, 1)
                    dve.wait_ge(kept, n + 1)
                    dve.scalar_tensor_tensor(out=k.x[:, c, cut], in0=k.x[:, c, cut], scalar=float(residual), in1=part[n % 2][:],
                                             op0=ALU.mult, op1=ALU.add)


def route(k, tag, weights, bias_row, slot_of, comb, most):
    nc = k.nc
    with ExitStack() as ctx:
        w = k.sb(ctx, f"{tag}_w", [P, KC, N_GRP + N_EXP])
        lg = k.sb(ctx, f"{tag}_lg", [P, TC, N_GRP + N_EXP])
        small = {n: k.sb(ctx, f"{tag}_{n}", [P, TC]) for n in ("gtop", "gsum", "gp", "m", "m1", "m2", "d", "w1", "w2")}
        ge = k.sb(ctx, f"{tag}_ge", [P, TC, N_GRP])
        goh = k.sb(ctx, f"{tag}_goh", [P, TC, N_GRP])
        pen = k.sb(ctx, f"{tag}_pen", [P, TC, N_EXP])
        el = k.sb(ctx, f"{tag}_el", [P, TC, N_EXP])
        eq = k.sb(ctx, f"{tag}_eq", [P, TC, N_EXP])
        oh = [k.sb(ctx, f"{tag}_oh{s}", [P, TC, N_EXP]) for s in range(2)]
        chosen = k.sb(ctx, f"{tag}_chosen", [P, TC, N_EXP])
        mostf = k.sb(ctx, f"{tag}_mostf", [P, 1])
        ps = k.banks(ctx, f"{tag}_ps", 3)
        w_loaded = k.sem(ctx, f"{tag}_w_loaded")
        logits_done = k.sem(ctx, f"{tag}_logits_done")
        shifted = k.sem(ctx, f"{tag}_shifted")
        risen = k.sem(ctx, f"{tag}_risen")
        chosen_ready = k.sem(ctx, f"{tag}_chosen_ready")
        counted = k.sem(ctx, f"{tag}_counted")
        with nc.Block() as block:
            @block.sync
            def _(sp):
                sp.dma_start(w[:], weights.rearrange("(k p) n -> p k n", p=P)).then_inc(w_loaded, 16)

            @block.tensor
            def _(pe):
                pe.wait_ge(w_loaded, 16)
                NL = N_GRP + N_EXP
                for c in range(TC):
                    for kc in range(KC):
                        last = pe.matmul(ps[0][:, c * NL:(c + 1) * NL], k.hT[:, kc, c * P:(c + 1) * P], w[:, kc, :],
                                         start=(kc == 0), stop=(kc == KC - 1))
                last.then_inc(logits_done, 1)
                pe.wait_ge(chosen_ready, 1)
                for c in range(TC):
                    for b in range(c + 1):
                        pe.matmul(ps[1][:, c * N_EXP:(c + 1) * N_EXP], k.const("before") if b == c else k.const("ones"),
                                  chosen[:, b, :], start=(b == 0), stop=(b == c))
                for b in range(TC):
                    last = pe.matmul(ps[2][:, 0:N_EXP], k.const("ones"), chosen[:, b, :], start=(b == 0), stop=(b == TC - 1))
                last.then_inc(counted, 1)

            @block.scalar
            def _(act):
                act.wait_ge(shifted, 1)
                act.activation(ge[:], ge[:], ACT.Exp).then_inc(risen, 1)
                act.wait_ge(shifted, 2)
                act.activation(small["d"][:], small["d"][:], ACT.Exp).then_inc(risen, 1)

            @block.vector
            def _(dve):
                def per_token(a, n):
                    return a[:].unsqueeze(2).broadcast_to([P, TC, n])

                def first_best(values, n, top, out):
                    dve.tensor_reduce(top[:], values, AX.X, ALU.max)
                    dve.drain()
                    dve.tensor_tensor(out, values, per_token(top, n), ALU.is_equal)
                    dve.drain()
                    dve.tensor_tensor(out, out, k.const("first", 0, n).unsqueeze(1).broadcast_to([P, TC, n]), ALU.mult)
                    dve.drain()
                    dve.tensor_reduce(small["m"][:], out, AX.X, ALU.max)
                    dve.drain()
                    dve.tensor_tensor(out, out, per_token(small["m"], n), ALU.is_equal)
                    dve.drain()

                dve.wait_ge(logits_done, 1)
                NL = N_GRP + N_EXP
                dve.tensor_tensor(lg[:], ps[0][:, 0:TC * NL].rearrange("p (c n) -> p c n", n=NL),
                                  bias_row.unsqueeze(1).broadcast_to([P, TC, NL]), ALU.add)
                dve.drain()
                first_best(lg[:, :, 0:N_GRP], N_GRP, small["gtop"], goh[:])
                dve.tensor_tensor(ge[:], lg[:, :, 0:N_GRP], per_token(small["gtop"], N_GRP), ALU.subtract).then_inc(shifted, 1)
                dve.tensor_scalar(pen[:].rearrange("p c (g e) -> p c g e", e=PER_GRP),
                                  goh[:].unsqueeze(3).broadcast_to([P, TC, N_GRP, PER_GRP]), 1.0, -NEG, ALU.subtract, ALU.mult)
                dve.drain()
                dve.tensor_tensor(el[:], lg[:, :, N_GRP:NL], pen[:], ALU.add)
                dve.drain()
                first_best(el[:], N_EXP, small["m1"], oh[0][:])
                dve.tensor_scalar(pen[:], oh[0][:], 2 * NEG, None, ALU.mult)
                dve.drain()
                dve.tensor_tensor(el[:], el[:], pen[:], ALU.add)
                dve.drain()
                first_best(el[:], N_EXP, small["m2"], oh[1][:])
                dve.tensor_tensor(chosen[:], oh[0][:], oh[1][:], ALU.add).then_inc(chosen_ready, 1)
                dve.tensor_tensor(small["d"][:], small["m2"][:], small["m1"][:], ALU.subtract).then_inc(shifted, 1)
                dve.wait_ge(risen, 2)
                dve.tensor_reduce(small["gsum"][:], ge[:], AX.X, ALU.add)
                dve.tensor_scalar(small["w1"][:], small["d"][:], 1.0, None, ALU.add)
                dve.drain()
                dve.tensor_tensor(small["w1"][:], small["w1"][:], small["gsum"][:], ALU.mult)
                dve.drain()
                dve.reciprocal(small["w1"][:], small["w1"][:])
                dve.drain()
                dve.tensor_tensor(small["w2"][:], small["w1"][:], small["d"][:], ALU.mult)
                dve.tensor_tensor(comb[:], oh[0][:], per_token(small["w1"], N_EXP), ALU.mult)
                dve.drain()
                dve.tensor_tensor(el[:], oh[1][:], per_token(small["w2"], N_EXP), ALU.mult)
                dve.drain()
                dve.tensor_tensor(comb[:], comb[:], el[:], ALU.add)
                dve.wait_ge(counted, 1)
                dve.tensor_scalar(slot_of[:], ps[1][:, 0:TC * N_EXP].rearrange("p (c n) -> p c n", n=N_EXP), 1.0, None, ALU.add)
                dve.tensor_reduce(mostf[:], ps[2][:, 0:N_EXP], AX.X, ALU.max)
                dve.drain()
                dve.tensor_tensor(slot_of[:], slot_of[:], chosen[:], ALU.mult)
                dve.tensor_copy(most[:], mostf[:])
                dve.drain()
                dve.tensor_scalar(slot_of[:], slot_of[:], -1.0, None, ALU.add)


def experts(k, tag, F, up_parts, down, source, scale, shift, slot_of, comb, most, y):
    nc = k.nc
    FC = F // P
    down_v = down.rearrange("e (f p) n -> e p f n", p=P)
    passes = SEQ // SLOTS
    S2 = 2 * SLOTS
    NU = len(up_parts)
    with ExitStack() as ctx:
        wu = [[k.sb(ctx, f"{tag}_wu{u}{e}", [P, KC, 512]) for e in range(2)] for u in range(NU)]
        wd = [k.sb(ctx, f"{tag}_wd{e}", [P, FC, D]) for e in range(2)]
        pick = k.sb(ctx, f"{tag}_pick", [P, TC, S2])
        picked = k.sb(ctx, f"{tag}_picked", [P, TC, S2])
        slots = k.sb(ctx, f"{tag}_slots", [P, SLOTS])
        back = k.sb(ctx, f"{tag}_back", [P, SEQ])
        hg = k.sb(ctx, f"{tag}_hg", [P, KC, S2])
        sig = k.sb(ctx, f"{tag}_sig", [P, F])
        mid = k.sb(ctx, f"{tag}_mid", [P, F])
        midT = k.sb(ctx, f"{tag}_midT", [P, FC, S2])
        res = k.sb(ctx, f"{tag}_res", [P, D])

        turn_ps, = k.banks(ctx, f"{tag}_turn", 1)
        rows_ps, = k.banks(ctx, f"{tag}_rows", 1)
        up_ps = k.banks(ctx, f"{tag}_up", 2)
        res_ps = k.banks(ctx, f"{tag}_res_ps", 2)
        y_ps = k.banks(ctx, f"{tag}_y", 2)

        def run(first_pass, one_pass):
            with ExitStack() as sems:
                names = ("pick_ready back_turned back_kept rows_done rows_kept up_done0 up_done1 sig_ready mid_ready mid_turned "
                         "midT_kept down_done res_kept y_done y_kept").split()
                S = {n: k.sem(sems, f"{tag}{first_pass}_{n}") for n in names}
                u_loaded = [[k.sem(sems, f"{tag}{first_pass}_u_loaded{u}{e}") for e in range(2)] for u in range(NU)]
                d_loaded = [k.sem(sems, f"{tag}{first_pass}_d_loaded{e}") for e in range(2)]

                def loop(eng, body, next_pass=None):
                    def one():
                        body(0, 0, True)
                        with eng.Fori(1, PAIRS) as m:
                            body(m, m, False)

                    if one_pass:
                        one()
                        return
                    busiest = eng.value_load(most[0:1, 0:1], min_val=0, max_val=SEQ)
                    with eng.If(busiest > first_pass * SLOTS):
                        one()
                        with eng.Fori(first_pass + 1, passes) as j:
                            if next_pass:
                                next_pass()
                            with eng.Fori(0, PAIRS) as m:
                                body(m, (j - first_pass) * PAIRS + m, False)

                with nc.Block() as block:
                    @block.sync
                    def _(sp):
                        def body(m, n, first):
                            for u in range(NU):
                                for e in range(2):
                                    if not first:
                                        sp.wait_ge(S[f"up_done{u}"], n)
                                    sp.dma_start(wu[u][e][:], up_parts[u].rearrange("e (k p) n -> e p k n", p=P)[m * 2 + e]).then_inc(u_loaded[u][e], 16)
                            for e in range(2):
                                if not first:
                                    sp.wait_ge(S["down_done"], n)
                                sp.dma_start(wd[e][:], down_v[m * 2 + e]).then_inc(d_loaded[e], 16)

                        loop(sp, body)

                    @block.tensor
                    def _(pe):
                        def body(m, n, first):
                            pe.wait_ge(S["pick_ready"], n + 1)
                            if not first:
                                pe.wait_ge(S["midT_kept"], n)
                            for c in range(TC):
                                last = pe.transpose(turn_ps[:, c * P:(c + 1) * P], picked[:, c, :], k.const("ident"))
                            last.then_inc(S["back_turned"], 1)
                            for half in range(2):
                                if half or not first:
                                    pe.wait_ge(S["rows_kept"], n * 2 + half)
                                for q in range(4):
                                    kc = half * 4 + q
                                    for c in range(TC):
                                        last = pe.matmul(rows_ps[:, q * P:(q + 1) * P], source[:, c, kc * P:(kc + 1) * P], pick[:, c, :],
                                                         start=(c == 0), stop=(c == TC - 1))
                                last.then_inc(S["rows_done"], 1)
                            pe.wait_ge(S["rows_kept"], n * 2 + 2)
                            for u in range(NU):
                                for e in range(2):
                                    pe.wait_ge(u_loaded[u][e], n * 16 + 16)
                                if not first:
                                    pe.wait_ge(S["mid_ready"], n)
                                for kc in range(KC):
                                    for e in range(2):
                                        last = pe.matmul(up_ps[u][e * SLOTS:(e + 1) * SLOTS, :], hg[:, kc, e * SLOTS:(e + 1) * SLOTS],
                                                         wu[u][e][:, kc, :], start=(kc == 0), stop=(kc == KC - 1))
                                last.then_inc(S[f"up_done{u}"], 1)
                            pe.wait_ge(S["mid_ready"], n + 1)
                            pe.wait_ge(S["back_kept"], n + 1)
                            for f in range(FC):
                                last = pe.transpose(turn_ps[:, f * P:(f + 1) * P], mid[:, f * P:(f + 1) * P], k.const("ident"))
                            last.then_inc(S["mid_turned"], 1)
                            pe.wait_ge(S["midT_kept"], n + 1)
                            for e in range(2):
                                pe.wait_ge(d_loaded[e], n * 16 + 16)
                            if not first:
                                pe.wait_ge(S["res_kept"], n)
                            for half in range(2):
                                for f in range(FC):
                                    for e in range(2):
                                        last = pe.matmul(res_ps[half][e * SLOTS:(e + 1) * SLOTS, :], midT[:, f, e * SLOTS:(e + 1) * SLOTS],
                                                         wd[e][:, f, half * 512:(half + 1) * 512], start=(f == 0), stop=(f == FC - 1))
                            last.then_inc(S["down_done"], 1)
                            pe.wait_ge(S["res_kept"], n + 1)
                            for c in range(TC):
                                for half in range(2):
                                    i = c * 2 + half
                                    if i >= 2 or not first:
                                        pe.wait_ge(S["y_kept"], n * 8 + (i - 1))
                                    pe.matmul(y_ps[half][:, :], back[:, c * P:(c + 1) * P], res[:, half * 512:(half + 1) * 512],
                                              start=True, stop=True).then_inc(S["y_done"], 1)

                        loop(pe, body)

                    @block.scalar
                    def _(act):
                        def body(m, n, first):
                            act.wait_ge(S["back_turned"], n + 1)
                            if not first:
                                act.wait_ge(S["y_done"], n * 8)
                            act.activation(back[:], turn_ps[:, :], ACT.Copy).then_inc(S["back_kept"], 1)
                            for half in range(2):
                                act.wait_ge(S["rows_done"], n * 2 + (half + 1))
                                if half == 0 and not first:
                                    act.wait_ge(S[f"up_done{NU - 1}"], n)
                                for q in range(4):
                                    kc = half * 4 + q
                                    last = act.activation(hg[:, kc, :], rows_ps[:, q * P:(q + 1) * P], ACT.Identity,
                                                          scale=scale[:, kc:kc + 1], bias=shift[:, kc:kc + 1])
                                last.then_inc(S["rows_kept"], 1)
                            act.wait_ge(S["up_done0"], n + 1)
                            act.activation(sig[:], up_ps[0][:, 0:F], ACT.Sigmoid).then_inc(S["sig_ready"], 1)
                            act.wait_ge(S["mid_turned"], n + 1)
                            act.activation(midT[:], turn_ps[:, 0:FC * P], ACT.Copy).then_inc(S["midT_kept"], 1)
                            act.wait_ge(S["down_done"], n + 1)
                            for half in range(2):
                                last = act.activation(res[:, half * 512:(half + 1) * 512], res_ps[half][:, :], ACT.Copy)
                            last.then_inc(S["res_kept"], 1)

                        loop(act, body)

                    @block.vector
                    def _(dve):
                        def picks(m, n, first):
                            if not first:
                                dve.wait_ge(S["back_turned"], n)
                                dve.wait_ge(S["rows_done"], n * 2)
                            pick_v = pick[:].rearrange("p c (e s) -> p c e s", s=SLOTS)
                            dve.tensor_tensor(pick_v, slots[:].unsqueeze(1).unsqueeze(1).broadcast_to([P, TC, 2, SLOTS]),
                                              slot_of[:, :, bass.ts(m, 2)].unsqueeze(3).broadcast_to([P, TC, 2, SLOTS]), ALU.is_equal)
                            dve.drain()
                            dve.tensor_tensor(picked[:].rearrange("p c (e s) -> p c e s", s=SLOTS), pick_v,
                                              comb[:, :, bass.ts(m, 2)].unsqueeze(3).broadcast_to([P, TC, 2, SLOTS]), ALU.mult).then_inc(S["pick_ready"], 1)

                        def middle(n):
                            dve.wait_ge(S["sig_ready"], n + 1)
                            dve.wait_ge(S[f"up_done{NU - 1}"], n + 1)
                            dve.tensor_tensor(sig[:], sig[:], up_ps[0][:, 0:F], ALU.mult)
                            dve.drain()
                            gate_ps = up_ps[1][:, :] if NU == 2 else up_ps[0][:, F:2 * F]
                            dve.tensor_tensor(mid[:], sig[:], gate_ps, ALU.mult).then_inc(S["mid_ready"], 1)

                        def sum_up(n):
                            for c in range(TC):
                                for half in range(2):
                                    i = c * 2 + half
                                    dve.wait_ge(S["y_done"], n * 8 + (i + 1))
                                    cut = y[:, c, half * 512:(half + 1) * 512]
                                    dve.tensor_tensor(cut, cut, y_ps[half][:, :], ALU.add).then_inc(S["y_kept"], 1)

                        def body(m, n, first):
                            picks(m, n, first)
                            middle(n)
                            sum_up(n)

                        def next_pass():
                            dve.tensor_scalar(slots[:], slots[:], float(SLOTS), None, ALU.add)
                            dve.drain()

                        dve.tensor_scalar(slots[:], k.const("slot"), float(first_pass * SLOTS), None, ALU.add)
                        dve.drain()
                        if one_pass:
                            dve.memset(y[:], 0.0)
                            dve.drain()
                        loop(dve, body, next_pass)

        run(0, True)
        run(1, False)


def first_mix_end(k, ohT, onT, mergedT):
    merge_branches(k, ohT, onT, mergedT)
    with ExitStack() as ctx:
        gain = k.sb(ctx, "mix_gain", [P, D])
        broadcast_rows(k, "mix_gb", [(k.mod[:, 2 * KC:3 * KC], gain, 1.0)])
        project_out(k, "mix_out", k.i["w_out"], mergedT, gain, ALPHA)
    affine_norm(k, "ln1")


def affine_norm(k, tag):
    with ExitStack() as ctx:
        g = k.sb(ctx, f"{tag}_gr", [P, D])
        b = k.sb(ctx, f"{tag}_br", [P, D])
        broadcast_rows(k, f"{tag}_bc", [(k.col(f"{tag}_g", 0, 8), g, 0.0), (k.col(f"{tag}_b", 0, 8), b, 0.0)])
        normalize(k, tag, 1e-5, gain=g[:], shift=b[:], out=k.x)


def plus_one(k, out, a, times=None):
    with k.nc.Block() as block:
        @block.vector
        def _(dve):
            if times is None:
                dve.tensor_scalar(out, a, 1.0, None, ALU.add)
            else:
                dve.scalar_tensor_tensor(out=out, in0=a, scalar=1.0, in1=times, op0=ALU.add, op1=ALU.mult)


def add_experts(k, tag, y, gate, plus, residual):
    with ExitStack() as ctx:
        gain = k.sb(ctx, f"{tag}_gain", [P, D])
        broadcast_rows(k, f"{tag}_gb", [(gate, gain, plus)])
        with k.nc.Block() as block:
            @block.vector
            def _(dve):
                for c in range(TC):
                    dve.tensor_tensor(y[:, c, :], y[:, c, :], gain[:], ALU.mult)
                    dve.drain()
                    dve.scalar_tensor_tensor(out=k.x[:, c, :], in0=k.x[:, c, :], scalar=float(residual), in1=y[:, c, :],
                                             op0=ALU.mult, op1=ALU.add)


def expert_layer(k, tag, F, w_router, bias_row, up_parts, down, y):
    with ExitStack() as ctx:
        slot_of = k.sb(ctx, f"{tag}_slot_of", [P, TC, N_EXP])
        comb = k.sb(ctx, f"{tag}_comb", [P, TC, N_EXP])
        most = k.sb(ctx, f"{tag}_most", [P, 1], I32)
        route(k, f"{tag}_route", w_router, bias_row, slot_of, comb, most)
        experts(k, tag, F, up_parts, down, k.xn, k.scale1, k.mod[:, 3 * KC:4 * KC], slot_of, comb, most, y)


def first_experts(k):
    plus_one(k, k.scale1[:], k.mod[:, 4 * KC:5 * KC])
    normalize(k, "ln1h", 1e-5)
    transposed(k, "h2", k.scale1, k.mod[:, 3 * KC:4 * KC])
    with ExitStack() as ctx:
        y = k.sb(ctx, "moe1_out", [P, TC, D])
        expert_layer(k, "moe1", F1, k.i["w_router"], k.row("router_b"), [k.i["exp_up"], k.i["exp_gate"]], k.i["exp_down"], y)
        add_experts(k, "moe1_add", y, k.mod[:, 5 * KC:6 * KC], 1.0, ALPHA)
    affine_norm(k, "ln2")


def second_mix(k):
    nc = k.nc
    with ExitStack() as outer:
        catT = k.sb(outer, "mx2_catT", [P, KC, SEQ])
        with ExitStack() as ctx:
            qk = k.sb(ctx, "mx2_qk", [P, 2, HEADS, SEQ])
            v_tok = k.sb(ctx, "mx2_v", [P, TC, 512])
            u = k.sb(ctx, "mx2_u", [P, 4, SEQ])
            project_second(k, qk, v_tok, u)
            pooling(k, u, catT)
            forgetting(k, qk, v_tok, catT)
        gain = k.sb(outer, "mx2_gain", [P, D])
        broadcast_rows(k, "mx2_gb", [(k.mod[:, 2 * KC:3 * KC], gain, 0.0)])
        project_out(k, "mx2_out", k.i["w_out_2"], catT, gain, 1.0)


def project_second(k, qk, v_tok, u):
    nc = k.nc
    NV = 512 + HEADS
    with ExitStack() as ctx:
        w = [k.sb(ctx, f"p2_w{s}", [P, KC, P]) for s in range(2)]
        wv = k.sb(ctx, "p2_wv", [P, KC, NV])
        z = {n: k.sb(ctx, f"p2_{n}", [P, TC, HEADS]) for n in ("f", "low", "mag", "logf")}
        F = k.sb(ctx, "p2_F", [HEADS, SEQ])
        nF = k.sb(ctx, "p2_nF", [HEADS, SEQ])
        ps = k.banks(ctx, "p2_ps", 2)
        psv = k.banks(ctx, "p2_psv", 2)
        psf, = k.banks(ctx, "p2_psf", 1)
        psF, = k.banks(ctx, "p2_psF", 1)
        w_loaded = [k.sem(ctx, f"p2_w_loaded{s}") for s in range(2)]
        names = "wv_loaded projected kept v_projected v_kept f_projected mag_ready exp_ready ln_ready logf_ready summed F_ready cleared rows_set".split()
        S = {n: k.sem(ctx, "p2_" + n) for n in names}
        NCH = 12
        with nc.Block() as block:
            @block.sync
            def _(sp):
                for s in range(2):
                    sp.dma_start(w[s][:], k.i["w_qku_2"][s]).then_inc(w_loaded[s], 16)
                sp.dma_start(wv[:], k.i["w_vf_2"].rearrange("(k p) n -> p k n", p=P)).then_inc(S["wv_loaded"], 16)
                with sp.Fori(1, NCH // 2) as it:
                    for s in range(2):
                        sp.wait_ge(S["projected"], it * 2 + (s - 1))
                        sp.dma_start(w[s][:], k.i["w_qku_2"][it * 2 + s]).then_inc(w_loaded[s], 16)
                sp.wait_ge(S["F_ready"], 2)
                sp.wait_ge(S["kept"], NCH)
                for h in range(HEADS):
                    at = DH2 * (1 - h % 2)
                    ones = k.const("ones")[0:1, :].unsqueeze(1).broadcast_to([1, TC, P])
                    for side, row, other in ((0, F, 1), (1, nF, 0)):
                        sp.dma_start(qk[at + side:at + side + 1, side, h, :], row[h:h + 1, :]).then_inc(S["rows_set"], 16)
                        sp.dma_start(qk[at + other:at + other + 1, side, h, :], ones).then_inc(S["rows_set"], 16)
                sp.wait_ge(S["rows_set"], 16 * 4 * HEADS)

            @block.tensor
            def _(pe):
                def feature_major(it, s, first):
                    pe.wait_ge(w_loaded[s], it * 16 + 16)
                    if not first:
                        pe.wait_ge(S["kept"], it * 2 + (s - 1))
                    for kc in range(KC):
                        last = pe.matmul(ps[s][:, :], w[s][:, kc, :], k.hT[:, kc, :], start=(kc == 0), stop=(kc == KC - 1))
                    last.then_inc(S["projected"], 1)

                for s in range(2):
                    feature_major(0, s, True)
                pe.wait_ge(S["wv_loaded"], 16)
                for c in range(TC):
                    for kc in range(KC):
                        last = pe.matmul(psf[:, c * HEADS:(c + 1) * HEADS], k.hT[:, kc, c * P:(c + 1) * P], wv[:, kc, 512:NV],
                                         start=(kc == 0), stop=(kc == KC - 1))
                last.then_inc(S["f_projected"], 1)
                with pe.Fori(1, NCH // 2) as it:
                    for s in range(2):
                        feature_major(it, s, False)
                pe.wait_ge(S["logf_ready"], 1)
                for c in range(TC):
                    at = BT0 - c * P
                    last = pe.matmul(psF[0:HEADS, :], z["logf"][:, c, :], k.const("upto")[:, at:at + SEQ], start=(c == 0), stop=(c == TC - 1))
                last.then_inc(S["summed"], 1)
                for c in range(TC):
                    if c >= 2:
                        pe.wait_ge(S["v_kept"], c - 1)
                    for kc in range(KC):
                        last = pe.matmul(psv[c % 2][:, :], k.hT[:, kc, c * P:(c + 1) * P], wv[:, kc, 0:512],
                                         start=(kc == 0), stop=(kc == KC - 1))
                    last.then_inc(S["v_projected"], 1)

            @block.scalar
            def _(act):
                act.wait_ge(S["mag_ready"], 1)
                act.activation(z["mag"][:], z["mag"][:], ACT.Exp, scale=-1.0).then_inc(S["exp_ready"], 1)
                act.wait_ge(S["exp_ready"], 1)
                act.activation(z["mag"][:], z["mag"][:], ACT.Ln, bias=1.0).then_inc(S["ln_ready"], 1)
                for c in range(TC):
                    act.wait_ge(S["v_projected"], c + 1)
                    act.activation(v_tok[:, c, :], psv[c % 2][:, :], ACT.Copy).then_inc(S["v_kept"], 1)

            @block.vector
            def _(dve):
                for j in range(NCH):
                    dve.wait_ge(S["projected"], j + 1)
                    if j < 8:
                        side, scale = (0, DH2 ** -0.5) if j < 4 else (1, 1.0)
                        for half in range(2):
                            last = dve.tensor_scalar(qk[:, side, 2 * (j % 4) + half, :], ps[j % 2][:, :],
                                                     k.const("half")[:, half:half + 1], scale, ALU.mult, ALU.mult)
                    else:
                        last = dve.tensor_copy(u[:, j - 8, :], ps[j % 2][:, :])
                    last.then_inc(S["kept"], 1)
                    if j == 1:
                        dve.wait_ge(S["f_projected"], 1)
                        dve.tensor_tensor(z["f"][:], psf[:, 0:TC * HEADS].rearrange("p (c h) -> p c h", h=HEADS),
                                          k.row("b_fgate_2").unsqueeze(1).broadcast_to([P, TC, HEADS]), ALU.add)
                        dve.drain()
                        dve.tensor_scalar(z["low"][:], z["f"][:], -1.0, None, ALU.mult)
                        dve.drain()
                        dve.tensor_tensor(z["mag"][:], z["f"][:], z["low"][:], ALU.max).then_inc(S["mag_ready"], 1)
                        dve.drain()
                        dve.tensor_scalar(z["low"][:], z["f"][:], 0.0, None, ALU.min)
                        dve.drain()
                        dve.wait_ge(S["ln_ready"], 1)
                        dve.tensor_tensor(z["logf"][:], z["low"][:], z["mag"][:], ALU.subtract).then_inc(S["logf_ready"], 1)
                dve.wait_ge(S["summed"], 1)
                dve.tensor_copy(F[:], psF[0:HEADS, :]).then_inc(S["F_ready"], 1)
                dve.tensor_scalar(nF[:], psF[0:HEADS, :], -1.0, None, ALU.mult).then_inc(S["F_ready"], 1)


def pooling(k, u, catT):
    nc = k.nc
    G = len(POOL_WINDOWS)
    with ExitStack() as ctx:
        w = k.sb(ctx, "po_w", [P, G, P])
        sums = k.sb(ctx, "po_sums", [P, G, SEQ])
        diff = k.sb(ctx, "po_diff", [P, G, SEQ])
        ps = k.banks(ctx, "po_ps", G)
        loaded = k.sem(ctx, "po_loaded")
        diff_ready = k.sem(ctx, "po_diff_ready")
        mixed = k.sem(ctx, "po_mixed")
        with nc.Block() as block:
            @block.sync
            def _(sp):
                sp.dma_start(w[:], k.i["w_pool_2"].rearrange("g c d -> c g d")).then_inc(loaded, 16)

            @block.vector
            def _(dve):
                for g in range(G):
                    dve.tensor_tensor_scan(sums[:, g, :], k.const("ones", 0, 1).broadcast_to([P, SEQ]), u[:, g, :], 0.0, ALU.mult, ALU.add)
                dve.drain()
                for g, win in enumerate(POOL_WINDOWS):
                    dve.tensor_copy(diff[:, g, 0:win], sums[:, g, 0:win])
                    dve.tensor_tensor(diff[:, g, win:SEQ], sums[:, g, win:SEQ], sums[:, g, 0:SEQ - win], ALU.subtract)
                dve.drain()
                for g, win in enumerate(POOL_WINDOWS):
                    dve.tensor_tensor(diff[:, g, 0:16], diff[:, g, 0:16], k.const("pool_inv", 16 * g, 16 * g + 16), ALU.mult)
                    dve.tensor_scalar(diff[:, g, 16:SEQ], diff[:, g, 16:SEQ], 1.0 / win, None, ALU.mult)
                dve.drain()
                dve.tensor_tensor(diff[:], diff[:], u[:], ALU.subtract).then_inc(diff_ready, 1)
                for g in range(G):
                    dve.wait_ge(mixed, g + 1)
                    dve.tensor_scalar(catT[:, 4 + g, :], ps[g][:, :], k.col("pool_scale_2", g), None, ALU.mult)

            @block.tensor
            def _(pe):
                pe.wait_ge(loaded, 16)
                pe.wait_ge(diff_ready, 1)
                for g in range(G):
                    pe.matmul(ps[g][:, :], w[:, g, :], diff[:, g, :], start=True, stop=True).then_inc(mixed, 1)


def forgetting(k, qk, v_tok, catT):
    nc = k.nc
    NU = 2 * TC
    with ExitStack() as ctx:
        NP = 4
        qst = k.sb(ctx, "fa_q", [P, 2, SEQ])
        vst = k.sb(ctx, "fa_v", [P, TC, P])
        p = [k.sb(ctx, f"fa_p{s}", [P, SEQ]) for s in range(NP)]
        pT = [k.sb(ctx, f"fa_pT{s}", [P, SEQ]) for s in range(2)]
        top, ntop, total, factor = (k.sb(ctx, f"fa_{n}", [P, NU]) for n in ("top", "ntop", "total", "factor"))
        spare = k.sb(ctx, "fa_spare", [P, 2])
        sc = k.banks(ctx, "fa_sc", 3)
        tr = k.banks(ctx, "fa_tr", 2)
        o_ps, = k.banks(ctx, "fa_o", 1)
        names = "staged scored logits_ready exp_ready p_ready turned pT_ready mixed o_kept".split()
        S = {n: k.sem(ctx, "fa_" + n) for n in names}

        def pairs(eng, body):
            body(0, True)
            with eng.Fori(1, HEADS // 2) as m:
                body(m, False)

        with nc.Block() as block:
            @block.tensor
            def _(pe):
                def scores(m, u, first):
                    c, e = u // 2, u % 2
                    if u == 0:
                        pe.wait_ge(S["staged"], m * 2 + 2)
                    if u >= 3 or not first:
                        pe.wait_ge(S["logits_ready"], m * NU + (u - 2))
                    keys = qk[:, 1, :, :].rearrange("p (m e) s -> p m e s", e=2)[:, :, e, :]
                    pe.matmul(sc[u % 3][:, 0:(c + 1) * P], qst[:, e, c * P:(c + 1) * P], keys[:, m, 0:(c + 1) * P],
                              start=True, stop=True).then_inc(S["scored"], 1)

                def turn(m, u, first):
                    pe.wait_ge(S["p_ready"], m * NU + (u + 1))
                    if u >= 2 or not first:
                        pe.wait_ge(S["pT_ready"], m * NU + (u - 1))
                    for kk in range(u // 2 + 1):
                        last = pe.transpose(tr[u % 2][:, kk * P:(kk + 1) * P], p[u % NP][:, kk * P:(kk + 1) * P], k.const("ident"))
                    last.then_inc(S["turned"], 1)

                def mix(m, u, first):
                    c, e = u // 2, u % 2
                    pe.wait_ge(S["pT_ready"], m * NU + (u + 1))
                    if u == 0 and not first:
                        pe.wait_ge(S["o_kept"], m)
                    for kk in range(c + 1):
                        last = pe.matmul(o_ps[e * DH2:(e + 1) * DH2, c * P:(c + 1) * P], vst[:, kk, e * DH2:(e + 1) * DH2],
                                         pT[u % 2][:, kk * P:(kk + 1) * P], start=(u < 2 and kk == 0), stop=False, skip_group_check=True)
                    last.then_inc(S["mixed"], 1)

                def body(m, first):
                    for u in range(3):
                        scores(m, u, first)
                    for u in range(NU):
                        turn(m, u, first)
                        if u + 3 < NU:
                            scores(m, u + 3, first)
                        if u:
                            mix(m, u - 1, first)
                    mix(m, NU - 1, first)

                pairs(pe, body)

            @block.scalar
            def _(act):
                def weights(m, u):
                    n = (u // 2 + 1) * P
                    act.wait_ge(S["logits_ready"], m * NU + (u + 1))
                    act.activation(p[u % NP][:, 0:n], p[u % NP][:, 0:n], ACT.Exp, bias=ntop[:, u:u + 1],
                                   accum_out=total[:, u:u + 1]).then_inc(S["exp_ready"], 1)

                def keep_turned(m, u, first):
                    n = (u // 2 + 1) * P
                    act.wait_ge(S["turned"], m * NU + (u + 1))
                    if u >= 2 or not first:
                        act.wait_ge(S["mixed"], m * NU + (u - 1))
                    act.activation(pT[u % 2][:, 0:n], tr[u % 2][:, 0:n], ACT.Copy).then_inc(S["pT_ready"], 1)

                def body(m, first):
                    for u in range(NU + 2):
                        if u < NU:
                            weights(m, u)
                        if u >= 2:
                            keep_turned(m, u - 2, first)

                pairs(act, body)

            @block.vector
            def _(dve):
                def logits(m, u, first):
                    n = (u // 2 + 1) * P
                    dve.wait_ge(S["scored"], m * NU + (u + 1))
                    if u >= NP or not first:
                        dve.wait_ge(S["turned"], m * NU + (u - NP + 1 if u >= NP else 0))
                    dve.memset(spare[:, 0:1], 0.0)
                    dve.tensor_tensor_reduce(p[u % NP][:, 0:n], sc[u % 3][:, 0:n], k.const("causal2", SEQ - n, SEQ), 1.0, NEG * 10,
                                             ALU.add, ALU.max, top[:, u:u + 1])
                    dve.drain()
                    dve.tensor_scalar(ntop[:, u:u + 1], top[:, u:u + 1], -1.0, None, ALU.mult).then_inc(S["logits_ready"], 1)

                def normalized(m, u):
                    n = (u // 2 + 1) * P
                    dve.wait_ge(S["exp_ready"], m * NU + (u + 1))
                    dve.reciprocal(factor[:, u:u + 1], total[:, u:u + 1])
                    dve.drain()
                    dve.tensor_scalar(p[u % NP][:, 0:n], p[u % NP][:, 0:n], factor[:, u:u + 1], None, ALU.mult).then_inc(S["p_ready"], 1)

                def body(m, first):
                    for u in range(NU + 1):
                        if u < NU:
                            logits(m, u, first)
                        if u:
                            normalized(m, u - 1)
                    dve.wait_ge(S["mixed"], m * NU + NU)
                    dve.tensor_copy(catT[:, m, :], o_ps[:, :]).then_inc(S["o_kept"], 1)

                pairs(dve, body)

            @block.gpsimd
            def _(pool):
                def stage(m, first):
                    if not first:
                        pool.wait_ge(S["mixed"], m * NU)
                        pool.tensor_tensor(spare[:, 1:2], k.const("ones", 0, 1), k.const("ones", 0, 1), ALU.add)
                    queries = qk[:, 0, :, :].rearrange("p (m e) s -> p m e s", e=2)
                    pool.tensor_copy(qst[:], queries[:, m, :, :]).then_inc(S["staged"], 1)
                    pool.tensor_copy(vst[:], v_tok[:].rearrange("p c (m e) -> p c m e", e=P)[:, :, m, :]).then_inc(S["staged"], 1)

                pairs(pool, stage)


def second_modulated(k, tag, gain, scale, shift):
    plus_one(k, k.scale1[:], scale, times=gain)
    normalize(k, tag, 1e-6, root_mean_square=True)
    transposed(k, f"{tag}T", k.scale1, shift)


def program(nc, inputs, out):
    with ExitStack() as ctx:
        k = Kit(nc, inputs, out)
        persistent(k, ctx)
        load_constants(k)

        modulation(k, "mod1", inputs["ada_w"], k.col("c", 0, 8), k.col("ada_b", 0, 48), k.mod)
        plus_one(k, k.scale1[:], k.mod[:, KC:2 * KC])
        normalize(k, "ln0", 1e-5)
        transposed(k, "h1", k.scale1, k.mod[:, 0:KC])
        with ExitStack() as mix:
            ohT = k.sb(mix, "ohT", [P, KC, SEQ])
            recurrence(k, ohT)
            onT = k.sb(mix, "onT", [P, KC, SEQ])
            sparse_attention(k, onT)
            mergedT = k.sb(mix, "mergedT", [P, KC, SEQ])
            first_mix_end(k, ohT, onT, mergedT)
        first_experts(k)

        modulation(k, "mod2", inputs["ada_w_2"], k.col("c_2", 0, 8), k.col("b_ada_2", 0, 48), k.mod)
        second_modulated(k, "rms0", k.col("norm_mix_g_2", 0, 8), k.mod[:, KC:2 * KC], k.mod[:, 0:KC])
        second_mix(k)
        second_modulated(k, "rms1", k.col("norm_ffn_g_2", 0, 8), k.mod[:, 4 * KC:5 * KC], k.mod[:, 3 * KC:4 * KC])
        with ExitStack() as ffn:
            y = k.sb(ffn, "moe2_out", [P, TC, D])
            expert_layer(k, "moe2", F2, inputs["w_router_2"], k.row("router_b_2"), [inputs["exp_in_2"]], inputs["exp_down_2"], y)
            add_experts(k, "moe2_add", y, k.mod[:, 5 * KC:6 * KC], 0.0, 1.0)
        with ExitStack() as fin:
            g = k.sb(fin, "final_g", [P, D])
            broadcast_rows(k, "final_gb", [(k.col("norm_final_g_2", 0, 8), g, 0.0)])
            normalize(k, "final", 1e-6, root_mean_square=True, gain=g[:], out=k.x)
        with ExitStack() as end:
            stored = k.sem(end, "out_stored")
            with nc.Block() as block:
                @block.sync
                def _(sp):
                    sp.dma_start(out.rearrange("(c p) d -> p c d", p=P), k.x[:]).then_inc(stored, 16)
                    sp.wait_ge(stored, 16)


def _columns(v):
    return np.asarray(v, np.float32).reshape(-1, P).T


def arrange(x, c, ada_w, ada_b, w_in, b_in, hg_lb_logits, hg_norm_w, cmp_pos_k, cmp_w1_k, cmp_b1_k, cmp_w2_k,
            cmp_pos_v, cmp_w1_v, cmp_b1_v, cmp_w2_v, rel_bias, w_br_hg, w_br_nsa, w_out, ln1_g, ln1_b,
            router_grp_w, router_grp_b, router_exp_w, router_exp_b, exp_w1, exp_w3, exp_w2, ln2_g, ln2_b,
            c_2, norm_mix_g_2, norm_ffn_g_2, norm_final_g_2, w_ada_2, b_ada_2, w_in_2, b_fgate_2, w_pool_2,
            pool_scale_2, w_out_2, w_router_group_2, b_router_group_2, w_router_expert_2, b_router_expert_2,
            w_expert_gate_2, w_expert_up_2, w_expert_down_2):
    f = lambda a: np.ascontiguousarray(np.asarray(a))
    w_in, b_in = f(w_in)[0], f(b_in)[0]
    at = dict(hq=0, hf=1024, hv=2048, hg=3072, nq=4096, kc=5120, vc=5376, ks=5632, vs=5888, kw=6144, vw=6400,
              gate=6656, mgh=6680, mgn=7704)

    def chunks(w, a, n):
        return w[:, a:a + n * P].reshape(KC, P, n, P).transpose(2, 1, 0, 3)

    vectors = dict(
        c=c, ada_b=ada_b, b_in=b_in[:at["gate"]], b_mg=b_in[at["mgh"]:], lb0=f(hg_lb_logits)[0],
        lb1=f(hg_lb_logits)[1], hg_norm_w=hg_norm_w, cmp_b1_k=cmp_b1_k, cmp_b1_v=cmp_b1_v, cmp_pos_k=cmp_pos_k,
        cmp_pos_v=cmp_pos_v, ln1_g=ln1_g, ln1_b=ln1_b, ln2_g=ln2_g, ln2_b=ln2_b, c_2=c_2, b_ada_2=b_ada_2,
        norm_mix_g_2=norm_mix_g_2, norm_ffn_g_2=norm_ffn_g_2, norm_final_g_2=norm_final_g_2,
        pool_scale_2=pool_scale_2)
    short = dict(b_gate=[b_in[at["gate"]:at["mgh"]]], router_b=[router_grp_b, router_exp_b],
                 router_b_2=[b_router_group_2, b_router_expert_2], b_fgate_2=[b_fgate_2])
    w2 = f(w_in_2)[0]
    out = dict(
        consts=np.concatenate([a for _, a in pack_consts()], 1),
        cols=np.concatenate([_columns(vectors[n]) for n, _ in pack_columns()], 1),
        rows=np.concatenate([f(v).reshape(-1) for n, _ in pack_rows() for v in short[n]]),
        buckets=bucket_rows(),
        x=f(x)[0], ada_w=f(ada_w)[0],
        w_hg=np.stack([chunks(w_in, at[n], 8) for n in ("hq", "hf", "hg", "hv")], 1),
        w_nq=chunks(w_in, at["nq"], 8),
        w_kv=np.concatenate([chunks(w_in, at[n], 2) for n in ("kc", "vc", "ks", "kw")]),
        w_v=np.concatenate([w_in[:, at["vs"]:at["vs"] + 256], w_in[:, at["vw"]:at["vw"] + 256],
                            w_in[:, at["gate"]:at["mgh"]]], 1),
        w_cmp=np.stack([f(cmp_w1_k)[0], f(cmp_w1_v)[0]]), w_cmp2=np.stack([f(cmp_w2_k)[0], f(cmp_w2_v)[0]]),
        rel_bias=f(rel_bias).T,
        w_merge=np.stack([chunks(w_in, at["mgh"], 8), chunks(w_in, at["mgn"], 8), chunks(f(w_br_hg)[0], 0, 8),
                          chunks(f(w_br_nsa)[0], 0, 8)], 1),
        w_out=f(w_out)[0],
        w_router=np.concatenate([f(router_grp_w)[0], f(router_exp_w)[0]], 1),
        exp_up=f(exp_w1)[0], exp_gate=f(exp_w3)[0], exp_down=f(exp_w2)[0],
        ada_w_2=f(w_ada_2)[0],
        w_qku_2=np.concatenate([chunks(w2, 0, 8), chunks(w2, 1544, 4)]),
        w_vf_2=w2[:, 1024:1544],
        w_pool_2=f(w_pool_2)[0], w_out_2=f(w_out_2)[0],
        w_router_2=np.concatenate([f(w_router_group_2)[0], f(w_router_expert_2)[0].transpose(1, 0, 2).reshape(D, N_EXP)], 1),
        exp_in_2=np.concatenate([f(w_expert_gate_2)[0].reshape(N_EXP, D, F2), f(w_expert_up_2)[0].reshape(N_EXP, D, F2)], 2),
        exp_down_2=f(w_expert_down_2)[0].reshape(N_EXP, F2, D),
    )
    return {n: np.ascontiguousarray(a) for n, a in out.items()}


def kernel(**inputs):
    from concourse import bacc
    from concourse.bass_utils import run_bass_kernel_spmd

    arrays = {f"in_{n}": a for n, a in arrange(**inputs).items()}
    nc = bacc.Bacc("TRN2", target_bir_lowering=False, num_devices=1)
    views = {n[3:]: nc.dram_tensor(n, a.shape, mybir.dt.from_np(a.dtype), kind="ExternalInput").ap() for n, a in arrays.items()}
    out = nc.dram_tensor("out_x", (SEQ, D), F32, kind="ExternalOutput").ap()
    program(nc, views, out)
    r = run_bass_kernel_spmd(nc, [arrays], core_ids=[0])
    return r.results[0]["out_x"].reshape(1, SEQ, D)
```

```python
from contextlib import ExitStack

import concourse.bass as bass
import numpy as np
from concourse import mybir

F32 = mybir.dt.float32
I32 = mybir.dt.int32
U32 = mybir.dt.uint32
ALU = mybir.AluOpType
ACT = mybir.ActivationFunctionType
AX = mybir.AxisListType

P = 128
SEQ = 512
D = 1024
TC = SEQ // P
KC = D // P
HEADS = 8

HG_CHUNK = 32
N_CHUNK = SEQ // HG_CHUNK
QC = P // HG_CHUNK
GROUPS = 2
REP = HEADS // GROUPS
CMP_BLOCK = 32
CMP_STRIDE = 16
N_CMP = SEQ // CMP_STRIDE - 1
BUCKETS = 32
MAX_DIST = 128
ALPHA = 2 ** 0.25
ATT_SCALE = P ** -0.5
NEG = -1e30

N_GRP = 4
PER_GRP = 8
N_EXP = N_GRP * PER_GRP
SLOTS = 64
PASSES = SEQ // SLOTS
PAIRS = N_EXP // 2
F1 = 512
F2 = 256

DH2 = 64
POOL_WINDOWS = (2, 4, 8, 16)

BT0 = SEQ - P
BTW = BT0 + SEQ
BT_ROW = 1024


def pack_columns():
    return [("c", 8), ("ada_b", 48), ("b_in", 52), ("b_mg", 16), ("lb0", 8), ("lb1", 8), ("hg_norm_w", 8),
            ("cmp_b1_k", 1), ("cmp_b1_v", 1), ("cmp_pos_k", 32), ("cmp_pos_v", 32),
            ("ln1_g", 8), ("ln1_b", 8), ("ln2_g", 8), ("ln2_b", 8),
            ("c_2", 8), ("b_ada_2", 48), ("norm_mix_g_2", 8), ("norm_ffn_g_2", 8), ("norm_final_g_2", 8),
            ("pool_scale_2", 4)]


def pack_rows():
    return [("b_gate", 24), ("router_b", 36), ("router_b_2", 36), ("b_fgate_2", 8)]


def pack_consts():
    p = np.arange(P)[:, None]
    j = np.arange(P)[None, :]
    w = np.arange(BTW)[None, :]
    ident = (p == j)
    before = (p < j)
    ones = np.ones((P, P))
    hg_causal = (p // HG_CHUNK == j // HG_CHUNK) & (p <= j)
    chunk_of = (p // HG_CHUNK == np.arange(QC)[None, :])
    every32 = (p % 32 == 0)
    half = (p // DH2 == np.arange(2)[None, :])
    chunk_cont = np.broadcast_to((np.arange(SEQ) % HG_CHUNK != 0)[None, :], (P, SEQ))
    upto = (p <= w - BT0)
    causal2 = np.where(w[:, :SEQ] - BT0 > p, NEG, 0.0)
    inv = np.array([[1.0 / min(t + 1, k) for t in range(16)] for k in POOL_WINDOWS]).reshape(1, -1)
    pool_inv = np.broadcast_to(inv, (P, inv.size))
    first = np.broadcast_to(np.arange(N_EXP, 0, -1)[None, :], (P, N_EXP))
    t = (np.arange(TC)[None, :, None] * P + p[:, :, None])
    cmp_ok = (t - (np.arange(N_CMP) * CMP_STRIDE + CMP_BLOCK - 1)[None, None, :] >= 0).reshape(P, -1)
    return [(n, np.asarray(a, np.float32)) for n, a in (
        ("ident", ident), ("before", before), ("ones", ones), ("hg_causal", hg_causal), ("chunk_of", chunk_of),
        ("half", half), ("chunk_cont", chunk_cont), ("upto", upto), ("causal2", causal2),
        ("pool_inv", pool_inv), ("first", first), ("cmp_ok", cmp_ok), ("every32", every32),
        ("expert_row", np.broadcast_to(np.arange(N_EXP)[None, :] * SLOTS, (P, N_EXP))),
        ("pass_start", np.broadcast_to(np.arange(1, PASSES)[None, :] * SLOTS, (P, PASSES - 1))))]


def bucket_rows():
    import math
    dist = SEQ - 1 - np.arange(BT_ROW)
    n = np.maximum(dist, 0)
    half = BUCKETS // 2
    nf = np.maximum(n, 1).astype(np.float32)
    large = half + (np.log(nf / np.float32(half)) / np.float32(math.log(MAX_DIST / half)) * np.float32(BUCKETS - half)).astype(np.int32)
    b = np.where(n < half, n, np.minimum(large, BUCKETS - 1))
    out = np.zeros((BUCKETS + 1, BT_ROW), np.float32)
    out[b, np.arange(BT_ROW)] = dist >= 0
    out[BUCKETS] = dist < 0
    return out


def offsets(spec):
    at, out = 0, {}
    for name, n in spec:
        out[name] = (at, n)
        at += n
    return out, at


class Kit:

    def __init__(self, nc, inputs, out):
        self.nc, self.i, self.out = nc, inputs, out
        self.owned, self.zeroed = [], []
        self.col_at, self.n_cols = offsets(pack_columns())
        self.row_at, self.n_rows = offsets(pack_rows())
        self.const_at, self.n_consts = offsets([(n, a.shape[1]) for n, a in pack_consts()])

    def sb(self, ctx, name, shape, dt=F32):
        return ctx.enter_context(self.nc.sbuf_tensor(name, shape, dt))

    def banks(self, ctx, name, n):
        return [ctx.enter_context(self.nc.psum_tensor(f"{name}{j}", [P, 512], F32)) for j in range(n)]

    def sem(self, ctx, name):
        if not any(owner is ctx for owner, _ in self.owned):
            self.owned.append((ctx, []))
            ctx.callback(self.stage_over, ctx)
        handle = self.nc.alloc_semaphore(name=name)
        next(sems for owner, sems in self.owned if owner is ctx).append(handle)
        return handle

    def stage_over(self, ctx):
        mine = next(pair for pair in self.owned if pair[0] is ctx)
        self.owned.remove(mine)
        for s in self.zeroed:
            self.nc.release_semaphore(s)
        numbers = sorted(s.num for s in mine[1])
        start = numbers[0]
        for a, b in zip(numbers, numbers[1:] + [None]):
            if b != a + 1:
                self.nc.gpsimd.sem_clear(range(start, a + 1))
                start = b
        self.zeroed = mine[1]

    def col(self, name, j=0, n=1):
        a = self.col_at[name][0] + j
        return self.cols[:, a:a + n]

    def row(self, name):
        a, n = self.row_at[name]
        return self.rows[:, a:a + n]

    def const(self, name, a=0, b=None):
        at, n = self.const_at[name]
        return self.consts[:, at + a:at + (n if b is None else b)]


def load_constants(k):
    nc = k.nc
    with ExitStack() as ctx:
        loaded = k.sem(ctx, "const_loaded")
        with nc.Block() as block:
            @block.sync
            def _(sp):
                sp.dma_start(k.consts[:], k.i["consts"]).then_inc(loaded, 16)
                sp.dma_start(k.cols[:], k.i["cols"]).then_inc(loaded, 16)
                sp.dma_start(k.rows[:], k.i["rows"].partition_broadcast(P)).then_inc(loaded, 16)
                sp.dma_start(k.x[:], k.i["x"].rearrange("(c p) d -> p c d", p=P)).then_inc(loaded, 16)
                sp.wait_ge(loaded, 64)


def modulation(k, tag, weights, act, bias, mod):
    nc = k.nc
    NBUF, BLK, QUARTER = 4, 512, 32
    blocks = 6 * D // BLK
    rounds = blocks // NBUF
    per = BLK // P
    w_v = weights.rearrange("(k p) n -> p k n", p=P)
    with ExitStack() as ctx:
        buf = [k.sb(ctx, f"{tag}_w{r}", [P, KC, BLK]) for r in range(NBUF)]
        rows = [k.sb(ctx, f"{tag}_rows{r}", [P, BLK]) for r in range(2)]
        sig = k.sb(ctx, f"{tag}_sig", [P, KC])
        c_act = k.sb(ctx, f"{tag}_cact", [P, KC])
        c_wide = k.sb(ctx, f"{tag}_cwide", [P, KC, QUARTER])
        ps = k.banks(ctx, f"{tag}_ps", 2)
        mod_ps, = k.banks(ctx, f"{tag}_mod_ps", 1)
        w_loaded = [k.sem(ctx, f"{tag}_w_loaded{r}") for r in range(NBUF)]
        w_used = k.sem(ctx, f"{tag}_w_used")
        sig_ready = k.sem(ctx, f"{tag}_sig_ready")
        act_ready = k.sem(ctx, f"{tag}_act_ready")
        rows_kept = k.sem(ctx, f"{tag}_rows_kept")
        folded = k.sem(ctx, f"{tag}_folded")

        def in_rounds(eng, body):
            for r in range(NBUF):
                body(r, r, True)
            with eng.Fori(1, rounds) as it:
                for r in range(NBUF):
                    body(it * NBUF + r, r, False)

        with nc.Block() as block:
            @block.sync
            def _(sp):
                def load(b, r, first):
                    if not first:
                        sp.wait_ge(w_used, b - (NBUF - 1))
                        sp.dma_start(buf[r][:], w_v[:, :, bass.ts(b, BLK)]).then_inc(w_loaded[r], 16)
                    else:
                        sp.dma_start(buf[r][:], w_v[:, :, b * BLK:(b + 1) * BLK]).then_inc(w_loaded[r], 16)

                in_rounds(sp, load)

            @block.tensor
            def _(pe):
                def fold(b, r):
                    pe.wait_ge(rows_kept, b + 1)
                    for j in range(per):
                        last = pe.matmul(mod_ps[:, bass.ds(b * per + j, 1)], rows[r % 2][:, j * P:(j + 1) * P],
                                         k.const("every32"), start=True, stop=True, skip_group_check=True)
                    last.then_inc(folded, 1)

                def multiply(it, r, first):
                    b = it * NBUF + r
                    pe.wait_ge(w_loaded[r], it * 16 + 16)
                    if r >= 2 or not first:
                        pe.wait_ge(rows_kept, b - 1)
                    for kc in range(KC):
                        q = kc % 4 * QUARTER
                        last = pe.matmul(ps[r % 2][q:q + QUARTER, :], c_wide[:, kc, :], buf[r][:, kc, :],
                                         start=(kc < 4), stop=(kc >= 4), skip_group_check=True)
                    last.then_inc(w_used, 1)
                    if r or not first:
                        fold(b - 1, r - 1)

                pe.wait_ge(act_ready, 2)
                for r in range(NBUF):
                    multiply(0, r, True)
                with pe.Fori(1, rounds) as it:
                    for r in range(NBUF):
                        multiply(it, r, False)
                fold(blocks - 1, NBUF - 1)

            @block.scalar
            def _(act_e):
                act_e.activation(sig[:], act, ACT.Sigmoid).then_inc(sig_ready, 1)

                def keep(b, r, first):
                    act_e.wait_ge(w_used, b + 1)
                    if r >= 2 or not first:
                        act_e.wait_ge(folded, b - 1)
                    act_e.activation(rows[r % 2][:], ps[r % 2][:, :], ACT.Copy).then_inc(rows_kept, 1)

                in_rounds(act_e, keep)

            @block.vector
            def _(dve):
                dve.wait_ge(sig_ready, 1)
                dve.tensor_tensor(c_act[:], act, sig[:], ALU.mult).then_inc(act_ready, 1)
                dve.drain()
                dve.tensor_copy(c_wide[:], c_act[:].unsqueeze(2).broadcast_to([P, KC, QUARTER])).then_inc(act_ready, 1)
                dve.wait_ge(folded, blocks)
                dve.tensor_tensor(mod[:], mod_ps[:, 0:blocks * per], bias, ALU.add)


def normalize(k, tag, eps, root_mean_square=False, gain=None, shift=None, out=None):
    nc = k.nc
    out = k.xn if out is None else out
    with ExitStack() as ctx:
        stats = k.sb(ctx, f"{tag}_stats", [P, TC, 2, 6])
        mv = k.sb(ctx, f"{tag}_mv", [P, TC, 2])
        var = k.sb(ctx, f"{tag}_var", [P, TC])
        dev = k.sb(ctx, f"{tag}_dev", [P, TC])
        rstd = k.sb(ctx, f"{tag}_rstd", [P, TC])
        var_ready = k.sem(ctx, f"{tag}_var_ready")
        dev_ready = k.sem(ctx, f"{tag}_dev_ready")
        scaled = k.sem(ctx, f"{tag}_scaled")
        gained = k.sem(ctx, f"{tag}_gained")
        with nc.Block() as block:
            @block.vector
            def _(dve):
                for c in range(TC):
                    for h in range(2):
                        dve.bn_stats(stats[:, c, h, :], k.x[:, c, h * 512:(h + 1) * 512])
                dve.drain()
                for c in range(TC):
                    dve.bn_aggr(mv[:, c, :], stats[:, c, :, :])
                dve.drain()
                if root_mean_square:
                    dve.tensor_tensor(var[:], mv[:, :, 0], mv[:, :, 0], ALU.mult)
                    dve.drain()
                    dve.tensor_tensor(var[:], var[:], mv[:, :, 1], ALU.add)
                    dve.drain()
                    dve.tensor_scalar(var[:], var[:], eps, None, ALU.add).then_inc(var_ready, 1)
                else:
                    dve.tensor_scalar(var[:], mv[:, :, 1], eps, None, ALU.add).then_inc(var_ready, 1)
                dve.wait_ge(dev_ready, 1)
                dve.reciprocal(rstd[:], dev[:])
                dve.drain()
                for c in range(TC):
                    if root_mean_square:
                        dve.tensor_scalar(out[:, c, :], k.x[:, c, :], rstd[:, c:c + 1], None, ALU.mult).then_inc(scaled, 1)
                    else:
                        dve.tensor_scalar(out[:, c, :], k.x[:, c, :], mv[:, c, 0:1], rstd[:, c:c + 1],
                                          ALU.subtract, ALU.mult).then_inc(scaled, 1)
                if gain is not None:
                    for c in (0, 1):
                        dve.wait_ge(scaled, c + 1)
                        dve.tensor_tensor(out[:, c, :], out[:, c, :], gain, ALU.mult)
                    dve.drain()
                    if shift is not None:
                        for c in (0, 1):
                            dve.tensor_tensor(out[:, c, :], out[:, c, :], shift, ALU.add)

            @block.scalar
            def _(act):
                act.wait_ge(var_ready, 1)
                act.activation(dev[:], var[:], ACT.Sqrt).then_inc(dev_ready, 1)

            @block.gpsimd
            def _(pool):
                if gain is not None:
                    for c in (2, 3):
                        pool.wait_ge(scaled, c + 1)
                        pool.tensor_tensor(out[:, c, :], out[:, c, :], gain, ALU.mult).then_inc(gained, 1)
                    if shift is not None:
                        for c in (2, 3):
                            pool.wait_ge(gained, c - 1)
                            pool.tensor_tensor(out[:, c, :], out[:, c, :], shift, ALU.add)


def transposed(k, tag, scale, shift):
    nc = k.nc
    with ExitStack() as ctx:
        ps = k.banks(ctx, f"{tag}_ps", 2)
        turned = k.sem(ctx, f"{tag}_turned")
        kept = k.sem(ctx, f"{tag}_kept")
        with nc.Block() as block:
            @block.tensor
            def _(pe):
                for kc in range(KC):
                    if kc >= 2:
                        pe.wait_ge(kept, kc - 1)
                    for c in range(TC):
                        last = pe.transpose(ps[kc % 2][:, c * P:(c + 1) * P], k.xn[:, c, kc * P:(kc + 1) * P],
                                            k.const("ident"))
                    last.then_inc(turned, 1)

            @block.scalar
            def _(act):
                for kc in range(KC):
                    act.wait_ge(turned, kc + 1)
                    act.activation(k.hT[:, kc, :], ps[kc % 2][:, :], ACT.Identity, scale=scale[:, kc:kc + 1],
                                   bias=shift[:, kc:kc + 1]).then_inc(kept, 1)


def broadcast_rows(k, tag, jobs):
    nc = k.nc
    with ExitStack() as ctx:
        ps = k.banks(ctx, f"{tag}_ps", 2)
        turned = k.sem(ctx, f"{tag}_turned")
        kept = k.sem(ctx, f"{tag}_kept")
        steps = [(cols, out, plus, j) for cols, out, plus in jobs for j in range(0, cols.shape[1], 4)]
        with nc.Block() as block:
            @block.tensor
            def _(pe):
                for n, (cols, out, plus, j) in enumerate(steps):
                    if n >= 2:
                        pe.wait_ge(kept, n - 1)
                    for q in range(min(4, cols.shape[1] - j)):
                        last = pe.transpose(ps[n % 2][:, q * P:(q + 1) * P],
                                            cols[:, j + q:j + q + 1].broadcast_to([P, P]), k.const("ident"))
                    last.then_inc(turned, 1)

            @block.vector
            def _(dve):
                for n, (cols, out, plus, j) in enumerate(steps):
                    dve.wait_ge(turned, n + 1)
                    width = min(4, cols.shape[1] - j) * P
                    dve.tensor_scalar(out[:, j * P:j * P + width], ps[n % 2][:, 0:width], float(plus), None,
                                      ALU.add).then_inc(kept, 1)


def persistent(k, ctx):
    k.consts = k.sb(ctx, "consts", [P, k.n_consts])
    k.cols = k.sb(ctx, "cols", [P, k.n_cols])
    k.rows = k.sb(ctx, "rows", [P, k.n_rows])
    k.x = k.sb(ctx, "x", [P, TC, D])
    k.xn = k.sb(ctx, "xn", [P, TC, D])
    k.hT = k.sb(ctx, "hT", [P, KC, SEQ])
    k.mod = k.sb(ctx, "mod", [P, 6 * KC])
    names = ["zeroed", "moe1_zeroed", "moe2_zeroed", "sent"] + [f"fetched{c}{s}" for c in range(TC) for s in range(2)]
    k.dma_sems = {n: k.sem(ctx, f"all_{n}") for n in names}
    k.sent = k.nc.dram_tensor("sent", (PASSES, N_EXP, SLOTS, D), F32, kind="Internal").ap()
    k.results = k.nc.dram_tensor("results", (PASSES, N_EXP, SLOTS, D), F32, kind="Internal").ap()
    k.scale1 = k.sb(ctx, "scale1", [P, KC])


def recurrence(k, ohT):
    nc = k.nc
    w_hg = k.i["w_hg"]
    raw = k.xn[:].rearrange("p c (h e) -> p c h e", e=P)
    with ExitStack() as ctx:
        w = [k.sb(ctx, f"hg_w{s}", [P, KC, P]) for s in range(4)]
        q = k.sb(ctx, "hg_q", [P, SEQ])
        sigf = k.sb(ctx, "hg_sigf", [P, SEQ])
        fg = k.sb(ctx, "hg_fg", [P, SEQ])
        key = k.sb(ctx, "hg_key", [P, SEQ])
        logf = k.sb(ctx, "hg_logf", [P, SEQ])
        b = k.sb(ctx, "hg_b", [P, SEQ])
        left = k.sb(ctx, "hg_left", [P, SEQ])
        eb = k.sb(ctx, "hg_eb", [P, SEQ])
        enb = k.sb(ctx, "hg_enb", [P, SEQ])
        eleft = k.sb(ctx, "hg_eleft", [P, SEQ])
        q_in = k.sb(ctx, "hg_q_in", [P, SEQ])
        k_in = k.sb(ctx, "hg_k_in", [P, SEQ])
        k_end = k.sb(ctx, "hg_k_end", [P, SEQ])
        k_tok = k.sb(ctx, "hg_k_tok", [P, TC, P])
        v_tok = k.sb(ctx, "hg_v_tok", [P, TC, P])
        v_parts = k.sb(ctx, "hg_v_parts", [P, TC, QC, P])
        att = k.sb(ctx, "hg_att", [P, TC, P])
        state = k.sb(ctx, "hg_state", [P, N_CHUNK, P])
        gate = k.sb(ctx, "hg_gate", [P, HEADS, SEQ])
        junk = k.sb(ctx, "hg_junk", [P, TC, P])
        squares = k.sb(ctx, "hg_squares", [P, HEADS, TC])
        rstd = k.sb(ctx, "hg_rstd", [P, HEADS, TC])
        lb = k.sb(ctx, "hg_lb", [P, HEADS])
        one_lb = k.sb(ctx, "hg_one_lb", [P, HEADS])
        v_bias = k.sb(ctx, "hg_v_bias", [P, D])
        lower_bound_layer(k, lb)
        broadcast_rows(k, "hg_vb", [(k.col("b_in", 16, 8), v_bias[:, :], 0.0)])

        proj = k.banks(ctx, "hg_proj", 2)
        upd = k.banks(ctx, "hg_upd", 4)
        tr_out, = k.banks(ctx, "hg_tr_out", 1)
        score, = k.banks(ctx, "hg_score", 1)

        names = ("loaded_q loaded_f loaded_g loaded_v used_q used_f used_g used_v "
                 "q_kept f_kept g_kept v_kept fg_ready key_ready logf_ready b_ready left_ready eb_ready enb_ready eleft_ready "
                 "qin_ready kin_ready kend_ready keys_turned ktok_kept scores_done att_ready "
                 "v_parts_ready updates_done chain_done outputs_done raw_kept").split()
        S = {n: k.sem(ctx, "hg_" + n) for n in names}
        slices = "qfgv"

        with nc.Block() as block:
            @block.sync
            def _(sp):
                for s, a in enumerate(slices):
                    sp.dma_start(w[s][:], w_hg[0, s]).then_inc(S["loaded_" + a], 16)
                with sp.Fori(1, HEADS) as n:
                    for s, a in enumerate(slices):
                        sp.wait_ge(S["used_" + a], n)
                        sp.dma_start(w[s][:], w_hg[n, s]).then_inc(S["loaded_" + a], 16)

            @block.tensor
            def _(pe):
                def feature_major(s, a, bank, n):
                    pe.wait_ge(S["loaded_" + a], n * 16 + 16)
                    for kc in range(KC):
                        last = pe.matmul(proj[bank][:, :], w[s][:, kc, :], k.hT[:, kc, :],
                                         start=(kc == 0), stop=(kc == KC - 1))
                    last.then_inc(S["used_" + a], 1)

                def project_qf(n, first):
                    if not first:
                        pe.wait_ge(S["g_kept"], n)
                    feature_major(0, "q", 0, n)
                    if not first:
                        pe.wait_ge(S["v_kept"], n)
                    feature_major(1, "f", 1, n)

                def project_gv(n):
                    pe.wait_ge(S["q_kept"], n + 1)
                    feature_major(2, "g", 0, n)
                    pe.wait_ge(S["f_kept"], n + 1)
                    pe.wait_ge(S["loaded_v"], n * 16 + 16)
                    for c in range(TC):
                        for kc in range(KC):
                            last = pe.matmul(proj[1][:, c * P:(c + 1) * P], k.hT[:, kc, c * P:(c + 1) * P],
                                             w[3][:, kc, :], start=(kc == 0), stop=(kc == KC - 1))
                    last.then_inc(S["used_v"], 1)

                def scores_and_updates(n, first):
                    pe.wait_ge(S["kend_ready"], n + 1)
                    if not first:
                        pe.wait_ge(S["raw_kept"], n)
                    for c in range(TC):
                        last = pe.transpose(tr_out[:, c * P:(c + 1) * P], k_end[:, c * P:(c + 1) * P], k.const("ident"))
                    last.then_inc(S["keys_turned"], 1)
                    pe.wait_ge(S["qin_ready"], n + 1)
                    pe.wait_ge(S["kin_ready"], n + 1)
                    for c in range(TC):
                        last = pe.matmul(score[:, c * P:(c + 1) * P], k_in[:, c * P:(c + 1) * P],
                                         q_in[:, c * P:(c + 1) * P], start=True, stop=True)
                    last.then_inc(S["scores_done"], 1)
                    pe.wait_ge(S["ktok_kept"], n + 1)
                    pe.wait_ge(S["v_parts_ready"], n + 1)
                    if not first:
                        pe.wait_ge(S["chain_done"], n)
                    for c in range(TC):
                        last = pe.matmul(upd[c][:, :], k_tok[:, c, :], v_parts[:, c, :, :], start=True, stop=True)
                    last.then_inc(S["updates_done"], 1)

                def outputs(n):
                    pe.wait_ge(S["att_ready"], n + 1)
                    pe.wait_ge(S["chain_done"], n + 1)
                    for c in range(TC):
                        last = pe.matmul(tr_out[:, c * P:(c + 1) * P], att[:, c, :], v_tok[:, c, :],
                                         start=True, stop=False, skip_group_check=True)
                        for r in range(QC):
                            ch = c * QC + r
                            if ch:
                                last = pe.matmul(tr_out[r * HG_CHUNK:(r + 1) * HG_CHUNK, c * P:(c + 1) * P],
                                                 q_in[:, ch * HG_CHUNK:(ch + 1) * HG_CHUNK], state[:, ch, :],
                                                 start=False, stop=True, skip_group_check=True)
                    last.then_inc(S["outputs_done"], 1)

                project_qf(0, True)
                project_gv(0)
                project_qf(1, False)
                scores_and_updates(0, True)
                project_gv(1)
                outputs(0)
                with pe.Fori(1, HEADS - 1) as n:
                    project_qf(n + 1, False)
                    scores_and_updates(n, False)
                    project_gv(n + 1)
                    outputs(n)
                scores_and_updates(HEADS - 1, False)
                outputs(HEADS - 1)

            @block.scalar
            def _(act):
                def keep_qf(n, first):
                    act.wait_ge(S["used_q"], n + 1)
                    if not first:
                        act.wait_ge(S["qin_ready"], n)
                    act.activation(q[:], proj[0][:, :], ACT.Identity, bias=k.col("b_in", 0, 8)[:, bass.ds(n, 1)]).then_inc(S["q_kept"], 1)
                    act.wait_ge(S["used_f"], n + 1)
                    act.activation(sigf[:], proj[1][:, :], ACT.Sigmoid, bias=k.col("b_in", 8, 8)[:, bass.ds(n, 1)]).then_inc(S["f_kept"], 1)

                def keep_gate(n):
                    act.wait_ge(S["used_g"], n + 1)
                    act.activation(gate[:, n, :], proj[0][:, :], ACT.Sigmoid, bias=k.col("b_in", 24, 8)[:, bass.ds(n, 1)]).then_inc(S["g_kept"], 1)

                def keep_keys(n):
                    act.wait_ge(S["keys_turned"], n + 1)
                    act.activation(k_tok[:], tr_out[:, :], ACT.Copy).then_inc(S["ktok_kept"], 1)

                def log_decay(n):
                    act.wait_ge(S["fg_ready"], n + 1)
                    act.activation(logf[:], fg[:], ACT.Ln).then_inc(S["logf_ready"], 1)

                def decays(n, first):
                    act.wait_ge(S["b_ready"], n + 1)
                    if not first:
                        act.wait_ge(S["chain_done"], n)
                        act.wait_ge(S["qin_ready"], n)
                        act.wait_ge(S["kin_ready"], n)
                        act.wait_ge(S["kend_ready"], n)
                    act.activation(eb[:], b[:], ACT.Exp).then_inc(S["eb_ready"], 1)
                    act.activation(enb[:], b[:], ACT.Exp, scale=-1.0).then_inc(S["enb_ready"], 1)
                    act.wait_ge(S["left_ready"], n + 1)
                    act.activation(eleft[:], left[:], ACT.Exp).then_inc(S["eleft_ready"], 1)

                def keep_outputs(n):
                    act.wait_ge(S["outputs_done"], n + 1)
                    for c in range(TC):
                        act.activation(junk[:, c, :], tr_out[:, c * P:(c + 1) * P], ACT.Square, accum_out=squares[:, n, c:c + 1])
                    act.activation(raw[:, :, n, :], tr_out[:, :].rearrange("p (c e) -> p c e", e=P), ACT.Copy).then_inc(S["raw_kept"], 1)
                    act.drain()

                keep_qf(0, True)
                keep_gate(0)
                log_decay(0)
                decays(0, True)
                with act.Fori(0, HEADS - 1) as n:
                    keep_qf(n + 1, False)
                    keep_keys(n)
                    keep_gate(n + 1)
                    log_decay(n + 1)
                    decays(n + 1, False)
                    keep_outputs(n)
                keep_keys(HEADS - 1)
                keep_outputs(HEADS - 1)

            @block.vector
            def _(dve):
                def forget(n, first):
                    dve.wait_ge(S["f_kept"], n + 1)
                    if not first:
                        dve.wait_ge(S["logf_ready"], n)
                        dve.wait_ge(S["kend_ready"], n)
                    dve.tensor_scalar(fg[:], sigf[:], one_lb[:, bass.ds(n, 1)], lb[:, bass.ds(n, 1)],
                                      ALU.mult, ALU.add).then_inc(S["fg_ready"], 1)
                    dve.wait_ge(S["fg_ready"], n + 1)
                    dve.tensor_scalar(key[:], fg[:], -1.0, 1.0, ALU.mult, ALU.add).then_inc(S["key_ready"], 1)

                def running(n):
                    dve.wait_ge(S["logf_ready"], n + 1)
                    dve.tensor_tensor_scan(b[:], k.const("chunk_cont"), logf[:], 0.0, ALU.mult, ALU.add).then_inc(S["b_ready"], 1)
                    dve.wait_ge(S["b_ready"], n + 1)
                    b_v = b[:].rearrange("p (n j) -> p n j", j=HG_CHUNK)
                    dve.tensor_tensor(left[:].rearrange("p (n j) -> p n j", j=HG_CHUNK),
                                      b_v[:, :, HG_CHUNK - 1:HG_CHUNK].broadcast_to([P, N_CHUNK, HG_CHUNK]), b_v,
                                      ALU.subtract).then_inc(S["left_ready"], 1)

                def masked_scores(n):
                    dve.wait_ge(S["scores_done"], n + 1)
                    dve.tensor_tensor(att[:], score[:, :].rearrange("p (c i) -> p c i", i=P),
                                      k.const("hg_causal").unsqueeze(1).broadcast_to([P, TC, P]), ALU.mult).then_inc(S["att_ready"], 1)

                def chain(n):
                    dve.wait_ge(S["updates_done"], n + 1)
                    dve.tensor_copy(state[:, 1, :], upd[0][:, 0:P])
                    for ch in range(1, N_CHUNK - 1):
                        dve.drain()
                        end = (ch + 1) * HG_CHUNK - 1
                        last = dve.scalar_tensor_tensor(out=state[:, ch + 1, :], in0=state[:, ch, :], scalar=eb[:, end:end + 1],
                                                        in1=upd[ch // QC][:, (ch % QC) * P:(ch % QC + 1) * P],
                                                        op0=ALU.mult, op1=ALU.add)
                    last.then_inc(S["chain_done"], 1)

                def keep_values(n, first):
                    dve.wait_ge(S["used_v"], n + 1)
                    if not first:
                        dve.wait_ge(S["outputs_done"], n)
                    dve.tensor_tensor(v_tok[:], proj[1][:, :].rearrange("p (c e) -> p c e", e=P),
                                      v_bias[:, bass.ts(n, P)].unsqueeze(1).broadcast_to([P, TC, P]), ALU.add).then_inc(S["v_kept"], 1)
                    dve.wait_ge(S["v_kept"], n + 1)
                    for r in range(QC):
                        last = dve.tensor_scalar(v_parts[:, :, r, :], v_tok[:], k.const("chunk_of")[:, r:r + 1], None, ALU.mult)
                    last.then_inc(S["v_parts_ready"], 1)

                def decayed(n, first):
                    dve.wait_ge(S["eb_ready"], n + 1)
                    dve.tensor_tensor(q_in[:], q[:], eb[:], ALU.mult).then_inc(S["qin_ready"], 1)
                    dve.wait_ge(S["enb_ready"], n + 1)
                    dve.tensor_tensor(k_in[:], key[:], enb[:], ALU.mult).then_inc(S["kin_ready"], 1)

                dve.tensor_scalar(one_lb[:], lb[:], -1.0, 1.0, ALU.mult, ALU.add)
                dve.drain()
                forget(0, True)
                running(0)
                keep_values(0, True)
                decayed(0, True)
                with dve.Fori(0, HEADS - 1) as n:
                    forget(n + 1, False)
                    masked_scores(n)
                    chain(n)
                    running(n + 1)
                    keep_values(n + 1, False)
                    decayed(n + 1, False)
                masked_scores(HEADS - 1)
                chain(HEADS - 1)

            @block.gpsimd
            def _(pool):
                def key_to_end(n, first):
                    pool.wait_ge(S["eleft_ready"], n + 1)
                    pool.wait_ge(S["key_ready"], n + 1)
                    if not first:
                        pool.wait_ge(S["keys_turned"], n)
                    pool.tensor_tensor(k_end[:], key[:], eleft[:], ALU.mult).then_inc(S["kend_ready"], 1)

                key_to_end(0, True)
                with pool.Fori(1, HEADS) as n:
                    key_to_end(n, False)

        normalize_heads(k, raw, squares, rstd, gate, ohT, [score])


def lower_bound_layer(k, lb):
    nc = k.nc
    with ExitStack() as ctx:
        top = k.sb(ctx, "lb_top", [P, HEADS])
        e = k.sb(ctx, "lb_e", [P, 2, HEADS])
        total = k.sb(ctx, "lb_total", [P, HEADS])
        shifted = k.sem(ctx, "lb_shifted")
        risen = k.sem(ctx, "lb_risen")
        with nc.Block() as block:
            @block.vector
            def _(dve):
                dve.tensor_tensor(top[:], k.col("lb0", 0, 8), k.col("lb1", 0, 8), ALU.max)
                dve.drain()
                dve.tensor_tensor(e[:, 0, :], k.col("lb0", 0, 8), top[:], ALU.subtract)
                dve.tensor_tensor(e[:, 1, :], k.col("lb1", 0, 8), top[:], ALU.subtract).then_inc(shifted, 1)
                dve.wait_ge(risen, 1)
                dve.tensor_tensor(total[:], e[:, 0, :], e[:, 1, :], ALU.add)
                dve.drain()
                dve.reciprocal(total[:], total[:])
                dve.drain()
                dve.tensor_tensor(lb[:], e[:, 0, :], total[:], ALU.mult)

            @block.scalar
            def _(act):
                act.wait_ge(shifted, 1)
                act.activation(e[:], e[:], ACT.Exp).then_inc(risen, 1)


def normalize_heads(k, raw, squares, rstd, gate, ohT, ps):
    nc = k.nc
    with ExitStack() as ctx:
        dev = k.sb(ctx, "hn_dev", [P, HEADS, TC])
        var_ready = k.sem(ctx, "hn_var_ready")
        dev_ready = k.sem(ctx, "hn_dev_ready")
        scaled = k.sem(ctx, "hn_scaled")
        rstd_ready = k.sem(ctx, "hn_rstd_ready")
        turned = k.sem(ctx, "hn_turned")
        kept = k.sem(ctx, "hn_kept")
        with nc.Block() as block:
            @block.vector
            def _(dve):
                dve.tensor_scalar(squares[:], squares[:], 1.0 / P, 1e-6, ALU.mult, ALU.add).then_inc(var_ready, 1)
                dve.wait_ge(dev_ready, 1)
                dve.reciprocal(rstd[:], dev[:]).then_inc(rstd_ready, 1)
                with dve.Fori(0, HEADS) as h:
                    dve.wait_ge(turned, h + 1)
                    dve.scalar_tensor_tensor(out=ohT[:, h, :], in0=ps[0][:, :], scalar=k.col("hg_norm_w", 0, 8)[:, bass.ds(h, 1)],
                                             in1=gate[:, h, :], op0=ALU.mult, op1=ALU.mult).then_inc(kept, 1)

            @block.scalar
            def _(act):
                act.wait_ge(var_ready, 1)
                act.activation(dev[:], squares[:], ACT.Sqrt).then_inc(dev_ready, 1)
                act.wait_ge(rstd_ready, 1)
                for h in range(HEADS):
                    for c in range(TC):
                        last = act.activation(raw[:, c, h, :], raw[:, c, h, :], ACT.Copy, scale=rstd[:, h, c:c + 1])
                    last.then_inc(scaled, 1)

            @block.tensor
            def _(pe):
                for h in range(HEADS):
                    pe.wait_ge(scaled, h + 1)
                    if h >= 1:
                        pe.wait_ge(kept, h)
                    for c in range(TC):
                        last = pe.transpose(ps[0][:, c * P:(c + 1) * P], raw[:, c, h, :], k.const("ident"))
                    last.then_inc(turned, 1)


def key_values(k, kvT, v_tok, gates, k_cmp, v_cmp, Tables):
    nc = k.nc
    w_kv, w_v, w_cmp = k.i["w_kv"], k.i["w_v"], k.i["w_cmp"]
    NV = 2 * GROUPS * P + 3 * HEADS
    with ExitStack() as ctx:
        w = [k.sb(ctx, f"kv_w{s}", [P, KC, P]) for s in range(2)]
        wv = k.sb(ctx, "kv_wv", [P, KC, NV])
        v_bias = k.sb(ctx, "kv_v_bias", [P, 4 * P])
        broadcast_rows(k, "kv_vb", [(k.col("b_in", 46, 2), v_bias[:, 0:256], 0.0), (k.col("b_in", 50, 2), v_bias[:, 256:512], 0.0)])
        ps = k.banks(ctx, "kv_ps", 2)
        psv = k.banks(ctx, "kv_psv", 2)
        psg, = k.banks(ctx, "kv_psg", 1)
        w_loaded = [k.sem(ctx, f"kv_w_loaded{s}") for s in range(2)]
        wv_loaded = k.sem(ctx, "kv_wv_loaded")
        projected = k.sem(ctx, "kv_projected")
        kept = k.sem(ctx, "kv_kept")
        v_projected = k.sem(ctx, "kv_v_projected")
        v_kept = k.sem(ctx, "kv_v_kept")
        g_projected = k.sem(ctx, "kv_g_projected")
        g_kept = k.sem(ctx, "kv_g_kept")
        with nc.Block() as block:
            @block.sync
            def _(sp):
                for s in range(2):
                    sp.dma_start(w[s][:], w_kv[s]).then_inc(w_loaded[s], 16)
                sp.dma_start(wv[:], w_v.rearrange("(k p) n -> p k n", p=P)).then_inc(wv_loaded, 16)
                with sp.Fori(1, 4) as it:
                    for s in range(2):
                        sp.wait_ge(projected, it * 2 + (s - 1))
                        sp.dma_start(w[s][:], w_kv[it * 2 + s]).then_inc(w_loaded[s], 16)

            @block.tensor
            def _(pe):
                def feature_major(it, s, first):
                    pe.wait_ge(w_loaded[s], it * 16 + 16)
                    if not first:
                        pe.wait_ge(kept, it * 2 + (s - 1))
                    for kc in range(KC):
                        last = pe.matmul(ps[s][:, :], w[s][:, kc, :], k.hT[:, kc, :], start=(kc == 0), stop=(kc == KC - 1))
                    last.then_inc(projected, 1)

                for s in range(2):
                    feature_major(0, s, True)
                with pe.Fori(1, 4) as it:
                    for s in range(2):
                        feature_major(it, s, False)
                pe.wait_ge(wv_loaded, 16)
                for c in range(TC):
                    if c >= 2:
                        pe.wait_ge(v_kept, c - 1)
                    for kc in range(KC):
                        last = pe.matmul(psv[c % 2][:, :], k.hT[:, kc, c * P:(c + 1) * P], wv[:, kc, 0:4 * P],
                                         start=(kc == 0), stop=(kc == KC - 1))
                    last.then_inc(v_projected, 1)
                for c in range(TC):
                    for kc in range(KC):
                        last = pe.matmul(psg[:, c * 24:(c + 1) * 24], k.hT[:, kc, c * P:(c + 1) * P], wv[:, kc, 4 * P:NV],
                                         start=(kc == 0), stop=(kc == KC - 1))
                last.then_inc(g_projected, 1)

            @block.scalar
            def _(act):
                for j, at in enumerate((40, 41, 42, 43, 44, 45, 48, 49)):
                    act.wait_ge(projected, j + 1)
                    act.activation(kvT[:, j, :], ps[j % 2][:, :], ACT.Identity, bias=k.col("b_in", at)).then_inc(kept, 1)
                act.wait_ge(g_kept, 1)
                act.activation(gates[:], gates[:], ACT.Sigmoid)

            @block.vector
            def _(dve):
                for c in range(TC):
                    dve.wait_ge(v_projected, c + 1)
                    dve.tensor_tensor(v_tok[:, c, :], psv[c % 2][:, :], v_bias[:], ALU.add).then_inc(v_kept, 1)
                dve.wait_ge(g_projected, 1)
                dve.tensor_tensor(gates[:], psg[:, 0:TC * 24].rearrange("p (c n) -> p c n", n=24),
                                  k.row("b_gate").unsqueeze(1).broadcast_to([P, TC, 24]), ALU.add).then_inc(g_kept, 1)

    NB = GROUPS * N_CMP
    with ExitStack() as ctx:
        w1 = [k.sb(ctx, f"cmp_w1_{s}", [P, CMP_BLOCK, P]) for s in range(2)]
        w2 = k.sb(ctx, "cmp_w2", [P, 2, P])
        bias = k.sb(ctx, "cmp_bias", [P, 2])
        pre = k.sb(ctx, "cmp_pre", [P, 2, NB])
        sig = k.sb(ctx, "cmp_sig", [P, 2, NB])
        ps, psp, psk, psv = k.banks(ctx, "cmp_ps", 4)
        loaded = [k.sem(ctx, f"cmp_loaded{s}") for s in range(2)]
        w2_loaded = k.sem(ctx, "cmp_w2_loaded")
        hidden_done = k.sem(ctx, "cmp_hidden_done")
        pre_ready = k.sem(ctx, "cmp_pre_ready")
        sig_ready = k.sem(ctx, "cmp_sig_ready")
        act_ready = k.sem(ctx, "cmp_act_ready")
        out_done = k.sem(ctx, "cmp_out_done")
        with nc.Block() as block:
            @block.sync
            def _(sp):
                for s in range(2):
                    sp.dma_start(w1[s][:], w_cmp[s].rearrange("(l d) h -> d l h", d=P)).then_inc(loaded[s], 16)
                sp.dma_start(w2[:], k.i["w_cmp2"].rearrange("s h d -> h s d")).then_inc(w2_loaded, 16)

            @block.tensor
            def _(pe):
                for s, pos in enumerate(("cmp_pos_k", "cmp_pos_v")):
                    pe.wait_ge(loaded[s], 16)
                    for l in range(CMP_BLOCK):
                        pe.matmul(ps[:, s * NB:(s + 1) * NB], w1[s][:, l, :],
                                  kvT[:, GROUPS * s:GROUPS * s + GROUPS, l:l + CMP_STRIDE * (N_CMP - 1) + 1:CMP_STRIDE],
                                  start=(l == 0), stop=(l == CMP_BLOCK - 1))
                        last = pe.matmul(psp[:, s:s + 1], w1[s][:, l, :], k.col(pos, l), start=(l == 0), stop=(l == CMP_BLOCK - 1))
                    last.then_inc(hidden_done, 1)
                pe.wait_ge(act_ready, 1)
                pe.wait_ge(w2_loaded, 16)
                pe.matmul(psk[:, 0:NB], w2[:, 0, :], pre[:, 0, :], start=True, stop=True)
                for g in range(GROUPS):
                    last = pe.matmul(psv[0:N_CMP, g * P:(g + 1) * P], pre[:, 1, g * N_CMP:(g + 1) * N_CMP], w2[:, 1, :],
                                     start=True, stop=True)
                last.then_inc(out_done, 1)

            @block.vector
            def _(dve):
                dve.memset(v_cmp[:], 0.0)
                for s, b1 in enumerate(("cmp_b1_k", "cmp_b1_v")):
                    dve.wait_ge(hidden_done, 2)
                    dve.tensor_scalar(bias[:, s:s + 1], psp[:, s:s + 1], k.col(b1), None, ALU.add)
                    dve.drain()
                    dve.tensor_scalar(pre[:, s, :], ps[:, s * NB:(s + 1) * NB], bias[:, s:s + 1], None, ALU.add).then_inc(pre_ready, 1)
                dve.wait_ge(sig_ready, 1)
                dve.tensor_tensor(pre[:], pre[:], sig[:], ALU.mult).then_inc(act_ready, 1)
                dve.wait_ge(out_done, 1)
                dve.tensor_copy(k_cmp[:], psk[:, 0:NB])
                dve.tensor_copy(v_cmp[0:N_CMP], psv[0:N_CMP, 0:GROUPS * P].rearrange("p (g e) -> p g e", e=P))

            @block.scalar
            def _(act):
                act.wait_ge(pre_ready, 2)
                act.activation(sig[:], pre[:], ACT.Sigmoid).then_inc(sig_ready, 1)

    with ExitStack() as ctx:
        onehot = k.sb(ctx, "bias_onehot", [BUCKETS + 1, BT_ROW])
        rel = k.sb(ctx, "bias_rel", [BUCKETS + 1, HEADS])
        r_sb = k.sb(ctx, "bias_r", [HEADS, BT_ROW])
        ps = k.banks(ctx, "bias_ps", 2)
        loaded = k.sem(ctx, "bias_loaded")
        neg_set = k.sem(ctx, "bias_neg_set")
        made = k.sem(ctx, "bias_made")
        kept = k.sem(ctx, "bias_kept")
        spread = k.sem(ctx, "bias_spread")
        with nc.Block() as block:
            @block.sync
            def _(sp):
                sp.dma_start(onehot[:], k.i["buckets"]).then_inc(loaded, 16)
                sp.wait_ge(neg_set, 1)
                sp.dma_start(rel[0:BUCKETS, :], k.i["rel_bias"]).then_inc(loaded, 16)
                sp.wait_ge(kept, 2)
                for h in range(HEADS):
                    sp.dma_start(Tables[h], r_sb[h:h + 1, :].unsqueeze(1).broadcast_to([1, P, BT_ROW])).then_inc(spread, 16)
                sp.wait_ge(spread, 16 * HEADS)

            @block.tensor
            def _(pe):
                pe.wait_ge(loaded, 32)
                for j in range(2):
                    pe.matmul(ps[j][0:HEADS, :], rel[:], onehot[:, j * 512:(j + 1) * 512], start=True, stop=True).then_inc(made, 1)

            @block.vector
            def _(dve):
                dve.memset(rel[:], NEG).then_inc(neg_set, 1)
                for j in range(2):
                    dve.wait_ge(made, j + 1)
                    dve.tensor_copy(r_sb[:, j * 512:(j + 1) * 512], ps[j][0:HEADS, :]).then_inc(kept, 1)


def sparse_attention(k, onT):
    nc = k.nc
    UNITS = [(br, c) for br in range(2) for c in range(TC)]
    NU = len(UNITS) + 1
    with ExitStack() as ctx:
        kvT = k.sb(ctx, "at_kvT", [P, 8, SEQ])
        v_tok = k.sb(ctx, "at_v_tok", [P, TC, 512])
        gates = k.sb(ctx, "at_gates", [P, TC, 24])
        k_cmp = k.sb(ctx, "at_k_cmp", [P, GROUPS * N_CMP])
        v_cmp = k.sb(ctx, "at_v_cmp", [P, GROUPS, P])
        spread = nc.dram_tensor("bias_spread_rows", [HEADS, P, BT_ROW], F32).ap()
        key_values(k, kvT, v_tok, gates, k_cmp, v_cmp, spread)

        wq = [k.sb(ctx, f"at_wq{s}", [P, KC, P]) for s in range(2)]
        q = [k.sb(ctx, f"at_q{s}", [P, SEQ]) for s in range(2)]
        q_bias = k.sb(ctx, "at_q_bias", [P, HEADS])
        table = [k.sb(ctx, f"at_table{s}", [P, BTW]) for s in range(2)]
        values = k.sb(ctx, "at_values", [P, 2, TC, P])
        cvalues = k.sb(ctx, "at_cvalues", [P, P])
        NP = 4
        p = [k.sb(ctx, f"at_p{s}", [P, SEQ]) for s in range(NP)]
        top = k.sb(ctx, "at_top", [P, NU, TC])
        ntop = k.sb(ctx, "at_ntop", [P, NU, TC])
        total = k.sb(ctx, "at_total", [P, NU, TC])
        factor = k.sb(ctx, "at_factor", [P, NU, TC])
        pT = [k.sb(ctx, f"at_pT{s}", [P, SEQ]) for s in range(2)]
        cpT = k.sb(ctx, "at_cpT", [P, SEQ])
        spare = k.sb(ctx, "at_spare", [P, 2])

        sc = k.banks(ctx, "at_sc", 3)
        tr = k.banks(ctx, "at_tr", 2)
        o_ps, = k.banks(ctx, "at_o", 1)
        proj, = k.banks(ctx, "at_proj", 1)

        names = ("wq_loaded0 wq_loaded1 table_loaded0 table_loaded1 q_projected q_kept bias_ready "
                 "scored logits_ready exp_ready factor_ready p_ready turned pT_ready mixed o_kept values_ready cleared").split()
        S = {n: k.sem(ctx, "at_" + n) for n in names}

        def pairs(eng, head):
            head(0, 0, 0)
            head(1, 1, 0)
            with eng.Fori(1, HEADS // 2 - 1) as it:
                head(it * 2, 0, it - 1)
                head(it * 2 + 1, 1, it - 1)
            head(HEADS - 2, 0, GROUPS - 1)
            head(HEADS - 1, 1, GROUPS - 1)

        def loads(h, s):
            return 16 * (h // 2 + 1) if isinstance(h, int) else (h - s) * 8 + 16

        def after_first(h):
            return not isinstance(h, int) or h > 0

        with nc.Block() as block:
            @block.sync
            def _(sp):
                def load_head(h, s, g):
                    if not isinstance(h, int) or h >= 2:
                        sp.wait_ge(S["q_projected"], h - 1)
                    sp.dma_start(wq[s][:], k.i["w_nq"][h]).then_inc(S[f"wq_loaded{s}"], 16)
                    if not isinstance(h, int) or h >= 2:
                        sp.wait_ge(S["logits_ready"], (h - 1) * NU)
                    view = spread[h].rearrange("p m -> (p m)")[P - 1:P - 1 + P * (BT_ROW - 1)]
                    view = view.rearrange("(p m) -> p m", m=BT_ROW - 1)[:, 0:BTW]
                    sp.dma_start(table[s][:], view).then_inc(S[f"table_loaded{s}"], 16)

                pairs(sp, load_head)

            @block.tensor
            def _(pe):
                def project(h, s):
                    pe.wait_ge(S[f"wq_loaded{s}"], loads(h, s))
                    if after_first(h):
                        pe.wait_ge(S["q_kept"], h)
                    for kc in range(KC):
                        last = pe.matmul(proj[:, :], wq[s][:, kc, :], k.hT[:, kc, :], start=(kc == 0), stop=(kc == KC - 1))
                    last.then_inc(S["q_projected"], 1)

                def scores(h, s, g, u):
                    if u >= 3 or after_first(h):
                        pe.wait_ge(S["logits_ready"], h * NU + (u - 2))
                    if u == 0:
                        pe.wait_ge(S["q_kept"], h + 1)
                    if u < len(UNITS):
                        br, c = UNITS[u]
                        keys = kvT[:, 4 + GROUPS * br:4 + GROUPS * (br + 1), :]
                        last = pe.matmul(sc[u % 3][:, 0:(c + 1) * P], q[s][:, c * P:(c + 1) * P],
                                         keys[:, g, 0:(c + 1) * P], start=True, stop=True)
                    else:
                        for c in range(TC):
                            last = pe.matmul(sc[u % 3][:, c * N_CMP:(c + 1) * N_CMP], q[s][:, c * P:(c + 1) * P],
                                             k_cmp[:, bass.ts(g, N_CMP)], start=True, stop=True)
                    last.then_inc(S["scored"], 1)

                def turn(h, u):
                    pe.wait_ge(S["p_ready"], h * NU + (u + 1))
                    if u >= 2 or after_first(h):
                        pe.wait_ge(S["pT_ready"], h * NU + (u - 1))
                    if u < len(UNITS):
                        for kk in range(UNITS[u][1] + 1):
                            last = pe.transpose(tr[u % 2][:, kk * P:(kk + 1) * P], p[u % NP][:, kk * P:(kk + 1) * P], k.const("ident"))
                    else:
                        for c in range(TC):
                            last = pe.transpose(tr[u % 2][0:N_CMP, c * P:(c + 1) * P],
                                                p[u % NP][:, c * N_CMP:(c + 1) * N_CMP], k.const("ident"))
                    last.then_inc(S["turned"], 1)

                def mix(h, u):
                    pe.wait_ge(S["pT_ready"], h * NU + (u + 1))
                    if u == 0:
                        pe.wait_ge(S["values_ready"], h + 1)
                        if after_first(h):
                            pe.wait_ge(S["o_kept"], h)
                    if u < len(UNITS):
                        br, c = UNITS[u]
                        for kk in range(c + 1):
                            last = pe.matmul(o_ps[:, c * P:(c + 1) * P], values[:, br, kk, :], pT[u % 2][:, kk * P:(kk + 1) * P],
                                             start=(u == 0), stop=False, skip_group_check=True)
                    else:
                        last = pe.matmul(o_ps[:, :], cvalues[:], cpT[:], start=False, stop=True, skip_group_check=True)
                    last.then_inc(S["mixed"], 1)

                def head(h, s, g):
                    for u in range(3):
                        scores(h, s, g, u)
                    if not (isinstance(h, int) and h == HEADS - 1):
                        project(h + 1, 1 - s)
                    for u in range(NU):
                        turn(h, u)
                        if u + 3 < NU:
                            scores(h, s, g, u + 3)
                        if u >= 1:
                            mix(h, u - 1)
                    mix(h, NU - 1)

                project(0, 0)
                pairs(pe, head)

            @block.scalar
            def _(act):
                act.activation(q_bias[:], k.col("b_in", 32, 8), ACT.Copy, scale=ATT_SCALE).then_inc(S["bias_ready"], 1)
                act.wait_ge(S["bias_ready"], 1)

                def keep_q(h, s):
                    act.wait_ge(S["q_projected"], h + 1)
                    act.activation(q[s][:], proj[:, :], ACT.Identity, bias=q_bias[:, bass.ds(h, 1)], scale=ATT_SCALE).then_inc(S["q_kept"], 1)

                def weights(h, u):
                    act.wait_ge(S["logits_ready"], h * NU + (u + 1))
                    if u < len(UNITS):
                        n = (UNITS[u][1] + 1) * P
                        act.activation(p[u % NP][:, 0:n], p[u % NP][:, 0:n], ACT.Exp, bias=ntop[:, u, 0:1],
                                       accum_out=total[:, u, 0:1]).then_inc(S["exp_ready"], 1)
                    else:
                        for c in range(TC):
                            last = act.activation(p[u % NP][:, c * N_CMP:(c + 1) * N_CMP], p[u % NP][:, c * N_CMP:(c + 1) * N_CMP],
                                                  ACT.Exp, bias=ntop[:, u, c:c + 1], accum_out=total[:, u, c:c + 1])
                        last.then_inc(S["exp_ready"], 1)

                def keep_turned(h, u):
                    act.wait_ge(S["turned"], h * NU + (u + 1))
                    if u < len(UNITS):
                        if u >= 2 or after_first(h):
                            act.wait_ge(S["mixed"], h * NU + (u - 1))
                        n = (UNITS[u][1] + 1) * P
                        act.activation(pT[u % 2][:, 0:n], tr[u % 2][:, 0:n], ACT.Copy).then_inc(S["pT_ready"], 1)
                    else:
                        if after_first(h):
                            act.wait_ge(S["mixed"], h * NU)
                        else:
                            act.wait_ge(S["cleared"], 1)
                        act.activation(cpT[0:N_CMP, :], tr[u % 2][0:N_CMP, :], ACT.Copy).then_inc(S["pT_ready"], 1)

                def head(h, s, g):
                    for u in range(NU + 2):
                        if u < NU:
                            weights(h, u)
                        if u == 2 and not (isinstance(h, int) and h == HEADS - 1):
                            keep_q(h + 1, 1 - s)
                        if u >= 2:
                            keep_turned(h, u - 2)

                keep_q(0, 0)
                pairs(act, head)

            @block.vector
            def _(dve):
                dve.memset(cpT[:], 0.0).then_inc(S["cleared"], 1)

                def logits(h, s, u):
                    if u == 0:
                        dve.wait_ge(S[f"table_loaded{s}"], loads(h, s))
                    dve.wait_ge(S["scored"], h * NU + (u + 1))
                    if u >= NP or after_first(h):
                        dve.wait_ge(S["turned"], h * NU + (u - NP + 1 if u >= NP else 0))
                    dve.memset(spare[:, 0:1], 0.0)
                    buf, bank = p[u % NP], sc[u % 3]
                    if u < len(UNITS):
                        n = (UNITS[u][1] + 1) * P
                        dve.tensor_tensor_reduce(buf[:, 0:n], bank[:, 0:n], table[s][:, BT0 + P - n:BT0 + P], 1.0, NEG * 10,
                                                 ALU.add, ALU.max, top[:, u, 0:1])
                        dve.drain()
                        dve.tensor_scalar(ntop[:, u, 0:1], top[:, u, 0:1], -1.0, None, ALU.mult).then_inc(S["logits_ready"], 1)
                    else:
                        for c in range(TC):
                            at = BT0 + CMP_BLOCK - 1 - c * P
                            dve.tensor_tensor_reduce(buf[:, c * N_CMP:(c + 1) * N_CMP], bank[:, c * N_CMP:(c + 1) * N_CMP],
                                                     table[s][:, at:at + CMP_STRIDE * (N_CMP - 1) + 1:CMP_STRIDE], 1.0, NEG * 10,
                                                     ALU.add, ALU.max, top[:, u, c:c + 1])
                        dve.drain()
                        dve.tensor_scalar(ntop[:, u, :], top[:, u, :], -1.0, None, ALU.mult).then_inc(S["logits_ready"], 1)

                def normalized(h, u):
                    dve.wait_ge(S["exp_ready"], h * NU + (u + 1))
                    nr = 1 if u < len(UNITS) else TC
                    dve.reciprocal(factor[:, u, 0:nr], total[:, u, 0:nr])
                    dve.drain()
                    buf = p[u % NP]
                    if u < len(UNITS):
                        br, c = UNITS[u]
                        n = (c + 1) * P
                        dve.tensor_scalar(buf[:, 0:n], buf[:, 0:n], factor[:, u, 0:1], gates[:, c, bass.ds(h * 3 + (1 + br), 1)],
                                          ALU.mult, ALU.mult).then_inc(S["p_ready"], 1)
                    else:
                        for c in range(TC):
                            blk = buf[:, c * N_CMP:(c + 1) * N_CMP]
                            dve.tensor_scalar(blk, blk, factor[:, u, c:c + 1], gates[:, c, bass.ds(h * 3, 1)], ALU.mult, ALU.mult)
                        dve.drain()
                        blk = buf[:, 0:TC * N_CMP]
                        dve.tensor_tensor(blk, blk, k.const("cmp_ok"), ALU.mult).then_inc(S["p_ready"], 1)

                def head(h, s, g):
                    for u in range(NU + 1):
                        if u < NU:
                            logits(h, s, u)
                        if u >= 1:
                            normalized(h, u - 1)
                    dve.wait_ge(S["mixed"], h * NU + NU)
                    dve.tensor_copy(onT[:, h, :], o_ps[:, :]).then_inc(S["o_kept"], 1)

                pairs(dve, head)

            @block.gpsimd
            def _(pool):
                def stage_values(h, s, g):
                    if after_first(h):
                        pool.wait_ge(S["mixed"], h * NU)
                        pool.tensor_tensor(spare[:, 1:2], k.const("ones", 0, 1), k.const("ones", 0, 1), ALU.add)
                    v_v = v_tok[:].rearrange("p c (b e) -> p c b e", e=P)
                    for br in range(2):
                        pool.tensor_copy(values[:, br, :, :], v_v[:, :, 2 * br:2 * br + 2, :][:, :, g, :])
                    pool.tensor_copy(cvalues[:], v_cmp[:, g, :]).then_inc(S["values_ready"], 1)

                pairs(pool, stage_values)


def merge_branches(k, ohT, onT, mergedT):
    nc = k.nc
    with ExitStack() as ctx:
        w = [k.sb(ctx, f"mg_w{s}", [P, KC, P]) for s in range(4)]
        sig = [k.sb(ctx, f"mg_sig{s}", [P, SEQ]) for s in range(2)]
        part = [k.sb(ctx, f"mg_part{s}", [P, SEQ]) for s in range(2)]
        ps = k.banks(ctx, "mg_ps", 4)
        loaded = [k.sem(ctx, f"mg_loaded{s}") for s in range(4)]
        done = [k.sem(ctx, f"mg_done{s}") for s in range(4)]
        sig_ready = [k.sem(ctx, f"mg_sig_ready{s}") for s in range(2)]
        part_ready = [k.sem(ctx, f"mg_part_ready{s}") for s in range(2)]
        sources = (k.hT, k.hT, ohT, onT)
        zeros = k.sb(ctx, "mg_zeros", [SLOTS, D])
        zeros_ready = k.sem(ctx, "mg_zeros_ready")
        zeroed = k.dma_sems["zeroed"]
        with nc.Block() as block:
            @block.sync
            def _(sp):
                for s in range(4):
                    sp.dma_start(w[s][:], k.i["w_merge"][0, s]).then_inc(loaded[s], 16)
                with sp.Fori(1, KC) as j:
                    for s in range(4):
                        sp.wait_ge(done[s], j)
                        sp.dma_start(w[s][:], k.i["w_merge"][j, s]).then_inc(loaded[s], 16)

            @block.gpsimd
            def _(pool):
                pool.memset(zeros[:], 0.0).then_inc(zeros_ready, 1)
                pool.wait_ge(zeros_ready, 1)
                pool.wait_ge(done[1], 2)
                pool.dma_start(k.sent[0].rearrange("e s d -> s e d"),
                               zeros[:].unsqueeze(1).broadcast_to([SLOTS, N_EXP, D])).then_inc(zeroed, 16)
                pool.wait_ge(zeroed, 16)

            @block.tensor
            def _(pe):
                def step(j, first):
                    for s in range(4):
                        pe.wait_ge(loaded[s], j * 16 + 16)
                        if not first:
                            pe.wait_ge(sig_ready[s] if s < 2 else part_ready[s - 2], j)
                        for kc in range(KC):
                            last = pe.matmul(ps[s][:, :], w[s][:, kc, :], sources[s][:, kc, :], start=(kc == 0), stop=(kc == KC - 1))
                        last.then_inc(done[s], 1)

                step(0, True)
                with pe.Fori(1, KC) as j:
                    step(j, False)

            @block.scalar
            def _(act):
                def step(j, first):
                    for s in range(2):
                        act.wait_ge(done[s], j + 1)
                        if not first:
                            act.wait_ge(part_ready[s], j)
                        act.activation(sig[s][:], ps[s][:, :], ACT.Sigmoid, bias=k.col("b_mg", 8 * s, 8)[:, bass.ds(j, 1)]).then_inc(sig_ready[s], 1)

                step(0, True)
                with act.Fori(1, KC) as j:
                    step(j, False)

            @block.vector
            def _(dve):
                with dve.Fori(0, KC) as j:
                    for s in range(2):
                        dve.wait_ge(done[2 + s], j + 1)
                        dve.wait_ge(sig_ready[s], j + 1)
                        dve.tensor_tensor(part[s][:], sig[s][:], ps[2 + s][:, :], ALU.mult).then_inc(part_ready[s], 1)
                    dve.drain()
                    dve.tensor_tensor(mergedT[:, j, :], part[0][:], part[1][:], ALU.add)
                    dve.drain()


def project_out(k, tag, weights, source, gain, residual):
    nc = k.nc
    HALF = 512
    with ExitStack() as ctx:
        w = [k.sb(ctx, f"{tag}_w{s}", [P, KC, HALF]) for s in range(2)]
        part = [k.sb(ctx, f"{tag}_part{s}", [P, HALF]) for s in range(2)]
        ps = k.banks(ctx, f"{tag}_ps", 2)
        loaded = [k.sem(ctx, f"{tag}_loaded{s}") for s in range(2)]
        done = k.sem(ctx, f"{tag}_done")
        kept = k.sem(ctx, f"{tag}_kept")
        w_v = weights.rearrange("(k p) n -> p k n", p=P)
        units = [(h, c) for h in range(2) for c in range(TC)]
        with nc.Block() as block:
            @block.sync
            def _(sp):
                for h in range(2):
                    sp.dma_start(w[h][:], w_v[:, :, h * HALF:(h + 1) * HALF]).then_inc(loaded[h], 16)

            @block.tensor
            def _(pe):
                for n, (h, c) in enumerate(units):
                    if c == 0:
                        pe.wait_ge(loaded[h], 16)
                    if n >= 2:
                        pe.wait_ge(kept, n - 1)
                    for kc in range(KC):
                        last = pe.matmul(ps[n % 2][:, :], source[:, kc, c * P:(c + 1) * P], w[h][:, kc, :],
                                         start=(kc == 0), stop=(kc == KC - 1))
                    last.then_inc(done, 1)

            @block.vector
            def _(dve):
                for n, (h, c) in enumerate(units):
                    cut = slice(h * HALF, (h + 1) * HALF)
                    dve.wait_ge(done, n + 1)
                    dve.tensor_tensor(part[n % 2][:], ps[n % 2][:, :], gain[:, cut], ALU.mult).then_inc(kept, 1)
                    dve.wait_ge(kept, n + 1)
                    dve.scalar_tensor_tensor(out=k.x[:, c, cut], in0=k.x[:, c, cut], scalar=float(residual), in1=part[n % 2][:],
                                             op0=ALU.mult, op1=ALU.add)


def route(k, tag, weights, bias_row, row_of, share, most):
    nc = k.nc
    with ExitStack() as ctx:
        w = k.sb(ctx, f"{tag}_w", [P, KC, N_GRP + N_EXP])
        lg = k.sb(ctx, f"{tag}_lg", [P, TC, N_GRP + N_EXP])
        small = {n: k.sb(ctx, f"{tag}_{n}", [P, TC]) for n in ("gtop", "gsum", "m", "m1", "m2", "d")}
        ge = k.sb(ctx, f"{tag}_ge", [P, TC, N_GRP])
        goh = k.sb(ctx, f"{tag}_goh", [P, TC, N_GRP])
        pen = k.sb(ctx, f"{tag}_pen", [P, TC, N_EXP])
        el = k.sb(ctx, f"{tag}_el", [P, TC, N_EXP])
        place = k.sb(ctx, f"{tag}_place", [P, TC, N_EXP])
        ohs = k.sb(ctx, f"{tag}_oh", [P, 2, TC, N_EXP])
        oh = [ohs[:, s] for s in range(2)]
        rows = k.sb(ctx, f"{tag}_rows", [P, 2, TC])
        earlier = k.sb(ctx, f"{tag}_earlier", [P, 2, TC])
        later = k.sb(ctx, f"{tag}_later", [P, 2, TC, PASSES - 1])
        passed = k.sb(ctx, f"{tag}_passed", [P, 2, TC])
        chosen = k.sb(ctx, f"{tag}_chosen", [P, TC, N_EXP])
        mostf = k.sb(ctx, f"{tag}_mostf", [P, 1])
        ps = k.banks(ctx, f"{tag}_ps", 3)
        w_loaded = k.sem(ctx, f"{tag}_w_loaded")
        logits_done = k.sem(ctx, f"{tag}_logits_done")
        shifted = k.sem(ctx, f"{tag}_shifted")
        risen = k.sem(ctx, f"{tag}_risen")
        chosen_ready = k.sem(ctx, f"{tag}_chosen_ready")
        counted = k.sem(ctx, f"{tag}_counted")
        with nc.Block() as block:
            @block.sync
            def _(sp):
                sp.dma_start(w[:], weights.rearrange("(k p) n -> p k n", p=P)).then_inc(w_loaded, 16)

            @block.tensor
            def _(pe):
                pe.wait_ge(w_loaded, 16)
                NL = N_GRP + N_EXP
                for c in range(TC):
                    for kc in range(KC):
                        last = pe.matmul(ps[0][:, c * NL:(c + 1) * NL], k.hT[:, kc, c * P:(c + 1) * P], w[:, kc, :],
                                         start=(kc == 0), stop=(kc == KC - 1))
                last.then_inc(logits_done, 1)
                pe.wait_ge(chosen_ready, 1)
                for c in range(TC):
                    for b in range(c + 1):
                        pe.matmul(ps[1][:, c * N_EXP:(c + 1) * N_EXP], k.const("before") if b == c else k.const("ones"),
                                  chosen[:, b, :], start=(b == 0), stop=(b == c))
                for b in range(TC):
                    last = pe.matmul(ps[2][:, 0:N_EXP], k.const("ones"), chosen[:, b, :], start=(b == 0), stop=(b == TC - 1))
                last.then_inc(counted, 1)

            @block.scalar
            def _(act):
                act.wait_ge(shifted, 1)
                act.activation(ge[:], ge[:], ACT.Exp).then_inc(risen, 1)
                act.wait_ge(shifted, 2)
                act.activation(small["d"][:], small["d"][:], ACT.Exp).then_inc(risen, 1)

            @block.vector
            def _(dve):
                def per_token(a, n):
                    return a[:].unsqueeze(2).broadcast_to([P, TC, n])

                def first_best(values, n, top, out):
                    dve.tensor_reduce(top[:], values, AX.X, ALU.max)
                    dve.drain()
                    dve.tensor_tensor(out, values, per_token(top, n), ALU.is_equal)
                    dve.drain()
                    dve.tensor_tensor(out, out, k.const("first", 0, n).unsqueeze(1).broadcast_to([P, TC, n]), ALU.mult)
                    dve.drain()
                    dve.tensor_reduce(small["m"][:], out, AX.X, ALU.max)
                    dve.drain()
                    dve.tensor_tensor(out, out, per_token(small["m"], n), ALU.is_equal)
                    dve.drain()

                dve.wait_ge(logits_done, 1)
                NL = N_GRP + N_EXP
                dve.tensor_tensor(lg[:], ps[0][:, 0:TC * NL].rearrange("p (c n) -> p c n", n=NL),
                                  bias_row.unsqueeze(1).broadcast_to([P, TC, NL]), ALU.add)
                dve.drain()
                first_best(lg[:, :, 0:N_GRP], N_GRP, small["gtop"], goh[:])
                dve.tensor_tensor(ge[:], lg[:, :, 0:N_GRP], per_token(small["gtop"], N_GRP), ALU.subtract).then_inc(shifted, 1)
                dve.tensor_scalar(pen[:].rearrange("p c (g e) -> p c g e", e=PER_GRP),
                                  goh[:].unsqueeze(3).broadcast_to([P, TC, N_GRP, PER_GRP]), 1.0, -NEG, ALU.subtract, ALU.mult)
                dve.drain()
                dve.tensor_tensor(el[:], lg[:, :, N_GRP:NL], pen[:], ALU.add)
                dve.drain()
                first_best(el[:], N_EXP, small["m1"], oh[0])
                dve.tensor_scalar(pen[:], oh[0], 2 * NEG, None, ALU.mult)
                dve.drain()
                dve.tensor_tensor(el[:], el[:], pen[:], ALU.add)
                dve.drain()
                first_best(el[:], N_EXP, small["m2"], oh[1])
                dve.tensor_tensor(chosen[:], oh[0], oh[1], ALU.add).then_inc(chosen_ready, 1)
                dve.tensor_tensor(small["d"][:], small["m2"][:], small["m1"][:], ALU.subtract).then_inc(shifted, 1)
                dve.wait_ge(risen, 2)
                dve.tensor_reduce(small["gsum"][:], ge[:], AX.X, ALU.add)
                dve.tensor_scalar(share[:, 0, :], small["d"][:], 1.0, None, ALU.add)
                dve.drain()
                dve.tensor_tensor(share[:, 0, :], share[:, 0, :], small["gsum"][:], ALU.mult)
                dve.drain()
                dve.reciprocal(share[:, 0, :], share[:, 0, :])
                dve.drain()
                dve.tensor_tensor(share[:, 1, :], share[:, 0, :], small["d"][:], ALU.mult)
                dve.wait_ge(counted, 1)
                counts = ps[1][:, 0:TC * N_EXP].rearrange("p (c n) -> p c n", n=N_EXP)
                dve.tensor_tensor(place[:], counts, k.const("expert_row").unsqueeze(1).broadcast_to([P, TC, N_EXP]), ALU.add)
                dve.tensor_reduce(mostf[:], ps[2][:, 0:N_EXP], AX.X, ALU.max)
                for s in range(2):
                    dve.tensor_tensor(el[:], oh[s], counts, ALU.mult)
                    dve.drain()
                    dve.tensor_reduce(earlier[:, s, :], el[:], AX.X, ALU.add)
                    dve.drain()
                for s in range(2):
                    dve.tensor_tensor(oh[s], oh[s], place[:], ALU.mult)
                dve.tensor_tensor(later[:], earlier[:].unsqueeze(3).broadcast_to([P, 2, TC, PASSES - 1]),
                                  k.const("pass_start").unsqueeze(1).unsqueeze(1).broadcast_to([P, 2, TC, PASSES - 1]), ALU.is_ge)
                dve.tensor_copy(most[:], mostf[:])
                dve.drain()
                dve.tensor_reduce(rows[:], ohs[:], AX.X, ALU.add)
                dve.tensor_reduce(passed[:], later[:], AX.X, ALU.add)
                dve.drain()
                dve.scalar_tensor_tensor(out=row_of, in0=passed[:], scalar=float((N_EXP - 1) * SLOTS), in1=rows[:],
                                         op0=ALU.mult, op1=ALU.add)


class Experts:

    def __init__(self, k, ctx, tag, nth, F, up_parts, down):
        self.nth = nth
        self.k, self.tag, self.F, self.FC, self.NU = k, tag, F, F // P, len(up_parts)
        self.up_v = [u.rearrange("e (k p) n -> e p k n", p=P) for u in up_parts]
        self.down_v = down.rearrange("e (f p) n -> e p f n", p=P)
        self.wu = [[k.sb(ctx, f"{tag}_wu{u}{e}", [P, KC, 512]) for e in range(2)] for u in range(self.NU)]
        self.wd = [k.sb(ctx, f"{tag}_wd{e}", [P, self.FC, D]) for e in range(2)]
        self.u_loaded = [[k.sem(ctx, f"{tag}_u_loaded{u}{e}") for e in range(2)] for u in range(self.NU)]
        self.d_loaded = [k.sem(ctx, f"{tag}_d_loaded{e}") for e in range(2)]
        self.row_of = k.sb(ctx, f"{tag}_row_of", [P, 2, TC], U32)
        self.share = k.sb(ctx, f"{tag}_share", [P, 2, TC])
        self.most = k.sb(ctx, f"{tag}_most", [P, 1], I32)

    def load_up(self, sp, m, u):
        for e in range(2):
            sp.dma_start(self.wu[u][e][:], self.up_v[u][m * 2 + e]).then_inc(self.u_loaded[u][e], 16)

    def load_down(self, sp, m):
        for e in range(2):
            sp.dma_start(self.wd[e][:], self.down_v[m * 2 + e]).then_inc(self.d_loaded[e], 16)

    def load_first(self):
        with self.k.nc.Block() as block:
            @block.sync
            def _(sp):
                for u in range(self.NU):
                    self.load_up(sp, 0, u)
                self.load_down(sp, 0)

    def run(self, rows, scale, shift):
        k, tag, F, FC, NU, most = self.k, self.tag, self.F, self.FC, self.NU, self.most
        wu, wd, u_loaded, d_loaded = self.wu, self.wd, self.u_loaded, self.d_loaded
        nc = k.nc
        S2 = 2 * SLOTS
        LAST_UP = f"up_done{NU - 1}"
        with ExitStack() as ctx:
            xg = k.sb(ctx, f"{tag}_xg", [P, D])
            hg = k.sb(ctx, f"{tag}_hg", [P, KC, S2])
            sig = k.sb(ctx, f"{tag}_sig", [P, F])
            mid = k.sb(ctx, f"{tag}_mid", [P, F])
            midT = k.sb(ctx, f"{tag}_midT", [P, FC, S2])
            res = k.sb(ctx, f"{tag}_res", [P, D])
            zeros = k.sb(ctx, f"{tag}_zeros", [SLOTS, D])
            x_ps = k.banks(ctx, f"{tag}_x_ps", 2)
            mid_ps, = k.banks(ctx, f"{tag}_mid_ps", 1)
            up_ps = k.banks(ctx, f"{tag}_up_ps", NU)
            res_ps = k.banks(ctx, f"{tag}_res_ps", 2)
            names = ("zeros_ready x_loaded x_turned hg_ready up_done0 up_done1 sig_ready mid_ready mid_turned "
                     "midT_ready down_done res_ready res_stored").split()
            S = {n: k.sem(ctx, f"{tag}_{n}") for n in names}
            sent, zeroed = k.dma_sems["sent"], k.dma_sems[f"{tag}_zeroed"]

            def over_pairs(eng, begin, step):
                begin(0, 0)
                step(0, 0, 0, True, True)
                with eng.Fori(1, PAIRS - 1) as m:
                    step(m, 0, m, False, True)
                step(PAIRS - 1, 0, PAIRS - 1, False, False)
                busiest = eng.value_load(most[0:1, 0:1], min_val=0, max_val=SEQ)
                with eng.If(busiest > SLOTS):
                    with eng.Fori(1, PASSES) as j:
                        begin(j, j * PAIRS)
                        with eng.Fori(0, PAIRS - 1) as m:
                            step(m, j, j * PAIRS + m, False, True)
                        step(PAIRS - 1, j, j * PAIRS + (PAIRS - 1), False, False)

            with nc.Block() as block:
                @block.sync
                def _(sp):
                    def load_rows(m, j):
                        for e in range(2):
                            sp.dma_start(xg[e * SLOTS:(e + 1) * SLOTS, :], k.sent[j, m * 2 + e]).then_inc(S["x_loaded"], 16)

                    def begin(j, n):
                        if isinstance(j, int):
                            sp.wait_ge(sent, 16 * 2 * TC * (self.nth + 1))
                        else:
                            sp.wait_ge(S["x_turned"], n)
                        load_rows(0, j)

                    def step(m, j, n, first, more):
                        for u in range(NU):
                            if not first:
                                sp.wait_ge(S[f"up_done{u}"], n)
                                self.load_up(sp, m, u)
                        if more:
                            sp.wait_ge(S["x_turned"], n + 1)
                            load_rows(m + 1, j)
                        if not first:
                            sp.wait_ge(S["down_done"], n)
                            self.load_down(sp, m)

                    over_pairs(sp, begin, step)

                @block.gpsimd
                def _(pool):
                    busiest = pool.value_load(most[0:1, 0:1], min_val=0, max_val=SEQ)
                    with pool.If(busiest > SLOTS):
                        pool.memset(zeros[:], 0.0).then_inc(S["zeros_ready"], 1)
                        pool.wait_ge(S["zeros_ready"], 1)
                        for j in range(1, PASSES):
                            pool.dma_start(k.sent[j].rearrange("e s d -> s e d"),
                                           zeros[:].unsqueeze(1).broadcast_to([SLOTS, N_EXP, D])).then_inc(zeroed, 16)
                        pool.wait_ge(zeroed, 16 * (PASSES - 1))
                    for c in range(TC):
                        for s in range(2):
                            pool.indirect_dma_start(k.sent.rearrange("j e s d -> (j e s) d"),
                                                    bass.IndirectOffsetOnAxis(ap=self.row_of[:, s, c:c + 1], axis=0),
                                                    rows[:, c, :], None).then_inc(sent, 16)

                @block.tensor
                def _(pe):
                    def turn_rows(n):
                        pe.wait_ge(S["x_loaded"], n * 32 + 32)
                        for kc in range(KC):
                            last = pe.transpose(x_ps[kc // 4][:, kc % 4 * P:(kc % 4 + 1) * P], xg[:, kc * P:(kc + 1) * P], k.const("ident"))
                        last.then_inc(S["x_turned"], 1)

                    def begin(j, n):
                        turn_rows(n)

                    def step(m, j, n, first, more):
                        pe.wait_ge(S["hg_ready"], n + 1)
                        for u in range(NU):
                            for e in range(2):
                                pe.wait_ge(u_loaded[u][e], n * 16 + 16)
                            if u == 0 and not first:
                                pe.wait_ge(S["mid_ready"], n)
                            for kc in range(KC):
                                for e in range(2):
                                    last = pe.matmul(up_ps[u][e * SLOTS:(e + 1) * SLOTS, :], hg[:, kc, e * SLOTS:(e + 1) * SLOTS],
                                                     wu[u][e][:, kc, :], start=(kc == 0), stop=(kc == KC - 1))
                            last.then_inc(S[f"up_done{u}"], 1)
                        if more:
                            turn_rows(n + 1)
                        pe.wait_ge(S["mid_ready"], n + 1)
                        for f in range(FC):
                            last = pe.transpose(mid_ps[:, f * P:(f + 1) * P], mid[:, f * P:(f + 1) * P], k.const("ident"))
                        last.then_inc(S["mid_turned"], 1)
                        pe.wait_ge(S["midT_ready"], n + 1)
                        for e in range(2):
                            pe.wait_ge(d_loaded[e], n * 16 + 16)
                        if not first:
                            pe.wait_ge(S["res_ready"], n)
                        for half in range(2):
                            for f in range(FC):
                                for e in range(2):
                                    last = pe.matmul(res_ps[half][e * SLOTS:(e + 1) * SLOTS, :], midT[:, f, e * SLOTS:(e + 1) * SLOTS],
                                                     wd[e][:, f, half * 512:(half + 1) * 512], start=(f == 0), stop=(f == FC - 1))
                        last.then_inc(S["down_done"], 1)

                    over_pairs(pe, begin, step)

                @block.scalar
                def _(act):
                    def modulated(n, first):
                        act.wait_ge(S["x_turned"], n + 1)
                        if not first:
                            act.wait_ge(S[LAST_UP], n)
                        for kc in range(KC):
                            last = act.activation(hg[:, kc, :], x_ps[kc // 4][:, kc % 4 * P:(kc % 4 + 1) * P], ACT.Identity,
                                                  scale=scale[:, kc:kc + 1], bias=shift[:, kc:kc + 1])
                        last.then_inc(S["hg_ready"], 1)

                    def begin(j, n):
                        modulated(n, isinstance(j, int))

                    def step(m, j, n, first, more):
                        act.wait_ge(S["up_done0"], n + 1)
                        if not first:
                            act.wait_ge(S["mid_ready"], n)
                        act.activation(sig[:], up_ps[0][:, 0:F], ACT.Sigmoid).then_inc(S["sig_ready"], 1)
                        if more:
                            modulated(n + 1, False)
                        act.wait_ge(S["down_done"], n + 1)
                        if not first:
                            act.wait_ge(S["res_stored"], n * 32)
                        for half in range(2):
                            last = act.activation(res[:, half * 512:(half + 1) * 512], res_ps[half][:, :], ACT.Copy)
                        last.then_inc(S["res_ready"], 1)
                        act.wait_ge(S["res_ready"], n + 1)
                        for e in range(2):
                            act.dma_start(k.results[j, m * 2 + e],
                                          res[e * SLOTS:(e + 1) * SLOTS, :]).then_inc(S["res_stored"], 16)
                        if not more:
                            act.wait_ge(S["res_stored"], n * 32 + 32)

                    over_pairs(act, begin, step)

                @block.vector
                def _(dve):
                    def step(m, j, n, first, more):
                        dve.wait_ge(S["sig_ready"], n + 1)
                        dve.tensor_tensor(sig[:], sig[:], up_ps[0][:, 0:F], ALU.mult)
                        dve.drain()
                        dve.wait_ge(S[LAST_UP], n + 1)
                        if not first:
                            dve.wait_ge(S["mid_turned"], n)
                        gate_ps = up_ps[1][:, :] if NU == 2 else up_ps[0][:, F:2 * F]
                        dve.tensor_tensor(mid[:], sig[:], gate_ps, ALU.mult).then_inc(S["mid_ready"], 1)
                        dve.wait_ge(S["mid_turned"], n + 1)
                        if not first:
                            dve.wait_ge(S["down_done"], n)
                        dve.tensor_copy(midT[:].rearrange("p f s -> p (f s)"), mid_ps[:, 0:FC * P]).then_inc(S["midT_ready"], 1)

                    over_pairs(dve, lambda j, n: None, step)

    def add(self, gate, plus, residual):
        k, tag, share = self.k, self.tag, self.share
        with ExitStack() as ctx:
            gain = k.sb(ctx, f"{tag}_gain", [P, D])
            y = [k.sb(ctx, f"{tag}_y{s}", [P, TC, D]) for s in range(2)]
            fetched = [[k.dma_sems[f"fetched{c}{s}"] for s in range(2)] for c in range(TC)]
            here = 16 * (self.nth + 1)
            weighted = k.sem(ctx, f"{tag}_weighted")
            ps = k.banks(ctx, f"{tag}_gain_ps", 2)
            gain_turned = k.sem(ctx, f"{tag}_gain_turned")
            with k.nc.Block() as block:
                @block.gpsimd
                def _(pool):
                    def fetch(results):
                        for c in range(TC):
                            for s in range(2):
                                pool.indirect_dma_start(y[s][:, c, :], None, results,
                                                        bass.IndirectOffsetOnAxis(ap=self.row_of[:, s, c:c + 1], axis=0)).then_inc(fetched[c][s], 16)

                    busiest = pool.value_load(self.most[0:1, 0:1], min_val=0, max_val=SEQ)
                    with pool.If(busiest > SLOTS):
                        fetch(k.results.rearrange("j e s d -> (j e s) d"))
                    with pool.Else():
                        fetch(k.results[0].rearrange("e s d -> (e s) d"))

                @block.tensor
                def _(pe):
                    for j in range(KC):
                        last = pe.transpose(ps[j // 4][:, j % 4 * P:(j % 4 + 1) * P], gate[:, j:j + 1].broadcast_to([P, P]), k.const("ident"))
                    last.then_inc(gain_turned, 1)

                @block.scalar
                def _(act):
                    for c in range(TC):
                        act.wait_ge(fetched[c][0], here)
                        act.activation(y[0][:, c, :], y[0][:, c, :], ACT.Copy, scale=share[:, 0, c:c + 1]).then_inc(weighted, 1)

                @block.vector
                def _(dve):
                    dve.wait_ge(gain_turned, 1)
                    for h in range(2):
                        dve.tensor_scalar(gain[:, h * 512:(h + 1) * 512], ps[h][:, :], float(plus), None, ALU.add)
                    for c in range(TC):
                        dve.wait_ge(fetched[c][1], here)
                        dve.wait_ge(weighted, c + 1)
                        dve.scalar_tensor_tensor(out=y[1][:, c, :], in0=y[1][:, c, :], scalar=share[:, 1, c:c + 1], in1=y[0][:, c, :],
                                                 op0=ALU.mult, op1=ALU.add)
                        dve.drain()
                        dve.tensor_tensor(y[1][:, c, :], y[1][:, c, :], gain[:], ALU.mult)
                        dve.drain()
                        dve.scalar_tensor_tensor(out=k.x[:, c, :], in0=k.x[:, c, :], scalar=float(residual), in1=y[1][:, c, :],
                                                 op0=ALU.mult, op1=ALU.add)


def first_mix_end(k, ohT, onT, mergedT):
    merge_branches(k, ohT, onT, mergedT)
    with ExitStack() as ctx:
        gain = k.sb(ctx, "mix_gain", [P, D])
        broadcast_rows(k, "mix_gb", [(k.mod[:, 2 * KC:3 * KC], gain, 1.0)])
        project_out(k, "mix_out", k.i["w_out"], mergedT, gain, ALPHA)


def affine_norm(k, tag):
    with ExitStack() as ctx:
        g = k.sb(ctx, f"{tag}_gr", [P, D])
        b = k.sb(ctx, f"{tag}_br", [P, D])
        broadcast_rows(k, f"{tag}_bc", [(k.col(f"{tag}_g", 0, 8), g, 0.0), (k.col(f"{tag}_b", 0, 8), b, 0.0)])
        normalize(k, tag, 1e-5, gain=g[:], shift=b[:], out=k.x)


def plus_one(k, out, a, times=None):
    with k.nc.Block() as block:
        @block.vector
        def _(dve):
            if times is None:
                dve.tensor_scalar(out, a, 1.0, None, ALU.add)
            else:
                dve.scalar_tensor_tensor(out=out, in0=a, scalar=1.0, in1=times, op0=ALU.add, op1=ALU.mult)


def first_experts(k):
    with ExitStack() as ctx:
        layer = Experts(k, ctx, "moe1", 0, F1, [k.i["exp_up"], k.i["exp_gate"]], k.i["exp_down"])
        layer.load_first()
        affine_norm(k, "ln1")
        plus_one(k, k.scale1[:], k.mod[:, 4 * KC:5 * KC])
        normalize(k, "ln1h", 1e-5)
        transposed(k, "h2", k.scale1, k.mod[:, 3 * KC:4 * KC])
        route(k, "route1", k.i["w_router"], k.row("router_b"), layer.row_of[:], layer.share[:], layer.most)
        layer.run(k.xn, k.scale1, k.mod[:, 3 * KC:4 * KC])
        layer.add(k.mod[:, 5 * KC:6 * KC], 1.0, ALPHA)
    affine_norm(k, "ln2")


def second_experts(k):
    with ExitStack() as ctx:
        layer = Experts(k, ctx, "moe2", 1, F2, [k.i["exp_in_2"]], k.i["exp_down_2"])
        layer.load_first()
        second_modulated(k, "rms1", k.col("norm_ffn_g_2", 0, 8), k.mod[:, 4 * KC:5 * KC], k.mod[:, 3 * KC:4 * KC])
        route(k, "route2", k.i["w_router_2"], k.row("router_b_2"), layer.row_of[:], layer.share[:], layer.most)
        layer.run(k.xn, k.scale1, k.mod[:, 3 * KC:4 * KC])
        layer.add(k.mod[:, 5 * KC:6 * KC], 0.0, 1.0)


def second_mix(k):
    nc = k.nc
    with ExitStack() as outer:
        catT = k.sb(outer, "mx2_catT", [P, KC, SEQ])
        with ExitStack() as ctx:
            qk = k.sb(ctx, "mx2_qk", [P, 2, HEADS, SEQ])
            v_tok = k.sb(ctx, "mx2_v", [P, TC, 512])
            u = k.sb(ctx, "mx2_u", [P, 4, SEQ])
            project_second(k, qk, v_tok, u)
            pooling(k, u, catT)
            forgetting(k, qk, v_tok, catT)
        gain = k.sb(outer, "mx2_gain", [P, D])
        broadcast_rows(k, "mx2_gb", [(k.mod[:, 2 * KC:3 * KC], gain, 0.0)])
        project_out(k, "mx2_out", k.i["w_out_2"], catT, gain, 1.0)


def project_second(k, qk, v_tok, u):
    nc = k.nc
    NV = 512 + HEADS
    with ExitStack() as ctx:
        w = [k.sb(ctx, f"p2_w{s}", [P, KC, P]) for s in range(2)]
        wv = k.sb(ctx, "p2_wv", [P, KC, NV])
        z = {n: k.sb(ctx, f"p2_{n}", [P, TC, HEADS]) for n in ("f", "low", "mag", "logf")}
        F = k.sb(ctx, "p2_F", [HEADS, SEQ])
        nF = k.sb(ctx, "p2_nF", [HEADS, SEQ])
        ps = k.banks(ctx, "p2_ps", 2)
        psv = k.banks(ctx, "p2_psv", 2)
        psf, = k.banks(ctx, "p2_psf", 1)
        psF, = k.banks(ctx, "p2_psF", 1)
        w_loaded = [k.sem(ctx, f"p2_w_loaded{s}") for s in range(2)]
        names = "wv_loaded projected kept v_projected v_kept f_projected mag_ready exp_ready ln_ready logf_ready summed F_ready cleared rows_set".split()
        S = {n: k.sem(ctx, "p2_" + n) for n in names}
        NCH = 12
        with nc.Block() as block:
            @block.sync
            def _(sp):
                for s in range(2):
                    sp.dma_start(w[s][:], k.i["w_qku_2"][s]).then_inc(w_loaded[s], 16)
                sp.dma_start(wv[:], k.i["w_vf_2"].rearrange("(k p) n -> p k n", p=P)).then_inc(S["wv_loaded"], 16)
                with sp.Fori(1, NCH // 2) as it:
                    for s in range(2):
                        sp.wait_ge(S["projected"], it * 2 + (s - 1))
                        sp.dma_start(w[s][:], k.i["w_qku_2"][it * 2 + s]).then_inc(w_loaded[s], 16)
                sp.wait_ge(S["F_ready"], 2)
                sp.wait_ge(S["kept"], NCH)
                for h in range(HEADS):
                    at = DH2 * (1 - h % 2)
                    ones = k.const("ones")[0:1, :].unsqueeze(1).broadcast_to([1, TC, P])
                    for side, row, other in ((0, F, 1), (1, nF, 0)):
                        sp.dma_start(qk[at + side:at + side + 1, side, h, :], row[h:h + 1, :]).then_inc(S["rows_set"], 16)
                        sp.dma_start(qk[at + other:at + other + 1, side, h, :], ones).then_inc(S["rows_set"], 16)
                sp.wait_ge(S["rows_set"], 16 * 4 * HEADS)

            @block.tensor
            def _(pe):
                def feature_major(it, s, first):
                    pe.wait_ge(w_loaded[s], it * 16 + 16)
                    if not first:
                        pe.wait_ge(S["kept"], it * 2 + (s - 1))
                    for kc in range(KC):
                        last = pe.matmul(ps[s][:, :], w[s][:, kc, :], k.hT[:, kc, :], start=(kc == 0), stop=(kc == KC - 1))
                    last.then_inc(S["projected"], 1)

                for s in range(2):
                    feature_major(0, s, True)
                pe.wait_ge(S["wv_loaded"], 16)
                for c in range(TC):
                    for kc in range(KC):
                        last = pe.matmul(psf[:, c * HEADS:(c + 1) * HEADS], k.hT[:, kc, c * P:(c + 1) * P], wv[:, kc, 512:NV],
                                         start=(kc == 0), stop=(kc == KC - 1))
                last.then_inc(S["f_projected"], 1)
                with pe.Fori(1, NCH // 2) as it:
                    for s in range(2):
                        feature_major(it, s, False)
                pe.wait_ge(S["logf_ready"], 1)
                for c in range(TC):
                    at = BT0 - c * P
                    last = pe.matmul(psF[0:HEADS, :], z["logf"][:, c, :], k.const("upto")[:, at:at + SEQ], start=(c == 0), stop=(c == TC - 1))
                last.then_inc(S["summed"], 1)
                for c in range(TC):
                    if c >= 2:
                        pe.wait_ge(S["v_kept"], c - 1)
                    for kc in range(KC):
                        last = pe.matmul(psv[c % 2][:, :], k.hT[:, kc, c * P:(c + 1) * P], wv[:, kc, 0:512],
                                         start=(kc == 0), stop=(kc == KC - 1))
                    last.then_inc(S["v_projected"], 1)

            @block.scalar
            def _(act):
                act.wait_ge(S["mag_ready"], 1)
                act.activation(z["mag"][:], z["mag"][:], ACT.Exp, scale=-1.0).then_inc(S["exp_ready"], 1)
                act.wait_ge(S["exp_ready"], 1)
                act.activation(z["mag"][:], z["mag"][:], ACT.Ln, bias=1.0).then_inc(S["ln_ready"], 1)
                for c in range(TC):
                    act.wait_ge(S["v_projected"], c + 1)
                    act.activation(v_tok[:, c, :], psv[c % 2][:, :], ACT.Copy).then_inc(S["v_kept"], 1)

            @block.vector
            def _(dve):
                for j in range(NCH):
                    dve.wait_ge(S["projected"], j + 1)
                    if j < 8:
                        side, scale = (0, DH2 ** -0.5) if j < 4 else (1, 1.0)
                        for half in range(2):
                            last = dve.tensor_scalar(qk[:, side, 2 * (j % 4) + half, :], ps[j % 2][:, :],
                                                     k.const("half")[:, half:half + 1], scale, ALU.mult, ALU.mult)
                    else:
                        last = dve.tensor_copy(u[:, j - 8, :], ps[j % 2][:, :])
                    last.then_inc(S["kept"], 1)
                    if j == 1:
                        dve.wait_ge(S["f_projected"], 1)
                        dve.tensor_tensor(z["f"][:], psf[:, 0:TC * HEADS].rearrange("p (c h) -> p c h", h=HEADS),
                                          k.row("b_fgate_2").unsqueeze(1).broadcast_to([P, TC, HEADS]), ALU.add)
                        dve.drain()
                        dve.tensor_scalar(z["low"][:], z["f"][:], -1.0, None, ALU.mult)
                        dve.drain()
                        dve.tensor_tensor(z["mag"][:], z["f"][:], z["low"][:], ALU.max).then_inc(S["mag_ready"], 1)
                        dve.drain()
                        dve.tensor_scalar(z["low"][:], z["f"][:], 0.0, None, ALU.min)
                        dve.drain()
                        dve.wait_ge(S["ln_ready"], 1)
                        dve.tensor_tensor(z["logf"][:], z["low"][:], z["mag"][:], ALU.subtract).then_inc(S["logf_ready"], 1)
                dve.wait_ge(S["summed"], 1)
                dve.tensor_copy(F[:], psF[0:HEADS, :]).then_inc(S["F_ready"], 1)
                dve.tensor_scalar(nF[:], psF[0:HEADS, :], -1.0, None, ALU.mult).then_inc(S["F_ready"], 1)


def pooling(k, u, catT):
    nc = k.nc
    G = len(POOL_WINDOWS)
    with ExitStack() as ctx:
        w = k.sb(ctx, "po_w", [P, G, P])
        sums = k.sb(ctx, "po_sums", [P, G, SEQ])
        diff = k.sb(ctx, "po_diff", [P, G, SEQ])
        ps = k.banks(ctx, "po_ps", G)
        loaded = k.sem(ctx, "po_loaded")
        diff_ready = k.sem(ctx, "po_diff_ready")
        mixed = k.sem(ctx, "po_mixed")
        with nc.Block() as block:
            @block.sync
            def _(sp):
                sp.dma_start(w[:], k.i["w_pool_2"].rearrange("g c d -> c g d")).then_inc(loaded, 16)

            @block.vector
            def _(dve):
                for g in range(G):
                    dve.tensor_tensor_scan(sums[:, g, :], k.const("ones", 0, 1).broadcast_to([P, SEQ]), u[:, g, :], 0.0, ALU.mult, ALU.add)
                dve.drain()
                for g, win in enumerate(POOL_WINDOWS):
                    dve.tensor_copy(diff[:, g, 0:win], sums[:, g, 0:win])
                    dve.tensor_tensor(diff[:, g, win:SEQ], sums[:, g, win:SEQ], sums[:, g, 0:SEQ - win], ALU.subtract)
                dve.drain()
                for g, win in enumerate(POOL_WINDOWS):
                    dve.tensor_tensor(diff[:, g, 0:16], diff[:, g, 0:16], k.const("pool_inv", 16 * g, 16 * g + 16), ALU.mult)
                    dve.tensor_scalar(diff[:, g, 16:SEQ], diff[:, g, 16:SEQ], 1.0 / win, None, ALU.mult)
                dve.drain()
                dve.tensor_tensor(diff[:], diff[:], u[:], ALU.subtract).then_inc(diff_ready, 1)
                for g in range(G):
                    dve.wait_ge(mixed, g + 1)
                    dve.tensor_scalar(catT[:, 4 + g, :], ps[g][:, :], k.col("pool_scale_2", g), None, ALU.mult)

            @block.tensor
            def _(pe):
                pe.wait_ge(loaded, 16)
                pe.wait_ge(diff_ready, 1)
                for g in range(G):
                    pe.matmul(ps[g][:, :], w[:, g, :], diff[:, g, :], start=True, stop=True).then_inc(mixed, 1)


def forgetting(k, qk, v_tok, catT):
    nc = k.nc
    NU = 2 * TC
    with ExitStack() as ctx:
        NP = 4
        qst = k.sb(ctx, "fa_q", [P, 2, SEQ])
        vst = k.sb(ctx, "fa_v", [P, TC, P])
        p = [k.sb(ctx, f"fa_p{s}", [P, SEQ]) for s in range(NP)]
        pT = [k.sb(ctx, f"fa_pT{s}", [P, SEQ]) for s in range(2)]
        top, ntop, total, factor = (k.sb(ctx, f"fa_{n}", [P, NU]) for n in ("top", "ntop", "total", "factor"))
        spare = k.sb(ctx, "fa_spare", [P, 2])
        sc = k.banks(ctx, "fa_sc", 3)
        tr = k.banks(ctx, "fa_tr", 2)
        o_ps, = k.banks(ctx, "fa_o", 1)
        names = "staged scored logits_ready exp_ready p_ready turned pT_ready mixed o_kept".split()
        S = {n: k.sem(ctx, "fa_" + n) for n in names}

        def pairs(eng, body):
            body(0, True)
            with eng.Fori(1, HEADS // 2) as m:
                body(m, False)

        with nc.Block() as block:
            @block.tensor
            def _(pe):
                def scores(m, u, first):
                    c, e = u // 2, u % 2
                    if u == 0:
                        pe.wait_ge(S["staged"], m * 2 + 2)
                    if u >= 3 or not first:
                        pe.wait_ge(S["logits_ready"], m * NU + (u - 2))
                    keys = qk[:, 1, :, :].rearrange("p (m e) s -> p m e s", e=2)[:, :, e, :]
                    pe.matmul(sc[u % 3][:, 0:(c + 1) * P], qst[:, e, c * P:(c + 1) * P], keys[:, m, 0:(c + 1) * P],
                              start=True, stop=True).then_inc(S["scored"], 1)

                def turn(m, u, first):
                    pe.wait_ge(S["p_ready"], m * NU + (u + 1))
                    if u >= 2 or not first:
                        pe.wait_ge(S["pT_ready"], m * NU + (u - 1))
                    for kk in range(u // 2 + 1):
                        last = pe.transpose(tr[u % 2][:, kk * P:(kk + 1) * P], p[u % NP][:, kk * P:(kk + 1) * P], k.const("ident"))
                    last.then_inc(S["turned"], 1)

                def mix(m, u, first):
                    c, e = u // 2, u % 2
                    pe.wait_ge(S["pT_ready"], m * NU + (u + 1))
                    if u == 0 and not first:
                        pe.wait_ge(S["o_kept"], m)
                    for kk in range(c + 1):
                        last = pe.matmul(o_ps[e * DH2:(e + 1) * DH2, c * P:(c + 1) * P], vst[:, kk, e * DH2:(e + 1) * DH2],
                                         pT[u % 2][:, kk * P:(kk + 1) * P], start=(u < 2 and kk == 0), stop=False, skip_group_check=True)
                    last.then_inc(S["mixed"], 1)

                def body(m, first):
                    for u in range(3):
                        scores(m, u, first)
                    for u in range(NU):
                        turn(m, u, first)
                        if u + 3 < NU:
                            scores(m, u + 3, first)
                        if u:
                            mix(m, u - 1, first)
                    mix(m, NU - 1, first)

                pairs(pe, body)

            @block.scalar
            def _(act):
                def weights(m, u):
                    n = (u // 2 + 1) * P
                    act.wait_ge(S["logits_ready"], m * NU + (u + 1))
                    act.activation(p[u % NP][:, 0:n], p[u % NP][:, 0:n], ACT.Exp, bias=ntop[:, u:u + 1],
                                   accum_out=total[:, u:u + 1]).then_inc(S["exp_ready"], 1)

                def keep_turned(m, u, first):
                    n = (u // 2 + 1) * P
                    act.wait_ge(S["turned"], m * NU + (u + 1))
                    if u >= 2 or not first:
                        act.wait_ge(S["mixed"], m * NU + (u - 1))
                    act.activation(pT[u % 2][:, 0:n], tr[u % 2][:, 0:n], ACT.Copy).then_inc(S["pT_ready"], 1)

                def body(m, first):
                    for u in range(NU + 2):
                        if u < NU:
                            weights(m, u)
                        if u >= 2:
                            keep_turned(m, u - 2, first)

                pairs(act, body)

            @block.vector
            def _(dve):
                def logits(m, u, first):
                    n = (u // 2 + 1) * P
                    dve.wait_ge(S["scored"], m * NU + (u + 1))
                    if u >= NP or not first:
                        dve.wait_ge(S["turned"], m * NU + (u - NP + 1 if u >= NP else 0))
                    dve.memset(spare[:, 0:1], 0.0)
                    dve.tensor_tensor_reduce(p[u % NP][:, 0:n], sc[u % 3][:, 0:n], k.const("causal2", SEQ - n, SEQ), 1.0, NEG * 10,
                                             ALU.add, ALU.max, top[:, u:u + 1])
                    dve.drain()
                    dve.tensor_scalar(ntop[:, u:u + 1], top[:, u:u + 1], -1.0, None, ALU.mult).then_inc(S["logits_ready"], 1)

                def normalized(m, u):
                    n = (u // 2 + 1) * P
                    dve.wait_ge(S["exp_ready"], m * NU + (u + 1))
                    dve.reciprocal(factor[:, u:u + 1], total[:, u:u + 1])
                    dve.drain()
                    dve.tensor_scalar(p[u % NP][:, 0:n], p[u % NP][:, 0:n], factor[:, u:u + 1], None, ALU.mult).then_inc(S["p_ready"], 1)

                def body(m, first):
                    for u in range(NU + 1):
                        if u < NU:
                            logits(m, u, first)
                        if u:
                            normalized(m, u - 1)
                    dve.wait_ge(S["mixed"], m * NU + NU)
                    dve.tensor_copy(catT[:, m, :], o_ps[:, :]).then_inc(S["o_kept"], 1)

                pairs(dve, body)

            @block.gpsimd
            def _(pool):
                def stage(m, first):
                    if not first:
                        pool.wait_ge(S["mixed"], m * NU)
                        pool.tensor_tensor(spare[:, 1:2], k.const("ones", 0, 1), k.const("ones", 0, 1), ALU.add)
                    queries = qk[:, 0, :, :].rearrange("p (m e) s -> p m e s", e=2)
                    pool.tensor_copy(qst[:], queries[:, m, :, :]).then_inc(S["staged"], 1)
                    pool.tensor_copy(vst[:], v_tok[:].rearrange("p c (m e) -> p c m e", e=P)[:, :, m, :]).then_inc(S["staged"], 1)

                pairs(pool, stage)


def second_modulated(k, tag, gain, scale, shift):
    plus_one(k, k.scale1[:], scale, times=gain)
    normalize(k, tag, 1e-6, root_mean_square=True)
    transposed(k, f"{tag}T", k.scale1, shift)


def program(nc, inputs, out):
    with ExitStack() as ctx:
        k = Kit(nc, inputs, out)
        persistent(k, ctx)
        load_constants(k)

        modulation(k, "mod1", inputs["ada_w"], k.col("c", 0, 8), k.col("ada_b", 0, 48), k.mod)
        plus_one(k, k.scale1[:], k.mod[:, KC:2 * KC])
        normalize(k, "ln0", 1e-5)
        transposed(k, "h1", k.scale1, k.mod[:, 0:KC])
        with ExitStack() as mix:
            ohT = k.sb(mix, "ohT", [P, KC, SEQ])
            recurrence(k, ohT)
            onT = k.sb(mix, "onT", [P, KC, SEQ])
            sparse_attention(k, onT)
            mergedT = k.sb(mix, "mergedT", [P, KC, SEQ])
            first_mix_end(k, ohT, onT, mergedT)
        first_experts(k)

        modulation(k, "mod2", inputs["ada_w_2"], k.col("c_2", 0, 8), k.col("b_ada_2", 0, 48), k.mod)
        second_modulated(k, "rms0", k.col("norm_mix_g_2", 0, 8), k.mod[:, KC:2 * KC], k.mod[:, 0:KC])
        second_mix(k)
        second_experts(k)
        with ExitStack() as fin:
            g = k.sb(fin, "final_g", [P, D])
            broadcast_rows(k, "final_gb", [(k.col("norm_final_g_2", 0, 8), g, 0.0)])
            normalize(k, "final", 1e-6, root_mean_square=True, gain=g[:], out=k.x)
        with ExitStack() as end:
            stored = k.sem(end, "out_stored")
            with nc.Block() as block:
                @block.sync
                def _(sp):
                    sp.dma_start(out.rearrange("(c p) d -> p c d", p=P), k.x[:]).then_inc(stored, 16)
                    sp.wait_ge(stored, 16)


def _columns(v):
    return np.asarray(v, np.float32).reshape(-1, P).T


def arrange(x, c, ada_w, ada_b, w_in, b_in, hg_lb_logits, hg_norm_w, cmp_pos_k, cmp_w1_k, cmp_b1_k, cmp_w2_k,
            cmp_pos_v, cmp_w1_v, cmp_b1_v, cmp_w2_v, rel_bias, w_br_hg, w_br_nsa, w_out, ln1_g, ln1_b,
            router_grp_w, router_grp_b, router_exp_w, router_exp_b, exp_w1, exp_w3, exp_w2, ln2_g, ln2_b,
            c_2, norm_mix_g_2, norm_ffn_g_2, norm_final_g_2, w_ada_2, b_ada_2, w_in_2, b_fgate_2, w_pool_2,
            pool_scale_2, w_out_2, w_router_group_2, b_router_group_2, w_router_expert_2, b_router_expert_2,
            w_expert_gate_2, w_expert_up_2, w_expert_down_2):
    f = lambda a: np.ascontiguousarray(np.asarray(a))
    w_in, b_in = f(w_in)[0], f(b_in)[0]
    at = dict(hq=0, hf=1024, hv=2048, hg=3072, nq=4096, kc=5120, vc=5376, ks=5632, vs=5888, kw=6144, vw=6400,
              gate=6656, mgh=6680, mgn=7704)

    def chunks(w, a, n):
        return w[:, a:a + n * P].reshape(KC, P, n, P).transpose(2, 1, 0, 3)

    vectors = dict(
        c=c, ada_b=ada_b, b_in=b_in[:at["gate"]], b_mg=b_in[at["mgh"]:], lb0=f(hg_lb_logits)[0],
        lb1=f(hg_lb_logits)[1], hg_norm_w=hg_norm_w, cmp_b1_k=cmp_b1_k, cmp_b1_v=cmp_b1_v, cmp_pos_k=cmp_pos_k,
        cmp_pos_v=cmp_pos_v, ln1_g=ln1_g, ln1_b=ln1_b, ln2_g=ln2_g, ln2_b=ln2_b, c_2=c_2, b_ada_2=b_ada_2,
        norm_mix_g_2=norm_mix_g_2, norm_ffn_g_2=norm_ffn_g_2, norm_final_g_2=norm_final_g_2,
        pool_scale_2=pool_scale_2)
    short = dict(b_gate=[b_in[at["gate"]:at["mgh"]]], router_b=[router_grp_b, router_exp_b],
                 router_b_2=[b_router_group_2, b_router_expert_2], b_fgate_2=[b_fgate_2])
    w2 = f(w_in_2)[0]
    out = dict(
        consts=np.concatenate([a for _, a in pack_consts()], 1),
        cols=np.concatenate([_columns(vectors[n]) for n, _ in pack_columns()], 1),
        rows=np.concatenate([f(v).reshape(-1) for n, _ in pack_rows() for v in short[n]]),
        buckets=bucket_rows(),
        x=f(x)[0], ada_w=f(ada_w)[0],
        w_hg=np.stack([chunks(w_in, at[n], 8) for n in ("hq", "hf", "hg", "hv")], 1),
        w_nq=chunks(w_in, at["nq"], 8),
        w_kv=np.concatenate([chunks(w_in, at[n], 2) for n in ("kc", "vc", "ks", "kw")]),
        w_v=np.concatenate([w_in[:, at["vs"]:at["vs"] + 256], w_in[:, at["vw"]:at["vw"] + 256],
                            w_in[:, at["gate"]:at["mgh"]]], 1),
        w_cmp=np.stack([f(cmp_w1_k)[0], f(cmp_w1_v)[0]]), w_cmp2=np.stack([f(cmp_w2_k)[0], f(cmp_w2_v)[0]]),
        rel_bias=f(rel_bias).T,
        w_merge=np.stack([chunks(w_in, at["mgh"], 8), chunks(w_in, at["mgn"], 8), chunks(f(w_br_hg)[0], 0, 8),
                          chunks(f(w_br_nsa)[0], 0, 8)], 1),
        w_out=f(w_out)[0],
        w_router=np.concatenate([f(router_grp_w)[0], f(router_exp_w)[0]], 1),
        exp_up=f(exp_w1)[0], exp_gate=f(exp_w3)[0], exp_down=f(exp_w2)[0],
        ada_w_2=f(w_ada_2)[0],
        w_qku_2=np.concatenate([chunks(w2, 0, 8), chunks(w2, 1544, 4)]),
        w_vf_2=w2[:, 1024:1544],
        w_pool_2=f(w_pool_2)[0], w_out_2=f(w_out_2)[0],
        w_router_2=np.concatenate([f(w_router_group_2)[0], f(w_router_expert_2)[0].transpose(1, 0, 2).reshape(D, N_EXP)], 1),
        exp_in_2=np.concatenate([f(w_expert_gate_2)[0].reshape(N_EXP, D, F2), f(w_expert_up_2)[0].reshape(N_EXP, D, F2)], 2),
        exp_down_2=f(w_expert_down_2)[0].reshape(N_EXP, F2, D),
    )
    return {n: np.ascontiguousarray(a) for n, a in out.items()}


def kernel(**inputs):
    from concourse import bacc
    from concourse.bass_utils import run_bass_kernel_spmd

    arrays = {f"in_{n}": a for n, a in arrange(**inputs).items()}
    nc = bacc.Bacc("TRN2", target_bir_lowering=False, num_devices=1)
    views = {n[3:]: nc.dram_tensor(n, a.shape, mybir.dt.from_np(a.dtype), kind="ExternalInput").ap() for n, a in arrays.items()}
    out = nc.dram_tensor("out_x", (SEQ, D), F32, kind="ExternalOutput").ap()
    program(nc, views, out)
    r = run_bass_kernel_spmd(nc, [arrays], core_ids=[0])
    return r.results[0]["out_x"].reshape(1, SEQ, D)
```

```python
from contextlib import ExitStack

import concourse.bass as bass
import numpy as np
from concourse import mybir

F32 = mybir.dt.float32
I32 = mybir.dt.int32
U32 = mybir.dt.uint32
ALU = mybir.AluOpType
ACT = mybir.ActivationFunctionType
AX = mybir.AxisListType

P = 128
SEQ = 512
D = 1024
TC = SEQ // P
KC = D // P
HEADS = 8

HG_CHUNK = 32
N_CHUNK = SEQ // HG_CHUNK
QC = P // HG_CHUNK
GROUPS = 2
REP = HEADS // GROUPS
CMP_BLOCK = 32
CMP_STRIDE = 16
N_CMP = SEQ // CMP_STRIDE - 1
BUCKETS = 32
MAX_DIST = 128
ALPHA = 2 ** 0.25
ATT_SCALE = P ** -0.5
NEG = -1e30

N_GRP = 4
PER_GRP = 8
N_EXP = N_GRP * PER_GRP
SLOTS = 64
PASSES = SEQ // SLOTS
PAIRS = N_EXP // 2
F1 = 512
F2 = 256

DH2 = 64
POOL_WINDOWS = (2, 4, 8, 16)

BT0 = SEQ - P
BTW = BT0 + SEQ
BT_ROW = 1024


def pack_columns():
    return [("c", 8), ("ada_b", 48), ("b_in", 52), ("b_mg", 16), ("lb0", 8), ("lb1", 8), ("hg_norm_w", 8),
            ("cmp_b1_k", 1), ("cmp_b1_v", 1), 
            ("ln1_g", 8), ("ln1_b", 8), ("ln2_g", 8), ("ln2_b", 8),
            ("c_2", 8), ("b_ada_2", 48), ("norm_mix_g_2", 8), ("norm_ffn_g_2", 8), ("norm_final_g_2", 8),
            ("pool_scale_2", 4)]


def pack_rows():
    return [("b_gate", 24), ("router_b", 36), ("router_b_2", 36), ("b_fgate_2", 8)]


def pack_consts():
    p = np.arange(P)[:, None]
    j = np.arange(P)[None, :]
    w = np.arange(BTW)[None, :]
    ident = (p == j)
    before = (p < j)
    ones = np.ones((P, P))
    hg_causal = (p // HG_CHUNK == j // HG_CHUNK) & (p <= j)
    chunk_of = (p // HG_CHUNK == np.arange(QC)[None, :])
    every32 = (p % 32 == 0)
    half = (p // DH2 == np.arange(2)[None, :])
    chunk_cont = np.broadcast_to((np.arange(SEQ) % HG_CHUNK != 0)[None, :], (P, SEQ))
    upto = (p <= w - BT0)
    causal2 = np.where(w[:, :SEQ] - BT0 > p, NEG, 0.0)
    inv = np.array([[1.0 / min(t + 1, k) for t in range(16)] for k in POOL_WINDOWS]).reshape(1, -1)
    pool_inv = np.broadcast_to(inv, (P, inv.size))
    first = np.broadcast_to(np.arange(N_EXP, 0, -1)[None, :], (P, N_EXP))
    t = (np.arange(TC)[None, :, None] * P + p[:, :, None])
    cmp_ok = (t - (np.arange(N_CMP) * CMP_STRIDE + CMP_BLOCK - 1)[None, None, :] >= 0).reshape(P, -1)
    return [(n, np.asarray(a, np.float32)) for n, a in (
        ("ident", ident), ("before", before), ("ones", ones), ("hg_causal", hg_causal), ("chunk_of", chunk_of),
        ("half", half), ("chunk_cont", chunk_cont), ("upto", upto), ("causal2", causal2),
        ("pool_inv", pool_inv), ("first", first), ("cmp_ok", cmp_ok), ("every32", every32),
        ("expert_row", np.broadcast_to(np.arange(N_EXP)[None, :] * SLOTS, (P, N_EXP))),
        ("pass_start", np.broadcast_to(np.arange(1, PASSES)[None, :] * SLOTS, (P, PASSES - 1))))]


def bucket_rows():
    import math
    dist = SEQ - 1 - np.arange(BT_ROW)
    n = np.maximum(dist, 0)
    half = BUCKETS // 2
    nf = np.maximum(n, 1).astype(np.float32)
    large = half + (np.log(nf / np.float32(half)) / np.float32(math.log(MAX_DIST / half)) * np.float32(BUCKETS - half)).astype(np.int32)
    b = np.where(n < half, n, np.minimum(large, BUCKETS - 1))
    out = np.zeros((BUCKETS + 1, BT_ROW), np.float32)
    out[b, np.arange(BT_ROW)] = dist >= 0
    out[BUCKETS] = dist < 0
    return out


def offsets(spec):
    at, out = 0, {}
    for name, n in spec:
        out[name] = (at, n)
        at += n
    return out, at


class Kit:

    def __init__(self, nc, inputs, out):
        self.nc, self.i, self.out = nc, inputs, out
        self.owned, self.zeroed = [], []
        self.col_at, self.n_cols = offsets(pack_columns())
        self.row_at, self.n_rows = offsets(pack_rows())
        self.const_at, self.n_consts = offsets([(n, a.shape[1]) for n, a in pack_consts()])

    def sb(self, ctx, name, shape, dt=F32):
        return ctx.enter_context(self.nc.sbuf_tensor(name, shape, dt))

    def banks(self, ctx, name, n):
        return [ctx.enter_context(self.nc.psum_tensor(f"{name}{j}", [P, 512], F32)) for j in range(n)]

    def sem(self, ctx, name):
        if not any(owner is ctx for owner, _ in self.owned):
            self.owned.append((ctx, []))
            ctx.callback(self.stage_over, ctx)
        handle = self.nc.alloc_semaphore(name=name)
        next(sems for owner, sems in self.owned if owner is ctx).append(handle)
        return handle

    def stage_over(self, ctx):
        mine = next(pair for pair in self.owned if pair[0] is ctx)
        self.owned.remove(mine)
        for s in self.zeroed:
            self.nc.release_semaphore(s)
        numbers = sorted(s.num for s in mine[1])
        start = numbers[0]
        for a, b in zip(numbers, numbers[1:] + [None]):
            if b != a + 1:
                self.nc.gpsimd.sem_clear(range(start, a + 1))
                start = b
        self.zeroed = mine[1]

    def col(self, name, j=0, n=1):
        a = self.col_at[name][0] + j
        return self.cols[:, a:a + n]

    def row(self, name):
        a, n = self.row_at[name]
        return self.rows[:, a:a + n]

    def const(self, name, a=0, b=None):
        at, n = self.const_at[name]
        return self.consts[:, at + a:at + (n if b is None else b)]


def load_constants(k, modulation):
    nc = k.nc
    with ExitStack() as ctx:
        loaded = k.sem(ctx, "const_loaded")
        with nc.Block() as block:
            @block.sync
            def _(sp):
                sp.dma_start(k.consts[:], k.i["consts"]).then_inc(loaded, 16)
                sp.dma_start(k.cols[:], k.i["cols"]).then_inc(loaded, 16)
                sp.dma_start(k.rows[:], k.i["rows"].partition_broadcast(P)).then_inc(loaded, 16)
                sp.dma_start(k.x[:], k.i["x"].rearrange("(c p) d -> p c d", p=P)).then_inc(loaded, 16)
                for w, name in ((k.w_router, "w_router"), (k.w_router_2, "w_router_2")):
                    sp.dma_start(w[:], k.i[name].rearrange("(k p) n -> p k n", p=P)).then_inc(loaded, 16)
                modulation.load_first(sp)
                sp.wait_ge(loaded, 96)


class Modulation:

    NBUF, BLK, QUARTER = 6, 512, 32
    BLOCKS = 6 * D // BLK

    def __init__(self, k, ctx, tag, weights):
        self.k, self.tag = k, tag
        self.w_v = weights
        self.buf = [k.sb(ctx, f"{tag}_w{r}", [P, KC, self.BLK]) for r in range(self.NBUF)]
        self.w_loaded = [k.sem(ctx, f"{tag}_w_loaded{r}") for r in range(self.NBUF)]

    def load(self, sp, b):
        r = b % self.NBUF
        sp.dma_start(self.buf[r][:], self.w_v[b]).then_inc(self.w_loaded[r], 16)

    def load_first(self, sp):
        for b in range(self.NBUF):
            self.load(sp, b)

    def run(self, act, bias, mod, gains=(None, None)):
        k, tag, buf, w_loaded, NBUF, BLK, QUARTER, blocks = (
            self.k, self.tag, self.buf, self.w_loaded, self.NBUF, self.BLK, self.QUARTER, self.BLOCKS)
        per = BLK // P
        with ExitStack() as ctx:
            rows = [k.sb(ctx, f"{tag}_rows{r}", [P, BLK]) for r in range(2)]
            sig = k.sb(ctx, f"{tag}_sig", [P, KC])
            c_act = k.sb(ctx, f"{tag}_cact", [P, KC])
            c_wide = k.sb(ctx, f"{tag}_cwide", [P, KC, QUARTER])
            ps = k.banks(ctx, f"{tag}_ps", 2)
            mod_ps, = k.banks(ctx, f"{tag}_mod_ps", 1)
            w_used = k.sem(ctx, f"{tag}_w_used")
            sig_ready = k.sem(ctx, f"{tag}_sig_ready")
            act_ready = k.sem(ctx, f"{tag}_act_ready")
            rows_kept = k.sem(ctx, f"{tag}_rows_kept")
            folded = k.sem(ctx, f"{tag}_folded")

            with k.nc.Block() as block:
                @block.sync
                def _(sp):
                    for b in range(NBUF, blocks):
                        sp.wait_ge(w_used, b - NBUF + 1)
                        self.load(sp, b)

                @block.tensor
                def _(pe):
                    def fold(b):
                        pe.wait_ge(rows_kept, b + 1)
                        for j in range(per):
                            last = pe.matmul(mod_ps[:, b * per + j:b * per + j + 1], rows[b % 2][:, j * P:(j + 1) * P],
                                             k.const("every32"), start=True, stop=True, skip_group_check=True)
                        last.then_inc(folded, 1)

                    pe.wait_ge(act_ready, 2)
                    for b in range(blocks):
                        pe.wait_ge(w_loaded[b % NBUF], b // NBUF * 16 + 16)
                        if b >= 2:
                            pe.wait_ge(rows_kept, b - 1)
                        for kc in range(KC):
                            q = kc % 4 * QUARTER
                            last = pe.matmul(ps[b % 2][q:q + QUARTER, :], c_wide[:, kc, :], buf[b % NBUF][:, kc, :],
                                             start=(kc < 4), stop=(kc >= 4), skip_group_check=True)
                        last.then_inc(w_used, 1)
                        if b:
                            fold(b - 1)
                    fold(blocks - 1)

                @block.scalar
                def _(act_e):
                    act_e.activation(sig[:], act, ACT.Sigmoid).then_inc(sig_ready, 1)
                    for b in range(blocks):
                        act_e.wait_ge(w_used, b + 1)
                        if b >= 2:
                            act_e.wait_ge(folded, b - 1)
                        act_e.activation(rows[b % 2][:], ps[b % 2][:, :], ACT.Copy).then_inc(rows_kept, 1)

                @block.vector
                def _(dve):
                    dve.wait_ge(sig_ready, 1)
                    dve.tensor_tensor(c_act[:], act, sig[:], ALU.mult).then_inc(act_ready, 1)
                    dve.drain()
                    dve.tensor_copy(c_wide[:], c_act[:].unsqueeze(2).broadcast_to([P, KC, QUARTER])).then_inc(act_ready, 1)
                    dve.wait_ge(folded, blocks)
                    dve.tensor_tensor(mod[:], mod_ps[:, 0:blocks * per], bias, ALU.add)
                    dve.drain()
                    for out, part, gain in ((k.scale_mix, 1, gains[0]), (k.scale_ffn, 4, gains[1])):
                        scale = mod[:, part * KC:(part + 1) * KC]
                        if gain is None:
                            dve.tensor_scalar(out[:], scale, 1.0, None, ALU.add)
                        else:
                            dve.scalar_tensor_tensor(out=out[:], in0=scale, scalar=1.0, in1=gain, op0=ALU.add, op1=ALU.mult)


def normalize(k, tag, eps, root_mean_square=False, gain=None, shift=None, out=None, store=None):
    nc = k.nc
    out = k.xn if out is None else out
    with ExitStack() as ctx:
        stats = k.sb(ctx, f"{tag}_stats", [P, TC, 2, 6])
        mv = k.sb(ctx, f"{tag}_mv", [P, TC, 2])
        var = k.sb(ctx, f"{tag}_var", [P, TC])
        dev = k.sb(ctx, f"{tag}_dev", [P, TC])
        rstd = k.sb(ctx, f"{tag}_rstd", [P, TC])
        along = [(cols, k.sb(ctx, f"{tag}_along{n}", [P, D])) for n, cols in enumerate((gain, shift)) if cols is not None]
        gain, shift = ([row[:] for _, row in along] + [None, None])[:2]
        ps = k.banks(ctx, f"{tag}_ps", 2 * len(along))
        turned = k.sem(ctx, f"{tag}_turned")
        rows_ready = k.sem(ctx, f"{tag}_rows_ready")
        var_ready = k.sem(ctx, f"{tag}_var_ready")
        dev_ready = k.sem(ctx, f"{tag}_dev_ready")
        scaled = k.sem(ctx, f"{tag}_scaled")
        gained = k.sem(ctx, f"{tag}_gained")
        pool_gained = k.sem(ctx, f"{tag}_pool_gained")
        stored = k.sem(ctx, f"{tag}_stored")
        with nc.Block() as block:
            @block.sync
            def _(sp):
                if store is not None:
                    for c, ready, n in ((1, gained, 1), (0, pool_gained, 1), (2, gained, 2), (3, gained, 3)):
                        sp.wait_ge(ready, n)
                        sp.dma_start(store.rearrange("(c p) d -> p c d", p=P)[:, c, :], out[:, c, :]).then_inc(stored, 16)
                    sp.wait_ge(stored, 16 * TC)

            @block.vector
            def _(dve):
                for c in range(TC):
                    for h in range(2):
                        dve.bn_stats(stats[:, c, h, :], k.x[:, c, h * 512:(h + 1) * 512])
                dve.drain()
                for c in range(TC):
                    dve.bn_aggr(mv[:, c, :], stats[:, c, :, :])
                dve.drain()
                if root_mean_square:
                    dve.tensor_tensor(var[:], mv[:, :, 0], mv[:, :, 0], ALU.mult)
                    dve.drain()
                    dve.tensor_tensor(var[:], var[:], mv[:, :, 1], ALU.add)
                    dve.drain()
                    dve.tensor_scalar(var[:], var[:], eps, None, ALU.add).then_inc(var_ready, 1)
                else:
                    dve.tensor_scalar(var[:], mv[:, :, 1], eps, None, ALU.add).then_inc(var_ready, 1)
                dve.wait_ge(dev_ready, 1)
                dve.reciprocal(rstd[:], dev[:])
                dve.drain()
                for c in range(TC):
                    if root_mean_square:
                        dve.tensor_scalar(out[:, c, :], k.x[:, c, :], rstd[:, c:c + 1], None, ALU.mult).then_inc(scaled, 1)
                    else:
                        dve.tensor_scalar(out[:, c, :], k.x[:, c, :], mv[:, c, 0:1], rstd[:, c:c + 1],
                                          ALU.subtract, ALU.mult).then_inc(scaled, 1)
                if gain is not None:
                    dve.wait_ge(rows_ready, len(along))
                    for c in range(1, TC):
                        dve.wait_ge(scaled, c + 1)
                        dve.tensor_tensor(out[:, c, :], out[:, c, :], gain, ALU.mult).then_inc(gained, 1)
                    dve.drain()
                    if shift is not None:
                        for c in range(1, TC):
                            dve.tensor_tensor(out[:, c, :], out[:, c, :], shift, ALU.add)

            @block.tensor
            def _(pe):
                for n, (cols, _) in enumerate(along):
                    for j in range(KC):
                        last = pe.transpose(ps[2 * n + j // 4][:, j % 4 * P:(j % 4 + 1) * P], cols[:, j:j + 1].broadcast_to([P, P]),
                                            k.const("ident"))
                    last.then_inc(turned, 1)

            @block.scalar
            def _(act):
                for n, (_, row) in enumerate(along):
                    act.wait_ge(turned, n + 1)
                    for h in range(2):
                        last = act.activation(row[:, h * 512:(h + 1) * 512], ps[2 * n + h][:, :], ACT.Copy)
                    last.then_inc(rows_ready, 1)
                act.wait_ge(var_ready, 1)
                act.activation(dev[:], var[:], ACT.Sqrt).then_inc(dev_ready, 1)

            @block.gpsimd
            def _(pool):
                if gain is not None:
                    pool.wait_ge(rows_ready, len(along))
                    pool.wait_ge(scaled, 1)
                    pool.tensor_tensor(out[:, 0, :], out[:, 0, :], gain, ALU.mult).then_inc(pool_gained, 1)
                    if shift is not None:
                        pool.wait_ge(pool_gained, 1)
                        pool.tensor_tensor(out[:, 0, :], out[:, 0, :], shift, ALU.add)


def transposed(k, tag, scale, shift, send_next=None):
    nc = k.nc
    with ExitStack() as ctx:
        ps = k.banks(ctx, f"{tag}_ps", 2)
        turned = k.sem(ctx, f"{tag}_turned")
        kept = k.sem(ctx, f"{tag}_kept")
        with nc.Block() as block:
            @block.sync
            def _(sp):
                if send_next:
                    send_next(sp)

            @block.tensor
            def _(pe):
                for kc in range(KC):
                    if kc >= 2:
                        pe.wait_ge(kept, kc - 1)
                    for c in range(TC):
                        last = pe.transpose(ps[kc % 2][:, c * P:(c + 1) * P], k.xn[:, c, kc * P:(kc + 1) * P],
                                            k.const("ident"))
                    last.then_inc(turned, 1)

            @block.scalar
            def _(act):
                for kc in range(KC):
                    act.wait_ge(turned, kc + 1)
                    act.activation(k.hT[:, kc, :], ps[kc % 2][:, :], ACT.Identity, scale=scale[:, kc:kc + 1],
                                   bias=shift[:, kc:kc + 1]).then_inc(kept, 1)


class SlicesAhead:

    def __init__(self, k, ctx, tag, count, source, inside=None):
        if inside is None:
            self.w = [k.sb(ctx, f"{tag}_w{n}", [P, KC, P])[:] for n in range(count)]
        else:
            self.w = [inside[:, n, :].rearrange("p (k j) -> p k j", j=P) for n in range(count)]
        self.loaded = [k.sem(ctx, f"{tag}_loaded{n}") for n in range(count)]
        self.source = source

    def send(self, sp):
        for n, w in enumerate(self.w):
            sp.dma_start(w, self.source(n)).then_inc(self.loaded[n], 16)


def broadcast_rows(k, tag, jobs):
    nc = k.nc
    with ExitStack() as ctx:
        ps = k.banks(ctx, f"{tag}_ps", 2)
        turned = k.sem(ctx, f"{tag}_turned")
        kept = k.sem(ctx, f"{tag}_kept")
        steps = [(cols, out, plus, j) for cols, out, plus in jobs for j in range(0, cols.shape[1], 4)]
        with nc.Block() as block:
            @block.tensor
            def _(pe):
                for n, (cols, out, plus, j) in enumerate(steps):
                    if n >= 2:
                        pe.wait_ge(kept, n - 1)
                    for q in range(min(4, cols.shape[1] - j)):
                        last = pe.transpose(ps[n % 2][:, q * P:(q + 1) * P],
                                            cols[:, j + q:j + q + 1].broadcast_to([P, P]), k.const("ident"))
                    last.then_inc(turned, 1)

            @block.vector
            def _(dve):
                for n, (cols, out, plus, j) in enumerate(steps):
                    dve.wait_ge(turned, n + 1)
                    width = min(4, cols.shape[1] - j) * P
                    dve.tensor_scalar(out[:, j * P:j * P + width], ps[n % 2][:, 0:width], float(plus), None,
                                      ALU.add).then_inc(kept, 1)


def persistent(k, ctx):
    k.consts = k.sb(ctx, "consts", [P, k.n_consts])
    k.cols = k.sb(ctx, "cols", [P, k.n_cols])
    k.rows = k.sb(ctx, "rows", [P, k.n_rows])
    k.x = k.sb(ctx, "x", [P, TC, D])
    k.xn = k.sb(ctx, "xn", [P, TC, D])
    k.hT = k.sb(ctx, "hT", [P, KC, SEQ])
    k.mod = k.sb(ctx, "mod", [P, 6 * KC])
    k.w_router = k.sb(ctx, "w_router_sb", [P, KC, N_GRP + N_EXP])
    k.w_router_2 = k.sb(ctx, "w_router_2_sb", [P, KC, N_GRP + N_EXP])
    names = ["zeroed", "moe1_zeroed", "moe2_zeroed", "sent"] + [f"fetched{c}{s}" for c in range(TC) for s in range(2)]
    k.dma_sems = {n: k.sem(ctx, f"all_{n}") for n in names}
    k.sent = k.nc.dram_tensor("sent", (PASSES, N_EXP, SLOTS, D), F32, kind="Internal").ap()
    k.results = k.nc.dram_tensor("results", (PASSES, N_EXP, SLOTS, D), F32, kind="Internal").ap()
    k.scale_mix = k.sb(ctx, "scale_mix", [P, KC])
    k.scale_ffn = k.sb(ctx, "scale_ffn", [P, KC])


def recurrence(k, gate, squares, first_slices, send_next):
    nc = k.nc
    w_hg = k.i["w_hg"]
    raw = k.xn[:].rearrange("p c (h e) -> p c h e", e=P)
    with ExitStack() as ctx:
        w = first_slices.w
        q = k.sb(ctx, "hg_q", [P, SEQ])
        sigf = k.sb(ctx, "hg_sigf", [P, SEQ])
        fg = k.sb(ctx, "hg_fg", [P, SEQ])
        key = k.sb(ctx, "hg_key", [P, SEQ])
        logf = k.sb(ctx, "hg_logf", [P, SEQ])
        b = k.sb(ctx, "hg_b", [P, SEQ])
        left = k.sb(ctx, "hg_left", [P, SEQ])
        eb = k.sb(ctx, "hg_eb", [P, SEQ])
        enb = k.sb(ctx, "hg_enb", [P, SEQ])
        eleft = k.sb(ctx, "hg_eleft", [P, SEQ])
        q_in = k.sb(ctx, "hg_q_in", [P, SEQ])
        k_in = k.sb(ctx, "hg_k_in", [P, SEQ])
        k_end = k.sb(ctx, "hg_k_end", [P, SEQ])
        k_tok = k.sb(ctx, "hg_k_tok", [P, TC, P])
        v_tok = k.sb(ctx, "hg_v_tok", [P, TC, P])
        v_parts = k.sb(ctx, "hg_v_parts", [P, TC, QC, P])
        att = k.sb(ctx, "hg_att", [P, TC, P])
        state = k.sb(ctx, "hg_state", [P, N_CHUNK, P])
        junk = k.sb(ctx, "hg_junk", [P, TC, P])
        one_lb = k.sb(ctx, "hg_one_lb", [P, HEADS])
        lb, v_bias = k.lb, k.hg_v_bias

        proj = k.banks(ctx, "hg_proj", 2)
        upd = k.banks(ctx, "hg_upd", 4)
        tr_out, = k.banks(ctx, "hg_tr_out", 1)
        score, = k.banks(ctx, "hg_score", 1)

        names = ("used_q used_f used_g used_v "
                 "q_kept f_kept g_kept v_kept fg_ready key_ready logf_ready b_ready left_ready eb_ready enb_ready eleft_ready "
                 "qin_ready kin_ready kend_ready keys_turned ktok_kept scores_done att_ready "
                 "v_parts_ready updates_done chain_done outputs_done raw_kept").split()
        S = {n: k.sem(ctx, "hg_" + n) for n in names}
        slices = "qfgv"
        S.update({"loaded_" + a: first_slices.loaded[s] for s, a in enumerate(slices)})

        with nc.Block() as block:
            @block.sync
            def _(sp):
                with sp.Fori(1, HEADS) as n:
                    for s, a in enumerate(slices):
                        sp.wait_ge(S["used_" + a], n)
                        sp.dma_start(w[s], w_hg[n, s]).then_inc(S["loaded_" + a], 16)
                send_next(sp)

            @block.tensor
            def _(pe):
                def feature_major(s, a, bank, n):
                    pe.wait_ge(S["loaded_" + a], n * 16 + 16)
                    for kc in range(KC):
                        last = pe.matmul(proj[bank][:, :], w[s][:, kc, :], k.hT[:, kc, :],
                                         start=(kc == 0), stop=(kc == KC - 1))
                    last.then_inc(S["used_" + a], 1)

                def project_qf(n, first):
                    if not first:
                        pe.wait_ge(S["g_kept"], n)
                    feature_major(0, "q", 0, n)
                    if not first:
                        pe.wait_ge(S["v_kept"], n)
                    feature_major(1, "f", 1, n)

                def project_gv(n):
                    pe.wait_ge(S["q_kept"], n + 1)
                    feature_major(2, "g", 0, n)
                    pe.wait_ge(S["f_kept"], n + 1)
                    pe.wait_ge(S["loaded_v"], n * 16 + 16)
                    for c in range(TC):
                        for kc in range(KC):
                            last = pe.matmul(proj[1][:, c * P:(c + 1) * P], k.hT[:, kc, c * P:(c + 1) * P],
                                             w[3][:, kc, :], start=(kc == 0), stop=(kc == KC - 1))
                    last.then_inc(S["used_v"], 1)

                def scores_and_updates(n, first):
                    pe.wait_ge(S["kend_ready"], n + 1)
                    if not first:
                        pe.wait_ge(S["raw_kept"], n)
                    for c in range(TC):
                        last = pe.transpose(tr_out[:, c * P:(c + 1) * P], k_end[:, c * P:(c + 1) * P], k.const("ident"))
                    last.then_inc(S["keys_turned"], 1)
                    pe.wait_ge(S["qin_ready"], n + 1)
                    pe.wait_ge(S["kin_ready"], n + 1)
                    for c in range(TC):
                        last = pe.matmul(score[:, c * P:(c + 1) * P], k_in[:, c * P:(c + 1) * P],
                                         q_in[:, c * P:(c + 1) * P], start=True, stop=True)
                    last.then_inc(S["scores_done"], 1)
                    pe.wait_ge(S["ktok_kept"], n + 1)
                    pe.wait_ge(S["v_parts_ready"], n + 1)
                    if not first:
                        pe.wait_ge(S["chain_done"], n)
                    for c in range(TC):
                        last = pe.matmul(upd[c][:, :], k_tok[:, c, :], v_parts[:, c, :, :], start=True, stop=True)
                    last.then_inc(S["updates_done"], 1)

                def outputs(n):
                    pe.wait_ge(S["att_ready"], n + 1)
                    pe.wait_ge(S["chain_done"], n + 1)
                    for c in range(TC):
                        last = pe.matmul(tr_out[:, c * P:(c + 1) * P], att[:, c, :], v_tok[:, c, :],
                                         start=True, stop=False, skip_group_check=True)
                        for r in range(QC):
                            ch = c * QC + r
                            if ch:
                                last = pe.matmul(tr_out[r * HG_CHUNK:(r + 1) * HG_CHUNK, c * P:(c + 1) * P],
                                                 q_in[:, ch * HG_CHUNK:(ch + 1) * HG_CHUNK], state[:, ch, :],
                                                 start=False, stop=True, skip_group_check=True)
                    last.then_inc(S["outputs_done"], 1)

                project_qf(0, True)
                project_gv(0)
                project_qf(1, False)
                scores_and_updates(0, True)
                project_gv(1)
                outputs(0)
                with pe.Fori(1, HEADS - 1) as n:
                    project_qf(n + 1, False)
                    scores_and_updates(n, False)
                    project_gv(n + 1)
                    outputs(n)
                scores_and_updates(HEADS - 1, False)
                outputs(HEADS - 1)

            @block.scalar
            def _(act):
                def keep_qf(n, first):
                    act.wait_ge(S["used_q"], n + 1)
                    if not first:
                        act.wait_ge(S["qin_ready"], n)
                    act.activation(q[:], proj[0][:, :], ACT.Identity, bias=k.col("b_in", 0, 8)[:, bass.ds(n, 1)]).then_inc(S["q_kept"], 1)
                    act.wait_ge(S["used_f"], n + 1)
                    act.activation(sigf[:], proj[1][:, :], ACT.Sigmoid, bias=k.col("b_in", 8, 8)[:, bass.ds(n, 1)]).then_inc(S["f_kept"], 1)

                def keep_gate(n):
                    act.wait_ge(S["used_g"], n + 1)
                    act.activation(gate[:, n, :], proj[0][:, :], ACT.Sigmoid, bias=k.col("b_in", 24, 8)[:, bass.ds(n, 1)]).then_inc(S["g_kept"], 1)

                def keep_keys(n):
                    act.wait_ge(S["keys_turned"], n + 1)
                    act.activation(k_tok[:], tr_out[:, :], ACT.Copy).then_inc(S["ktok_kept"], 1)

                def log_decay(n):
                    act.wait_ge(S["fg_ready"], n + 1)
                    act.activation(logf[:], fg[:], ACT.Ln).then_inc(S["logf_ready"], 1)

                def decays(n, first):
                    act.wait_ge(S["b_ready"], n + 1)
                    if not first:
                        act.wait_ge(S["chain_done"], n)
                        act.wait_ge(S["qin_ready"], n)
                        act.wait_ge(S["kin_ready"], n)
                        act.wait_ge(S["kend_ready"], n)
                    act.activation(eb[:], b[:], ACT.Exp).then_inc(S["eb_ready"], 1)
                    act.activation(enb[:], b[:], ACT.Exp, scale=-1.0).then_inc(S["enb_ready"], 1)
                    act.wait_ge(S["left_ready"], n + 1)
                    act.activation(eleft[:], left[:], ACT.Exp).then_inc(S["eleft_ready"], 1)

                def keep_outputs(n):
                    act.wait_ge(S["outputs_done"], n + 1)
                    for c in range(TC):
                        act.activation(junk[:, c, :], tr_out[:, c * P:(c + 1) * P], ACT.Square, accum_out=squares[:, n, c:c + 1])
                    act.activation(raw[:, :, n, :], tr_out[:, :].rearrange("p (c e) -> p c e", e=P), ACT.Copy).then_inc(S["raw_kept"], 1)
                    act.drain()

                keep_qf(0, True)
                keep_gate(0)
                log_decay(0)
                decays(0, True)
                with act.Fori(0, HEADS - 1) as n:
                    keep_qf(n + 1, False)
                    keep_keys(n)
                    keep_gate(n + 1)
                    log_decay(n + 1)
                    decays(n + 1, False)
                    keep_outputs(n)
                keep_keys(HEADS - 1)
                keep_outputs(HEADS - 1)

            @block.vector
            def _(dve):
                def forget(n, first):
                    dve.wait_ge(S["f_kept"], n + 1)
                    if not first:
                        dve.wait_ge(S["logf_ready"], n)
                        dve.wait_ge(S["kend_ready"], n)
                    dve.tensor_scalar(fg[:], sigf[:], one_lb[:, bass.ds(n, 1)], lb[:, bass.ds(n, 1)],
                                      ALU.mult, ALU.add).then_inc(S["fg_ready"], 1)
                    dve.wait_ge(S["fg_ready"], n + 1)
                    dve.tensor_scalar(key[:], fg[:], -1.0, 1.0, ALU.mult, ALU.add).then_inc(S["key_ready"], 1)

                def running(n):
                    dve.wait_ge(S["logf_ready"], n + 1)
                    dve.tensor_tensor_scan(b[:], k.const("chunk_cont"), logf[:], 0.0, ALU.mult, ALU.add).then_inc(S["b_ready"], 1)
                    dve.wait_ge(S["b_ready"], n + 1)
                    b_v = b[:].rearrange("p (n j) -> p n j", j=HG_CHUNK)
                    dve.tensor_tensor(left[:].rearrange("p (n j) -> p n j", j=HG_CHUNK),
                                      b_v[:, :, HG_CHUNK - 1:HG_CHUNK].broadcast_to([P, N_CHUNK, HG_CHUNK]), b_v,
                                      ALU.subtract).then_inc(S["left_ready"], 1)

                def masked_scores(n):
                    dve.wait_ge(S["scores_done"], n + 1)
                    dve.tensor_scalar(att[:].rearrange("p c i -> p (c i)"), score[:, :], 3e38, -3e38, ALU.min, ALU.max)
                    dve.drain()
                    dve.tensor_tensor(att[:], att[:],
                                      k.const("hg_causal").unsqueeze(1).broadcast_to([P, TC, P]), ALU.mult).then_inc(S["att_ready"], 1)

                def chain(n):
                    dve.wait_ge(S["updates_done"], n + 1)
                    dve.tensor_copy(state[:, 1, :], upd[0][:, 0:P])
                    for ch in range(1, N_CHUNK - 1):
                        dve.drain()
                        end = (ch + 1) * HG_CHUNK - 1
                        last = dve.scalar_tensor_tensor(out=state[:, ch + 1, :], in0=state[:, ch, :], scalar=eb[:, end:end + 1],
                                                        in1=upd[ch // QC][:, (ch % QC) * P:(ch % QC + 1) * P],
                                                        op0=ALU.mult, op1=ALU.add)
                    last.then_inc(S["chain_done"], 1)

                def keep_values(n, first):
                    dve.wait_ge(S["used_v"], n + 1)
                    if not first:
                        dve.wait_ge(S["outputs_done"], n)
                    dve.tensor_tensor(v_tok[:], proj[1][:, :].rearrange("p (c e) -> p c e", e=P),
                                      v_bias[:, bass.ts(n, P)].unsqueeze(1).broadcast_to([P, TC, P]), ALU.add).then_inc(S["v_kept"], 1)
                    dve.wait_ge(S["v_kept"], n + 1)
                    for r in range(QC):
                        last = dve.tensor_scalar(v_parts[:, :, r, :], v_tok[:], k.const("chunk_of")[:, r:r + 1], None, ALU.mult)
                    last.then_inc(S["v_parts_ready"], 1)

                def decayed(n, first):
                    dve.wait_ge(S["eb_ready"], n + 1)
                    dve.tensor_tensor(q_in[:], q[:], eb[:], ALU.mult).then_inc(S["qin_ready"], 1)
                    dve.wait_ge(S["enb_ready"], n + 1)
                    dve.tensor_tensor(k_in[:], key[:], enb[:], ALU.mult).then_inc(S["kin_ready"], 1)

                dve.tensor_scalar(one_lb[:], lb[:], -1.0, 1.0, ALU.mult, ALU.add)
                dve.drain()
                forget(0, True)
                running(0)
                keep_values(0, True)
                decayed(0, True)
                with dve.Fori(0, HEADS - 1) as n:
                    forget(n + 1, False)
                    masked_scores(n)
                    chain(n)
                    running(n + 1)
                    keep_values(n + 1, False)
                    decayed(n + 1, False)
                masked_scores(HEADS - 1)
                chain(HEADS - 1)

            @block.gpsimd
            def _(pool):
                def key_to_end(n, first):
                    pool.wait_ge(S["eleft_ready"], n + 1)
                    pool.wait_ge(S["key_ready"], n + 1)
                    if not first:
                        pool.wait_ge(S["keys_turned"], n)
                    pool.tensor_tensor(k_end[:], key[:], eleft[:], ALU.mult).then_inc(S["kend_ready"], 1)

                key_to_end(0, True)
                with pool.Fori(1, HEADS) as n:
                    key_to_end(n, False)


def lower_bound_layer(k, lb):
    nc = k.nc
    with ExitStack() as ctx:
        top = k.sb(ctx, "lb_top", [P, HEADS])
        e = k.sb(ctx, "lb_e", [P, 2, HEADS])
        total = k.sb(ctx, "lb_total", [P, HEADS])
        shifted = k.sem(ctx, "lb_shifted")
        risen = k.sem(ctx, "lb_risen")
        with nc.Block() as block:
            @block.vector
            def _(dve):
                dve.tensor_tensor(top[:], k.col("lb0", 0, 8), k.col("lb1", 0, 8), ALU.max)
                dve.drain()
                dve.tensor_tensor(e[:, 0, :], k.col("lb0", 0, 8), top[:], ALU.subtract)
                dve.tensor_tensor(e[:, 1, :], k.col("lb1", 0, 8), top[:], ALU.subtract).then_inc(shifted, 1)
                dve.wait_ge(risen, 1)
                dve.tensor_tensor(total[:], e[:, 0, :], e[:, 1, :], ALU.add)
                dve.drain()
                dve.reciprocal(total[:], total[:])
                dve.drain()
                dve.tensor_tensor(lb[:], e[:, 0, :], total[:], ALU.mult)

            @block.scalar
            def _(act):
                act.wait_ge(shifted, 1)
                act.activation(e[:], e[:], ACT.Exp).then_inc(risen, 1)


class HeadNorm:

    def __init__(self, k, ctx, gate, squares):
        self.k, self.gate, self.squares = k, gate, squares
        self.raw = k.xn[:].rearrange("p c (h e) -> p c h e", e=P)
        self.dev = k.sb(ctx, "hn_dev", [P, HEADS, TC])
        self.rstd = k.sb(ctx, "hn_rstd", [P, HEADS, TC])
        self.ps, = k.banks(ctx, "hn_ps", 1)
        self.var_ready, self.dev_ready, self.rstd_ready, self.scaled, self.turned, self.bank_free = (
            k.sem(ctx, f"hn_{n}") for n in "var_ready dev_ready rstd_ready scaled turned bank_free".split())

    def begin_vector(self, dve):
        dve.tensor_scalar(self.squares[:], self.squares[:], 1.0 / P, 1e-6, ALU.mult, ALU.add).then_inc(self.var_ready, 1)
        dve.wait_ge(self.dev_ready, 1)
        dve.reciprocal(self.rstd[:], self.dev[:]).then_inc(self.rstd_ready, 1)
        dve.drain().then_inc(self.bank_free, 1)

    def begin_scalar(self, act):
        act.wait_ge(self.var_ready, 1)
        act.activation(self.dev[:], self.squares[:], ACT.Sqrt).then_inc(self.dev_ready, 1)
        act.wait_ge(self.rstd_ready, 1)

    def scale(self, act, h):
        for c in range(TC):
            last = act.activation(self.raw[:, c, h, :], self.raw[:, c, h, :], ACT.Copy, scale=self.rstd[:, h, c:c + 1])
        last.then_inc(self.scaled, 1)

    def turn(self, pe, h):
        pe.wait_ge(self.scaled, h + 1)
        pe.wait_ge(self.bank_free, h + 1)
        for c in range(TC):
            last = pe.transpose(self.ps[:, c * P:(c + 1) * P], self.raw[:, c, h, :], self.k.const("ident"))
        last.then_inc(self.turned, 1)

    def gated(self, dve, h):
        dve.wait_ge(self.turned, h + 1)
        dve.scalar_tensor_tensor(out=self.gate[:, h, :], in0=self.ps[:, :], scalar=self.k.col("hg_norm_w", h),
                                 in1=self.gate[:, h, :], op0=ALU.mult, op1=ALU.mult).then_inc(self.bank_free, 1)


class KeyWeights:

    def __init__(self, k, ctx):
        self.k = k
        self.slices = SlicesAhead(k, ctx, "kv", 2, lambda n: k.i["w_kv"][n])

    def add_compression(self, ctx):
        k = self.k
        self.w1 = [k.sb(ctx, f"cmp_w1_{s}", [P, CMP_BLOCK, P]) for s in range(2)]
        self.w2 = k.sb(ctx, "cmp_w2", [P, 2, P])
        self.w1_loaded = [k.sem(ctx, f"cmp_w1_loaded{s}") for s in range(2)]
        self.w2_loaded = k.sem(ctx, "cmp_w2_loaded")
        self.pos_loaded = k.sem(ctx, "cmp_pos_loaded")


def key_values(k, kvT, v_tok, gates, k_cmp, v_cmp, Tables, ahead, gate, squares, send_next):
    with ExitStack() as ctx:
        ahead.add_compression(ctx)
        project_keys_values(k, kvT, v_tok, gates, Tables, ahead, gate, squares)
        compress(k, kvT, k_cmp, v_cmp, ahead, send_next)


def project_keys_values(k, kvT, v_tok, gates, Tables, ahead, gate, squares):
    nc = k.nc
    w_kv, w_v, w_cmp = k.i["w_kv"], k.i["w_v"], k.i["w_cmp"]
    NV = 2 * GROUPS * P + 3 * HEADS
    with ExitStack() as ctx:
        w, w_loaded = ahead.slices.w, ahead.slices.loaded
        wv = k.sb(ctx, "kv_wv", [P, KC, NV])
        v_bias = k.kv_v_bias
        ps = k.banks(ctx, "kv_ps", 2)
        psv = k.banks(ctx, "kv_psv", 2)
        psg, = k.banks(ctx, "kv_psg", 1)
        norm = HeadNorm(k, ctx, gate, squares)
        wv_loaded = k.sem(ctx, "kv_wv_loaded")
        projected = k.sem(ctx, "kv_projected")
        kept = k.sem(ctx, "kv_kept")
        v_projected = k.sem(ctx, "kv_v_projected")
        v_kept = k.sem(ctx, "kv_v_kept")
        g_projected = k.sem(ctx, "kv_g_projected")
        g_kept = k.sem(ctx, "kv_g_kept")
        onehot = k.sb(ctx, "bias_onehot", [BUCKETS + 1, BT_ROW])
        rel = k.sb(ctx, "bias_rel", [BUCKETS + 1, HEADS])
        r_sb = k.sb(ctx, "bias_r", [HEADS, BT_ROW])
        bias_ps = k.banks(ctx, "bias_ps", 2)
        bias_loaded = k.sem(ctx, "bias_loaded")
        neg_set = k.sem(ctx, "bias_neg_set")
        bias_made = k.sem(ctx, "bias_made")
        bias_kept = k.sem(ctx, "bias_kept")
        spread = k.sem(ctx, "bias_spread")
        with nc.Block() as block:
            @block.sync
            def _(sp):
                sp.dma_start(onehot[:], k.i["buckets"]).then_inc(bias_loaded, 16)
                sp.wait_ge(neg_set, 1)
                sp.dma_start(rel[0:BUCKETS, :], k.i["rel_bias"]).then_inc(bias_loaded, 16)
                sp.dma_start(wv[:], w_v.rearrange("(k p) n -> p k n", p=P)).then_inc(wv_loaded, 16)
                with sp.Fori(1, 4) as it:
                    for s in range(2):
                        sp.wait_ge(projected, it * 2 + (s - 1))
                        sp.dma_start(w[s], w_kv[it * 2 + s]).then_inc(w_loaded[s], 16)
                sp.wait_ge(neg_set, 2)
                for s in range(2):
                    sp.dma_start(kvT[:, 3 * s + 2, 0:CMP_BLOCK], k.i["cmp_pos"][s]).then_inc(ahead.pos_loaded, 16)
                for s in range(2):
                    sp.dma_start(ahead.w1[s][:], w_cmp[s].rearrange("(l d) h -> d l h", d=P)).then_inc(ahead.w1_loaded[s], 16)
                sp.dma_start(ahead.w2[:], k.i["w_cmp2"].rearrange("s h d -> h s d")).then_inc(ahead.w2_loaded, 16)
                sp.wait_ge(bias_kept, 2)
                for h in range(HEADS):
                    sp.dma_start(Tables[h], r_sb[h:h + 1, :].unsqueeze(1).broadcast_to([1, P, BT_ROW])).then_inc(spread, 16)
                sp.wait_ge(spread, 16 * HEADS)

            @block.tensor
            def _(pe):
                def feature_major(it, s, first):
                    pe.wait_ge(w_loaded[s], it * 16 + 16)
                    if not first:
                        pe.wait_ge(kept, it * 2 + (s - 1))
                    for kc in range(KC):
                        last = pe.matmul(ps[s][:, :], w[s][:, kc, :], k.hT[:, kc, :], start=(kc == 0), stop=(kc == KC - 1))
                    last.then_inc(projected, 1)

                for s in range(2):
                    feature_major(0, s, True)
                for j in range(2, 8):
                    feature_major(j // 2, j % 2, False)
                    norm.turn(pe, j - 2)
                for h in (HEADS - 2, HEADS - 1):
                    norm.turn(pe, h)
                pe.wait_ge(bias_loaded, 32)
                for j in range(2):
                    pe.matmul(bias_ps[j][0:HEADS, :], rel[:], onehot[:, j * 512:(j + 1) * 512], start=True, stop=True).then_inc(bias_made, 1)
                pe.wait_ge(wv_loaded, 16)
                for c in range(TC):
                    if c >= 2:
                        pe.wait_ge(v_kept, c - 1)
                    for kc in range(KC):
                        last = pe.matmul(psv[c % 2][:, :], k.hT[:, kc, c * P:(c + 1) * P], wv[:, kc, 0:4 * P],
                                         start=(kc == 0), stop=(kc == KC - 1))
                    last.then_inc(v_projected, 1)
                for c in range(TC):
                    for kc in range(KC):
                        last = pe.matmul(psg[:, c * 24:(c + 1) * 24], k.hT[:, kc, c * P:(c + 1) * P], wv[:, kc, 4 * P:NV],
                                         start=(kc == 0), stop=(kc == KC - 1))
                last.then_inc(g_projected, 1)

            @block.scalar
            def _(act):
                norm.begin_scalar(act)
                for j, (plane, at) in enumerate(((0, 40), (1, 41), (3, 42), (4, 43), (6, 44), (7, 45), (8, 48), (9, 49))):
                    act.wait_ge(projected, j + 1)
                    act.activation(kvT[:, plane, :], ps[j % 2][:, :], ACT.Identity, bias=k.col("b_in", at)).then_inc(kept, 1)
                    norm.scale(act, j)
                act.wait_ge(g_kept, 1)
                act.activation(gates[:], gates[:], ACT.Sigmoid)

            @block.vector
            def _(dve):
                dve.memset(rel[:], NEG).then_inc(neg_set, 1)
                dve.memset(kvT[:, 2, :], 0.0)
                dve.memset(kvT[:, 5, :], 0.0).then_inc(neg_set, 1)
                norm.begin_vector(dve)
                for h in range(HEADS):
                    norm.gated(dve, h)
                for j in range(2):
                    dve.wait_ge(bias_made, j + 1)
                    dve.tensor_copy(r_sb[:, j * 512:(j + 1) * 512], bias_ps[j][0:HEADS, :]).then_inc(bias_kept, 1)
                for c in range(TC):
                    dve.wait_ge(v_projected, c + 1)
                    dve.tensor_tensor(v_tok[:, c, :], psv[c % 2][:, :], v_bias[:], ALU.add).then_inc(v_kept, 1)
                dve.wait_ge(g_projected, 1)
                dve.tensor_tensor(gates[:], psg[:, 0:TC * 24].rearrange("p (c n) -> p c n", n=24),
                                  k.row("b_gate").unsqueeze(1).broadcast_to([P, TC, 24]), ALU.add).then_inc(g_kept, 1)


def compress(k, kvT, k_cmp, v_cmp, ahead, send_next):
    nc = k.nc
    NB = GROUPS * N_CMP
    NB1 = NB + N_CMP
    w1, w2, loaded, w2_loaded = ahead.w1, ahead.w2, ahead.w1_loaded, ahead.w2_loaded
    with ExitStack() as ctx:
        bias = k.sb(ctx, "cmp_bias", [P, 2])
        pre = k.sb(ctx, "cmp_pre", [P, 2, NB])
        sig = k.sb(ctx, "cmp_sig", [P, 2, NB])
        ps, psk, psv = k.banks(ctx, "cmp_ps", 3)
        hidden_done = k.sem(ctx, "cmp_hidden_done")
        pre_ready = k.sem(ctx, "cmp_pre_ready")
        sig_ready = k.sem(ctx, "cmp_sig_ready")
        act_ready = k.sem(ctx, "cmp_act_ready")
        out_done = k.sem(ctx, "cmp_out_done")
        with nc.Block() as block:
            @block.sync
            def _(sp):
                send_next(sp)

            @block.tensor
            def _(pe):
                pe.wait_ge(ahead.pos_loaded, 32)
                for s in range(2):
                    pe.wait_ge(loaded[s], 16)
                    for l in range(CMP_BLOCK):
                        last = pe.matmul(ps[:, s * NB1:(s + 1) * NB1], w1[s][:, l, :],
                                         kvT[:, 3 * s:3 * s + 3, l:l + CMP_STRIDE * (N_CMP - 1) + 1:CMP_STRIDE],
                                         start=(l == 0), stop=(l == CMP_BLOCK - 1))
                    last.then_inc(hidden_done, 1)
                pe.wait_ge(act_ready, 1)
                pe.wait_ge(w2_loaded, 16)
                pe.matmul(psk[:, 0:NB], w2[:, 0, :], pre[:, 0, :], start=True, stop=True)
                for g in range(GROUPS):
                    last = pe.matmul(psv[0:N_CMP, g * P:(g + 1) * P], pre[:, 1, g * N_CMP:(g + 1) * N_CMP], w2[:, 1, :],
                                     start=True, stop=True)
                last.then_inc(out_done, 1)

            @block.vector
            def _(dve):
                dve.memset(v_cmp[:], 0.0)
                for s, b1 in enumerate(("cmp_b1_k", "cmp_b1_v")):
                    dve.wait_ge(hidden_done, 2)
                    dve.tensor_scalar(bias[:, s:s + 1], ps[:, s * NB1 + NB:s * NB1 + NB + 1], k.col(b1), None, ALU.add)
                    dve.drain()
                    dve.tensor_scalar(pre[:, s, :], ps[:, s * NB1:s * NB1 + NB], bias[:, s:s + 1], None, ALU.add).then_inc(pre_ready, 1)
                dve.wait_ge(sig_ready, 1)
                dve.tensor_tensor(pre[:], pre[:], sig[:], ALU.mult).then_inc(act_ready, 1)
                dve.wait_ge(out_done, 1)
                dve.tensor_copy(k_cmp[:], psk[:, 0:NB])
                dve.tensor_copy(v_cmp[0:N_CMP], psv[0:N_CMP, 0:GROUPS * P].rearrange("p (g e) -> p g e", e=P))

            @block.scalar
            def _(act):
                act.wait_ge(pre_ready, 2)
                act.activation(sig[:], pre[:], ACT.Sigmoid).then_inc(sig_ready, 1)


def sparse_attention(k, onT, ahead, gate, squares, send_next):
    nc = k.nc
    UNITS = [(br, c) for br in range(2) for c in range(TC)]
    NU = len(UNITS) + 1
    with ExitStack() as ctx:
        first_queries = SlicesAhead(k, ctx, "at_wq", 2, lambda n: k.i["w_nq"][n])
        kvT = k.sb(ctx, "at_kvT", [P, 10, SEQ])
        v_tok = k.sb(ctx, "at_v_tok", [P, TC, 512])
        gates = k.sb(ctx, "at_gates", [P, TC, 24])
        k_cmp = k.sb(ctx, "at_k_cmp", [P, GROUPS * N_CMP])
        v_cmp = k.sb(ctx, "at_v_cmp", [P, GROUPS, P])
        spread = nc.dram_tensor("bias_spread_rows", [HEADS, P, BT_ROW], F32).ap()
        key_values(k, kvT, v_tok, gates, k_cmp, v_cmp, spread, ahead, gate, squares, first_queries.send)

        wq = first_queries.w
        q = [k.sb(ctx, f"at_q{s}", [P, SEQ]) for s in range(2)]
        q_bias = k.sb(ctx, "at_q_bias", [P, HEADS])
        table = [k.sb(ctx, f"at_table{s}", [P, BTW]) for s in range(2)]
        values = k.sb(ctx, "at_values", [P, 2, TC, P])
        cvalues = k.sb(ctx, "at_cvalues", [P, P])
        p = [k.sb(ctx, f"at_p{u}", [P, SEQ]) for u in range(NU)]
        top = k.sb(ctx, "at_top", [P, NU, TC])
        ntop = k.sb(ctx, "at_ntop", [P, NU, TC])
        total = k.sb(ctx, "at_total", [P, NU, TC])
        factor = k.sb(ctx, "at_factor", [P, NU, TC])
        pT = [k.sb(ctx, f"at_pT{s}", [P, SEQ]) for s in range(2)]
        cpT = k.sb(ctx, "at_cpT", [P, SEQ])
        spare = k.sb(ctx, "at_spare", [P, 2])

        sc = k.banks(ctx, "at_sc", 3)
        tr = k.banks(ctx, "at_tr", 2)
        o_ps = k.banks(ctx, "at_o", 2)
        proj, = k.banks(ctx, "at_proj", 1)

        names = ("table_loaded0 table_loaded1 q_projected q_kept bias_ready "
                 "scored logits_ready exp_ready factor_ready p_ready turned pT_ready mixed o_kept values_ready cleared").split()
        S = {n: k.sem(ctx, "at_" + n) for n in names}
        S.update({f"wq_loaded{s}": first_queries.loaded[s] for s in range(2)})

        def pairs(eng, head):
            head(0, 0)
            head(1, 1)
            with eng.Fori(1, HEADS // 2 - 1) as it:
                head(it * 2, 0)
                head(it * 2 + 1, 1)
            head(HEADS - 2, 0)
            head(HEADS - 1, 1)

        def step(do, h, s, u):
            if u < NU:
                do(h, s, u)
            elif not (isinstance(h, int) and h == HEADS - 1):
                do(h + 1, 1 - s, u - NU)

        def loads(h, s):
            return 16 * (h // 2 + 1) if isinstance(h, int) else (h - s) * 8 + 16

        def stagings(h, s):
            if isinstance(h, int):
                return 1 if h < 2 else 3
            return (h - s) // 2 + 1

        def after_first(h):
            return not isinstance(h, int) or h > 0

        with nc.Block() as block:
            @block.sync
            def _(sp):
                def load_head(h, s):
                    if not isinstance(h, int) or h >= 2:
                        sp.wait_ge(S["q_projected"], h - 1)
                        sp.dma_start(wq[s], k.i["w_nq"][h]).then_inc(S[f"wq_loaded{s}"], 16)
                    if not isinstance(h, int) or h >= 2:
                        sp.wait_ge(S["logits_ready"], (h - 1) * NU)
                    view = spread[h].rearrange("p m -> (p m)")[P - 1:P - 1 + P * (BT_ROW - 1)]
                    view = view.rearrange("(p m) -> p m", m=BT_ROW - 1)[:, 0:BTW]
                    sp.dma_start(table[s][:], view).then_inc(S[f"table_loaded{s}"], 16)

                pairs(sp, load_head)
                send_next(sp)

            @block.tensor
            def _(pe):
                def project(h, s, part):
                    if part == 0:
                        pe.wait_ge(S[f"wq_loaded{s}"], loads(h, s))
                        if after_first(h):
                            pe.wait_ge(S["q_kept"], h)
                    for kc in range(part * 2, part * 2 + 2):
                        last = pe.matmul(proj[:, :], wq[s][:, kc, :], k.hT[:, kc, :], start=(kc == 0), stop=(kc == KC - 1))
                    if part == 3:
                        last.then_inc(S["q_projected"], 1)

                def scores(h, s, u):
                    g = h // REP
                    if u >= 3 or after_first(h):
                        pe.wait_ge(S["logits_ready"], h * NU + (u - 2))
                    if u == 0:
                        pe.wait_ge(S["q_kept"], h + 1)
                    if u < len(UNITS):
                        br, c = UNITS[u]
                        keys = kvT[:, 6 + GROUPS * br:6 + GROUPS * (br + 1), :]
                        last = pe.matmul(sc[u % 3][:, 0:(c + 1) * P], q[s][:, c * P:(c + 1) * P],
                                         keys[:, g, 0:(c + 1) * P], start=True, stop=True)
                    else:
                        for c in range(TC):
                            last = pe.matmul(sc[u % 3][:, c * N_CMP:(c + 1) * N_CMP], q[s][:, c * P:(c + 1) * P],
                                             k_cmp[:, bass.ts(g, N_CMP)], start=True, stop=True)
                    last.then_inc(S["scored"], 1)

                def turn(h, u):
                    pe.wait_ge(S["p_ready"], h * NU + (u + 1))
                    if u >= 2 or after_first(h):
                        pe.wait_ge(S["pT_ready"], h * NU + max(u - 1, 0))
                    if u < len(UNITS):
                        for kk in range(UNITS[u][1] + 1):
                            last = pe.transpose(tr[u % 2][:, kk * P:(kk + 1) * P], p[u][:, kk * P:(kk + 1) * P], k.const("ident"))
                    else:
                        for c in range(TC):
                            last = pe.transpose(tr[u % 2][0:N_CMP, c * P:(c + 1) * P],
                                                p[u][:, c * N_CMP:(c + 1) * N_CMP], k.const("ident"))
                    last.then_inc(S["turned"], 1)

                def mix(h, s, u):
                    pe.wait_ge(S["pT_ready"], h * NU + (u + 1))
                    if u == 0:
                        pe.wait_ge(S["values_ready"], stagings(h, s))
                        if not isinstance(h, int) or h >= 2:
                            pe.wait_ge(S["o_kept"], h - 1)
                    if u < len(UNITS):
                        br, c = UNITS[u]
                        for kk in range(c + 1):
                            last = pe.matmul(o_ps[s][:, c * P:(c + 1) * P], values[:, br, kk, :], pT[u % 2][:, kk * P:(kk + 1) * P],
                                             start=(u == 0), stop=False, skip_group_check=True)
                    else:
                        last = pe.matmul(o_ps[s][:, :], cvalues[:], cpT[:], start=False, stop=True, skip_group_check=True)
                    last.then_inc(S["mixed"], 1)

                def head(h, s):
                    for u in range(NU):
                        turn(h, u)
                        step(scores, h, s, u + 3)
                        if u < 4 and not (isinstance(h, int) and h == HEADS - 1):
                            project(h + 1, 1 - s, u)
                        if u:
                            mix(h, s, u - 1)
                        elif after_first(h):
                            mix(h - 1, 1 - s, NU - 1)

                for part in range(4):
                    project(0, 0, part)
                for u in range(3):
                    scores(0, 0, u)
                pairs(pe, head)
                mix(HEADS - 1, 1, NU - 1)

            @block.scalar
            def _(act):
                act.activation(q_bias[:], k.col("b_in", 32, 8), ACT.Copy, scale=ATT_SCALE).then_inc(S["bias_ready"], 1)
                act.wait_ge(S["bias_ready"], 1)

                def keep_q(h, s):
                    act.wait_ge(S["q_projected"], h + 1)
                    act.activation(q[s][:], proj[:, :], ACT.Identity, bias=q_bias[:, bass.ds(h, 1)], scale=ATT_SCALE).then_inc(S["q_kept"], 1)

                def weights(h, s, u):
                    act.wait_ge(S["logits_ready"], h * NU + (u + 1))
                    if u < len(UNITS):
                        n = (UNITS[u][1] + 1) * P
                        act.activation(p[u][:, 0:n], p[u][:, 0:n], ACT.Exp, bias=ntop[:, u, 0:1],
                                       accum_out=total[:, u, 0:1]).then_inc(S["exp_ready"], 1)
                    else:
                        for c in range(TC):
                            last = act.activation(p[u][:, c * N_CMP:(c + 1) * N_CMP], p[u][:, c * N_CMP:(c + 1) * N_CMP],
                                                  ACT.Exp, bias=ntop[:, u, c:c + 1], accum_out=total[:, u, c:c + 1])
                        last.then_inc(S["exp_ready"], 1)

                def keep_turned(h, u):
                    act.wait_ge(S["turned"], h * NU + (u + 1))
                    if u < len(UNITS):
                        if u >= 2 or after_first(h):
                            act.wait_ge(S["mixed"], h * NU + (u - 1))
                        n = (UNITS[u][1] + 1) * P
                        act.activation(pT[u % 2][:, 0:n], tr[u % 2][:, 0:n], ACT.Copy).then_inc(S["pT_ready"], 1)
                    else:
                        if after_first(h):
                            act.wait_ge(S["mixed"], h * NU)
                        else:
                            act.wait_ge(S["cleared"], 1)
                        act.activation(cpT[0:N_CMP, :], tr[u % 2][0:N_CMP, :], ACT.Copy).then_inc(S["pT_ready"], 1)

                def head(h, s):
                    for u in range(NU):
                        step(weights, h, s, u + 1)
                        if u == 4 and not (isinstance(h, int) and h == HEADS - 1):
                            keep_q(h + 1, 1 - s)
                        if u:
                            keep_turned(h, u - 1)
                        elif after_first(h):
                            keep_turned(h - 1, NU - 1)

                keep_q(0, 0)
                weights(0, 0, 0)
                pairs(act, head)
                keep_turned(HEADS - 1, NU - 1)

            @block.vector
            def _(dve):
                dve.memset(cpT[:], 0.0).then_inc(S["cleared"], 1)

                def logits(h, s, u):
                    if u == 0:
                        dve.wait_ge(S[f"table_loaded{s}"], loads(h, s))
                    dve.wait_ge(S["scored"], h * NU + (u + 1))
                    if after_first(h):
                        dve.wait_ge(S["turned"], (h - 1) * NU + (u + 1))
                    dve.memset(spare[:, 0:1], 0.0)
                    buf, bank = p[u], sc[u % 3]
                    if u < len(UNITS):
                        n = (UNITS[u][1] + 1) * P
                        dve.tensor_tensor_reduce(buf[:, 0:n], bank[:, 0:n], table[s][:, BT0 + P - n:BT0 + P], 1.0, NEG * 10,
                                                 ALU.add, ALU.max, top[:, u, 0:1])
                        dve.drain()
                        dve.tensor_scalar(ntop[:, u, 0:1], top[:, u, 0:1], -1.0, None, ALU.mult).then_inc(S["logits_ready"], 1)
                    else:
                        for c in range(TC):
                            at = BT0 + CMP_BLOCK - 1 - c * P
                            dve.tensor_tensor_reduce(buf[:, c * N_CMP:(c + 1) * N_CMP], bank[:, c * N_CMP:(c + 1) * N_CMP],
                                                     table[s][:, at:at + CMP_STRIDE * (N_CMP - 1) + 1:CMP_STRIDE], 1.0, NEG * 10,
                                                     ALU.add, ALU.max, top[:, u, c:c + 1])
                        dve.drain()
                        dve.tensor_scalar(ntop[:, u, :], top[:, u, :], -1.0, None, ALU.mult).then_inc(S["logits_ready"], 1)

                def normalized(h, u):
                    dve.wait_ge(S["exp_ready"], h * NU + (u + 1))
                    nr = 1 if u < len(UNITS) else TC
                    dve.reciprocal(factor[:, u, 0:nr], total[:, u, 0:nr])
                    dve.drain()
                    buf = p[u]
                    if u < len(UNITS):
                        br, c = UNITS[u]
                        n = (c + 1) * P
                        dve.tensor_scalar(buf[:, 0:n], buf[:, 0:n], factor[:, u, 0:1], gates[:, c, bass.ds(h * 3 + (1 + br), 1)],
                                          ALU.mult, ALU.mult).then_inc(S["p_ready"], 1)
                    else:
                        for c in range(TC):
                            blk = buf[:, c * N_CMP:(c + 1) * N_CMP]
                            dve.tensor_scalar(blk, blk, factor[:, u, c:c + 1], gates[:, c, bass.ds(h * 3, 1)], ALU.mult, ALU.mult)
                        dve.drain()
                        blk = buf[:, 0:TC * N_CMP]
                        dve.tensor_tensor(blk, blk, k.const("cmp_ok"), ALU.mult).then_inc(S["p_ready"], 1)

                def keep_output(h, s):
                    dve.wait_ge(S["mixed"], h * NU + NU)
                    dve.tensor_copy(onT[:, h, :], o_ps[s][:, :]).then_inc(S["o_kept"], 1)

                def head(h, s):
                    for u in range(NU):
                        step(logits, h, s, u + 1)
                        normalized(h, u)
                        if u == 2 and after_first(h):
                            keep_output(h - 1, 1 - s)

                logits(0, 0, 0)
                pairs(dve, head)
                keep_output(HEADS - 1, 1)

            @block.gpsimd
            def _(pool):
                def stage_values(h, s):
                    if s == 1 or (isinstance(h, int) and h > 0):
                        return
                    if after_first(h):
                        pool.wait_ge(S["mixed"], h * NU)
                        pool.tensor_tensor(spare[:, 1:2], k.const("ones", 0, 1), k.const("ones", 0, 1), ALU.add)
                    g = h // REP
                    v_v = v_tok[:].rearrange("p c (b e) -> p c b e", e=P)
                    for br in range(2):
                        pool.tensor_copy(values[:, br, :, :], v_v[:, :, 2 * br:2 * br + 2, :][:, :, g, :])
                    pool.tensor_copy(cvalues[:], v_cmp[:, g, :]).then_inc(S["values_ready"], 1)

                pairs(pool, stage_values)


def merge_branches(k, ohT, onT, mergedT, first_slices, send_next):
    nc = k.nc
    with ExitStack() as ctx:
        w, loaded = first_slices.w, first_slices.loaded
        sig = [k.sb(ctx, f"mg_sig{s}", [P, SEQ]) for s in range(2)]
        part = [k.sb(ctx, f"mg_part{s}", [P, SEQ]) for s in range(2)]
        ps = k.banks(ctx, "mg_ps", 4)
        done = [k.sem(ctx, f"mg_done{s}") for s in range(4)]
        sig_ready = [k.sem(ctx, f"mg_sig_ready{s}") for s in range(2)]
        part_ready = [k.sem(ctx, f"mg_part_ready{s}") for s in range(2)]
        sources = (k.hT, k.hT, ohT, onT)
        zeros = k.sb(ctx, "mg_zeros", [SLOTS, D])
        zeros_ready = k.sem(ctx, "mg_zeros_ready")
        zeroed = k.dma_sems["zeroed"]
        with nc.Block() as block:
            @block.sync
            def _(sp):
                with sp.Fori(1, KC) as j:
                    for s in range(4):
                        sp.wait_ge(done[s], j)
                        sp.dma_start(w[s], k.i["w_merge"][j, s]).then_inc(loaded[s], 16)
                send_next(sp)

            @block.gpsimd
            def _(pool):
                pool.memset(zeros[:], 0.0).then_inc(zeros_ready, 1)
                pool.wait_ge(zeros_ready, 1)
                pool.wait_ge(done[1], 2)
                pool.dma_start(k.sent[0].rearrange("e s d -> s e d"),
                               zeros[:].unsqueeze(1).broadcast_to([SLOTS, N_EXP, D])).then_inc(zeroed, 16)
                pool.wait_ge(zeroed, 16)

            @block.tensor
            def _(pe):
                def step(j, first):
                    for s in range(4):
                        pe.wait_ge(loaded[s], j * 16 + 16)
                        if not first:
                            pe.wait_ge(sig_ready[s] if s < 2 else part_ready[s - 2], j)
                        for kc in range(KC):
                            last = pe.matmul(ps[s][:, :], w[s][:, kc, :], sources[s][:, kc, :], start=(kc == 0), stop=(kc == KC - 1))
                        last.then_inc(done[s], 1)

                step(0, True)
                with pe.Fori(1, KC) as j:
                    step(j, False)

            @block.scalar
            def _(act):
                def step(j, first):
                    for s in range(2):
                        act.wait_ge(done[s], j + 1)
                        if not first:
                            act.wait_ge(part_ready[s], j)
                        act.activation(sig[s][:], ps[s][:, :], ACT.Sigmoid, bias=k.col("b_mg", 8 * s, 8)[:, bass.ds(j, 1)]).then_inc(sig_ready[s], 1)

                step(0, True)
                with act.Fori(1, KC) as j:
                    step(j, False)

            @block.vector
            def _(dve):
                with dve.Fori(0, KC) as j:
                    for s in range(2):
                        dve.wait_ge(done[2 + s], j + 1)
                        dve.wait_ge(sig_ready[s], j + 1)
                        dve.tensor_tensor(part[s][:], sig[s][:], ps[2 + s][:, :], ALU.mult).then_inc(part_ready[s], 1)
                    dve.drain()
                    dve.tensor_tensor(mergedT[:, j, :], part[0][:], part[1][:], ALU.add)
                    dve.drain()


class OutWeights:

    HALF = 512

    def __init__(self, k, ctx, tag, weights):
        self.w_v = weights
        self.w = [k.sb(ctx, f"{tag}_w{s}", [P, KC, self.HALF]) for s in range(2)]
        self.loaded = [k.sem(ctx, f"{tag}_loaded{s}") for s in range(2)]

    def send(self, sp):
        for h in range(2):
            sp.dma_start(self.w[h][:], self.w_v[h]).then_inc(self.loaded[h], 16)


def project_out(k, tag, weights, source, gate, plus, residual):
    nc = k.nc
    w, loaded, HALF = weights.w, weights.loaded, weights.HALF
    with ExitStack() as ctx:
        gain = k.sb(ctx, f"{tag}_gain", [P, D])
        gain_ps = k.banks(ctx, f"{tag}_gain_ps", 2)
        gain_turned = k.sem(ctx, f"{tag}_gain_turned")
        part = [k.sb(ctx, f"{tag}_part{s}", [P, HALF]) for s in range(2)]
        ps = k.banks(ctx, f"{tag}_ps", 2)
        done = k.sem(ctx, f"{tag}_done")
        kept = k.sem(ctx, f"{tag}_kept")
        units = [(h, c) for h in range(2) for c in range(TC)]
        with nc.Block() as block:
            @block.tensor
            def _(pe):
                for j in range(KC):
                    last = pe.transpose(gain_ps[j // 4][:, j % 4 * P:(j % 4 + 1) * P], gate[:, j:j + 1].broadcast_to([P, P]), k.const("ident"))
                last.then_inc(gain_turned, 1)
                for n, (h, c) in enumerate(units):
                    if c == 0:
                        pe.wait_ge(loaded[h], 16)
                    if n >= 2:
                        pe.wait_ge(kept, n - 1)
                    for kc in range(KC):
                        last = pe.matmul(ps[n % 2][:, :], source[:, kc, c * P:(c + 1) * P], w[h][:, kc, :],
                                         start=(kc == 0), stop=(kc == KC - 1))
                    last.then_inc(done, 1)

            @block.vector
            def _(dve):
                dve.wait_ge(gain_turned, 1)
                for h in range(2):
                    dve.tensor_scalar(gain[:, h * HALF:(h + 1) * HALF], gain_ps[h][:, :], float(plus), None, ALU.add)
                dve.drain()
                for n, (h, c) in enumerate(units):
                    cut = slice(h * HALF, (h + 1) * HALF)
                    dve.wait_ge(done, n + 1)
                    dve.tensor_tensor(part[n % 2][:], ps[n % 2][:, :], gain[:, cut], ALU.mult).then_inc(kept, 1)
                    dve.wait_ge(kept, n + 1)
                    dve.scalar_tensor_tensor(out=k.x[:, c, cut], in0=k.x[:, c, cut], scalar=float(residual), in1=part[n % 2][:],
                                             op0=ALU.mult, op1=ALU.add)


def route(k, tag, w, bias_row, row_of, share, most):
    nc = k.nc
    with ExitStack() as ctx:
        lg = k.sb(ctx, f"{tag}_lg", [P, TC, N_GRP + N_EXP])
        small = {n: k.sb(ctx, f"{tag}_{n}", [P, TC]) for n in ("gtop", "gsum", "m", "m1", "m2", "d")}
        ge = k.sb(ctx, f"{tag}_ge", [P, TC, N_GRP])
        goh = k.sb(ctx, f"{tag}_goh", [P, TC, N_GRP])
        pen = k.sb(ctx, f"{tag}_pen", [P, TC, N_EXP])
        el = k.sb(ctx, f"{tag}_el", [P, TC, N_EXP])
        place = k.sb(ctx, f"{tag}_place", [P, TC, N_EXP])
        ohs = k.sb(ctx, f"{tag}_oh", [P, 2, TC, N_EXP])
        oh = [ohs[:, s] for s in range(2)]
        rows = k.sb(ctx, f"{tag}_rows", [P, 2, TC])
        earlier = k.sb(ctx, f"{tag}_earlier", [P, 2, TC])
        later = k.sb(ctx, f"{tag}_later", [P, 2, TC, PASSES - 1])
        passed = k.sb(ctx, f"{tag}_passed", [P, 2, TC])
        chosen = k.sb(ctx, f"{tag}_chosen", [P, TC, N_EXP])
        mostf = k.sb(ctx, f"{tag}_mostf", [P, 1])
        ps = k.banks(ctx, f"{tag}_ps", 3)
        logits_done = k.sem(ctx, f"{tag}_logits_done")
        shifted = k.sem(ctx, f"{tag}_shifted")
        risen = k.sem(ctx, f"{tag}_risen")
        chosen_ready = k.sem(ctx, f"{tag}_chosen_ready")
        counted = k.sem(ctx, f"{tag}_counted")
        with nc.Block() as block:
            @block.tensor
            def _(pe):
                NL = N_GRP + N_EXP
                for c in range(TC):
                    for kc in range(KC):
                        last = pe.matmul(ps[0][:, c * NL:(c + 1) * NL], k.hT[:, kc, c * P:(c + 1) * P], w[:, kc, :],
                                         start=(kc == 0), stop=(kc == KC - 1))
                last.then_inc(logits_done, 1)
                pe.wait_ge(chosen_ready, 1)
                for c in range(TC):
                    for b in range(c + 1):
                        pe.matmul(ps[1][:, c * N_EXP:(c + 1) * N_EXP], k.const("before") if b == c else k.const("ones"),
                                  chosen[:, b, :], start=(b == 0), stop=(b == c))
                for b in range(TC):
                    last = pe.matmul(ps[2][:, 0:N_EXP], k.const("ones"), chosen[:, b, :], start=(b == 0), stop=(b == TC - 1))
                last.then_inc(counted, 1)

            @block.scalar
            def _(act):
                act.wait_ge(shifted, 1)
                act.activation(ge[:], ge[:], ACT.Exp).then_inc(risen, 1)
                act.wait_ge(shifted, 2)
                act.activation(small["d"][:], small["d"][:], ACT.Exp).then_inc(risen, 1)

            @block.vector
            def _(dve):
                def per_token(a, n):
                    return a[:].unsqueeze(2).broadcast_to([P, TC, n])

                def first_best(values, n, top, out):
                    dve.tensor_reduce(top[:], values, AX.X, ALU.max)
                    dve.drain()
                    dve.tensor_tensor(out, values, per_token(top, n), ALU.is_equal)
                    dve.drain()
                    dve.tensor_tensor(out, out, k.const("first", 0, n).unsqueeze(1).broadcast_to([P, TC, n]), ALU.mult)
                    dve.drain()
                    dve.tensor_reduce(small["m"][:], out, AX.X, ALU.max)
                    dve.drain()
                    dve.tensor_tensor(out, out, per_token(small["m"], n), ALU.is_equal)
                    dve.drain()

                dve.wait_ge(logits_done, 1)
                NL = N_GRP + N_EXP
                dve.tensor_tensor(lg[:], ps[0][:, 0:TC * NL].rearrange("p (c n) -> p c n", n=NL),
                                  bias_row.unsqueeze(1).broadcast_to([P, TC, NL]), ALU.add)
                dve.drain()
                first_best(lg[:, :, 0:N_GRP], N_GRP, small["gtop"], goh[:])
                dve.tensor_tensor(ge[:], lg[:, :, 0:N_GRP], per_token(small["gtop"], N_GRP), ALU.subtract).then_inc(shifted, 1)
                dve.tensor_scalar(pen[:].rearrange("p c (g e) -> p c g e", e=PER_GRP),
                                  goh[:].unsqueeze(3).broadcast_to([P, TC, N_GRP, PER_GRP]), 1.0, -NEG, ALU.subtract, ALU.mult)
                dve.drain()
                dve.tensor_tensor(el[:], lg[:, :, N_GRP:NL], pen[:], ALU.add)
                dve.drain()
                first_best(el[:], N_EXP, small["m1"], oh[0])
                dve.tensor_scalar(pen[:], oh[0], 2 * NEG, None, ALU.mult)
                dve.drain()
                dve.tensor_tensor(el[:], el[:], pen[:], ALU.add)
                dve.drain()
                first_best(el[:], N_EXP, small["m2"], oh[1])
                dve.tensor_tensor(chosen[:], oh[0], oh[1], ALU.add).then_inc(chosen_ready, 1)
                dve.tensor_tensor(small["d"][:], small["m2"][:], small["m1"][:], ALU.subtract).then_inc(shifted, 1)
                dve.wait_ge(risen, 2)
                dve.tensor_reduce(small["gsum"][:], ge[:], AX.X, ALU.add)
                dve.tensor_scalar(share[:, 0, :], small["d"][:], 1.0, None, ALU.add)
                dve.drain()
                dve.tensor_tensor(share[:, 0, :], share[:, 0, :], small["gsum"][:], ALU.mult)
                dve.drain()
                dve.reciprocal(share[:, 0, :], share[:, 0, :])
                dve.drain()
                dve.tensor_tensor(share[:, 1, :], share[:, 0, :], small["d"][:], ALU.mult)
                dve.wait_ge(counted, 1)
                counts = ps[1][:, 0:TC * N_EXP].rearrange("p (c n) -> p c n", n=N_EXP)
                dve.tensor_tensor(place[:], counts, k.const("expert_row").unsqueeze(1).broadcast_to([P, TC, N_EXP]), ALU.add)
                dve.tensor_reduce(mostf[:], ps[2][:, 0:N_EXP], AX.X, ALU.max)
                for s in range(2):
                    dve.tensor_tensor(el[:], oh[s], counts, ALU.mult)
                    dve.drain()
                    dve.tensor_reduce(earlier[:, s, :], el[:], AX.X, ALU.add)
                    dve.drain()
                for s in range(2):
                    dve.tensor_tensor(oh[s], oh[s], place[:], ALU.mult)
                dve.tensor_tensor(later[:], earlier[:].unsqueeze(3).broadcast_to([P, 2, TC, PASSES - 1]),
                                  k.const("pass_start").unsqueeze(1).unsqueeze(1).broadcast_to([P, 2, TC, PASSES - 1]), ALU.is_ge)
                dve.tensor_copy(most[:], mostf[:])
                dve.drain()
                dve.tensor_reduce(rows[:], ohs[:], AX.X, ALU.add)
                dve.tensor_reduce(passed[:], later[:], AX.X, ALU.add)
                dve.drain()
                dve.scalar_tensor_tensor(out=row_of, in0=passed[:], scalar=float((N_EXP - 1) * SLOTS), in1=rows[:],
                                         op0=ALU.mult, op1=ALU.add)


class Experts:

    def __init__(self, k, ctx, weights_ctx, tag, nth, F, up_parts, down):
        self.nth = nth
        self.k, self.tag, self.F, self.FC, self.NU = k, tag, F, F // P, len(up_parts)
        self.up_v = up_parts
        self.down_v = down
        self.row_of = k.sb(ctx, f"{tag}_row_of", [P, 2, TC], U32)
        self.share = k.sb(ctx, f"{tag}_share", [P, 2, TC])
        self.most = k.sb(ctx, f"{tag}_most", [P, 1], I32)
        self.u_sets, self.d_sets = ([2], 2) if self.NU == 1 else ([2, 1], 1)
        self.wu = [[[k.sb(weights_ctx, f"{tag}_wu{u}{b}{e}", [P, KC, 512]) for e in range(2)] for b in range(self.u_sets[u])]
                   for u in range(self.NU)]
        self.wd = [[k.sb(weights_ctx, f"{tag}_wd{b}{e}", [P, self.FC, D]) for e in range(2)] for b in range(self.d_sets)]
        self.u_loaded = [[[k.sem(weights_ctx, f"{tag}_u_loaded{u}{b}{e}") for e in range(2)] for b in range(self.u_sets[u])]
                         for u in range(self.NU)]
        self.d_loaded = [[k.sem(weights_ctx, f"{tag}_d_loaded{b}{e}") for e in range(2)] for b in range(self.d_sets)]

    def load_up(self, sp, m, u, b):
        for e in range(2):
            sp.dma_start(self.wu[u][b][e][:], self.up_v[u][m * 2 + e]).then_inc(self.u_loaded[u][b][e], 16)

    def load_down(self, sp, m, b):
        for e in range(2):
            sp.dma_start(self.wd[b][e][:], self.down_v[m * 2 + e]).then_inc(self.d_loaded[b][e], 16)

    def load_first(self):
        with self.k.nc.Block() as block:
            @block.sync
            def _(sp):
                for m in range(2):
                    for u in range(self.NU):
                        if m < self.u_sets[u]:
                            self.load_up(sp, m, u, m)
                    if m < self.d_sets:
                        self.load_down(sp, m, m)

    def run(self, rows, scale, shift):
        k, tag, F, FC, NU, most = self.k, self.tag, self.F, self.FC, self.NU, self.most
        wu, wd, u_loaded, d_loaded = self.wu, self.wd, self.u_loaded, self.d_loaded
        nc, u_sets, d_sets = k.nc, self.u_sets, self.d_sets
        S2 = 2 * SLOTS
        LAST_UP = f"up_done{NU - 1}"
        with ExitStack() as ctx:
            xg = k.hT[:, 0:2, :].rearrange("p a b -> p (a b)")
            zeros = k.hT[0:SLOTS, 2:4, :].rearrange("p a b -> p (a b)")
            hg = k.sb(ctx, f"{tag}_hg", [P, KC, S2])
            sig = k.sb(ctx, f"{tag}_sig", [P, F])
            mid = k.sb(ctx, f"{tag}_mid", [P, F])
            midT = k.sb(ctx, f"{tag}_midT", [P, FC, S2])
            res = k.sb(ctx, f"{tag}_res", [P, D])
            x_ps = k.banks(ctx, f"{tag}_x_ps", 2)
            mid_ps, = k.banks(ctx, f"{tag}_mid_ps", 1)
            up_ps = k.banks(ctx, f"{tag}_up_ps", NU)
            res_ps = k.banks(ctx, f"{tag}_res_ps", 2)
            names = ("zeros_ready x_loaded x_turned hg_ready up_done0 up_done1 sig_ready mid_ready mid_turned "
                     "midT_ready down_done res_ready res_stored").split()
            S = {n: k.sem(ctx, f"{tag}_{n}") for n in names}
            sent, zeroed = k.dma_sems["sent"], k.dma_sems[f"{tag}_zeroed"]

            def over_pairs(eng, begin, step):
                def of_pass(j, first):
                    n, half = j * PAIRS, j * (PAIRS // 2)
                    begin(j, n)
                    step(0, j, n, 0, half, first, True)
                    step(1, j, n + 1, 1, half, False, True)
                    with eng.Fori(1, PAIRS // 2 - 1) as it:
                        step(it * 2, j, n + it * 2, 0, half + it, False, True)
                        step(it * 2 + 1, j, n + (it * 2 + 1), 1, half + it, False, True)
                    step(PAIRS - 2, j, n + (PAIRS - 2), 0, half + (PAIRS // 2 - 1), False, True)
                    step(PAIRS - 1, j, n + (PAIRS - 1), 1, half + (PAIRS // 2 - 1), False, False)

                of_pass(0, True)
                busiest = eng.value_load(most[0:1, 0:1], min_val=0, max_val=SEQ)
                with eng.If(busiest > SLOTS):
                    with eng.Fori(1, PASSES) as j:
                        of_pass(j, False)

            def of_pair(rows):
                return rows.rearrange("j (m e) s d -> j m (e s) d", e=2)

            def loads(sets, n, half):
                return (half if sets == 2 else n) * 16 + 16

            with nc.Block() as block:
                @block.sync
                def _(sp):
                    def load_rows(m, j):
                        sp.dma_start(xg, of_pair(k.sent)[j, m]).then_inc(S["x_loaded"], 16)

                    def begin(j, n):
                        if isinstance(j, int):
                            sp.wait_ge(sent, 16 * 2 * TC * (self.nth + 1))
                        else:
                            sp.wait_ge(S["x_turned"], n)
                        load_rows(0, j)

                    def step(m, j, n, b, half, first, more):
                        def sent_before(sets):
                            return isinstance(j, int) and isinstance(m, int) and m < sets

                        for u in range(NU):
                            if not sent_before(u_sets[u]):
                                sp.wait_ge(S[f"up_done{u}"], n - (u_sets[u] - 1))
                                self.load_up(sp, m, u, b % u_sets[u])
                        if more:
                            sp.wait_ge(S["x_turned"], n + 1)
                            load_rows(m + 1, j)
                        if not sent_before(d_sets):
                            sp.wait_ge(S["down_done"], n - (d_sets - 1))
                            self.load_down(sp, m, b % d_sets)

                    over_pairs(sp, begin, step)

                @block.gpsimd
                def _(pool):
                    busiest = pool.value_load(most[0:1, 0:1], min_val=0, max_val=SEQ)
                    with pool.If(busiest > SLOTS):
                        pool.memset(zeros, 0.0).then_inc(S["zeros_ready"], 1)
                        pool.wait_ge(S["zeros_ready"], 1)
                        for j in range(1, PASSES):
                            pool.dma_start(k.sent[j].rearrange("e s d -> s e d"),
                                           zeros.unsqueeze(1).broadcast_to([SLOTS, N_EXP, D])).then_inc(zeroed, 16)
                        pool.wait_ge(zeroed, 16 * (PASSES - 1))
                    for c in range(TC):
                        for s in range(2):
                            pool.indirect_dma_start(k.sent.rearrange("j e s d -> (j e s) d"),
                                                    bass.IndirectOffsetOnAxis(ap=self.row_of[:, s, c:c + 1], axis=0),
                                                    rows[:, c, :], None).then_inc(sent, 16)

                @block.tensor
                def _(pe):
                    def turn_rows(n):
                        pe.wait_ge(S["x_loaded"], n * 16 + 16)
                        for kc in range(KC):
                            last = pe.transpose(x_ps[kc // 4][:, kc % 4 * P:(kc % 4 + 1) * P], xg[:, kc * P:(kc + 1) * P], k.const("ident"))
                        last.then_inc(S["x_turned"], 1)

                    def begin(j, n):
                        turn_rows(n)

                    def step(m, j, n, b, half, first, more):
                        pe.wait_ge(S["hg_ready"], n + 1)
                        for u in range(NU):
                            for e in range(2):
                                pe.wait_ge(u_loaded[u][b % u_sets[u]][e], loads(u_sets[u], n, half))
                            if u == 0 and not first:
                                pe.wait_ge(S["mid_ready"], n)
                            for kc in range(KC):
                                for e in range(2):
                                    last = pe.matmul(up_ps[u][e * SLOTS:(e + 1) * SLOTS, :], hg[:, kc, e * SLOTS:(e + 1) * SLOTS],
                                                     wu[u][b % u_sets[u]][e][:, kc, :], start=(kc == 0), stop=(kc == KC - 1))
                            last.then_inc(S[f"up_done{u}"], 1)
                        if more:
                            turn_rows(n + 1)
                        pe.wait_ge(S["mid_ready"], n + 1)
                        for f in range(FC):
                            last = pe.transpose(mid_ps[:, f * P:(f + 1) * P], mid[:, f * P:(f + 1) * P], k.const("ident"))
                        last.then_inc(S["mid_turned"], 1)
                        pe.wait_ge(S["midT_ready"], n + 1)
                        for e in range(2):
                            pe.wait_ge(d_loaded[b % d_sets][e], loads(d_sets, n, half))
                        if not first:
                            pe.wait_ge(S["res_ready"], n)
                        for side in range(2):
                            for f in range(FC):
                                for e in range(2):
                                    last = pe.matmul(res_ps[side][e * SLOTS:(e + 1) * SLOTS, :], midT[:, f, e * SLOTS:(e + 1) * SLOTS],
                                                     wd[b % d_sets][e][:, f, side * 512:(side + 1) * 512], start=(f == 0), stop=(f == FC - 1))
                        last.then_inc(S["down_done"], 1)

                    over_pairs(pe, begin, step)

                @block.scalar
                def _(act):
                    def modulated(n, first):
                        act.wait_ge(S["x_turned"], n + 1)
                        if not first:
                            act.wait_ge(S[LAST_UP], n)
                        for kc in range(KC):
                            last = act.activation(hg[:, kc, :], x_ps[kc // 4][:, kc % 4 * P:(kc % 4 + 1) * P], ACT.Identity,
                                                  scale=scale[:, kc:kc + 1], bias=shift[:, kc:kc + 1])
                        last.then_inc(S["hg_ready"], 1)

                    def begin(j, n):
                        modulated(n, isinstance(j, int))

                    def step(m, j, n, b, half, first, more):
                        act.wait_ge(S["up_done0"], n + 1)
                        if not first:
                            act.wait_ge(S["mid_ready"], n)
                        act.activation(sig[:], up_ps[0][:, 0:F], ACT.Sigmoid).then_inc(S["sig_ready"], 1)
                        if more:
                            modulated(n + 1, False)
                        act.wait_ge(S["down_done"], n + 1)
                        if not first:
                            act.wait_ge(S["res_stored"], n * 16)
                        for side in range(2):
                            last = act.activation(res[:, side * 512:(side + 1) * 512], res_ps[side][:, :], ACT.Copy)
                        last.then_inc(S["res_ready"], 1)
                        act.wait_ge(S["res_ready"], n + 1)
                        act.dma_start(of_pair(k.results)[j, m], res[:]).then_inc(S["res_stored"], 16)
                        if not more:
                            act.wait_ge(S["res_stored"], n * 16 + 16)

                    over_pairs(act, begin, step)

                @block.vector
                def _(dve):
                    def step(m, j, n, b, half, first, more):
                        dve.wait_ge(S["sig_ready"], n + 1)
                        dve.tensor_tensor(sig[:], sig[:], up_ps[0][:, 0:F], ALU.mult)
                        dve.drain()
                        dve.wait_ge(S[LAST_UP], n + 1)
                        if not first:
                            dve.wait_ge(S["mid_turned"], n)
                        gate_ps = up_ps[1][:, :] if NU == 2 else up_ps[0][:, F:2 * F]
                        dve.tensor_tensor(mid[:], sig[:], gate_ps, ALU.mult).then_inc(S["mid_ready"], 1)
                        dve.wait_ge(S["mid_turned"], n + 1)
                        if not first:
                            dve.wait_ge(S["down_done"], n)
                        dve.tensor_copy(midT[:].rearrange("p f s -> p (f s)"), mid_ps[:, 0:FC * P]).then_inc(S["midT_ready"], 1)

                    over_pairs(dve, lambda j, n: None, step)

    def add(self, gate, plus, residual, send_next=None):
        k, tag, share = self.k, self.tag, self.share
        with ExitStack() as ctx:
            gain = k.sb(ctx, f"{tag}_gain", [P, D])
            y = [k.sb(ctx, f"{tag}_y{s}", [P, TC, D]) for s in range(2)]
            fetched = [[k.dma_sems[f"fetched{c}{s}"] for s in range(2)] for c in range(TC)]
            here = 16 * (self.nth + 1)
            weighted = k.sem(ctx, f"{tag}_weighted")
            ps = k.banks(ctx, f"{tag}_gain_ps", 2)
            gain_turned = k.sem(ctx, f"{tag}_gain_turned")
            with k.nc.Block() as block:
                @block.gpsimd
                def _(pool):
                    def fetch(results):
                        for c in range(TC):
                            for s in range(2):
                                pool.indirect_dma_start(y[s][:, c, :], None, results,
                                                        bass.IndirectOffsetOnAxis(ap=self.row_of[:, s, c:c + 1], axis=0)).then_inc(fetched[c][s], 16)

                    busiest = pool.value_load(self.most[0:1, 0:1], min_val=0, max_val=SEQ)
                    with pool.If(busiest > SLOTS):
                        fetch(k.results.rearrange("j e s d -> (j e s) d"))
                    with pool.Else():
                        fetch(k.results[0].rearrange("e s d -> (e s) d"))

                @block.sync
                def _(sp):
                    if send_next:
                        for c in range(TC):
                            for s in range(2):
                                sp.wait_ge(fetched[c][s], here)
                        send_next(sp)

                @block.tensor
                def _(pe):
                    for j in range(KC):
                        last = pe.transpose(ps[j // 4][:, j % 4 * P:(j % 4 + 1) * P], gate[:, j:j + 1].broadcast_to([P, P]), k.const("ident"))
                    last.then_inc(gain_turned, 1)

                @block.scalar
                def _(act):
                    for c in range(TC):
                        act.wait_ge(fetched[c][0], here)
                        act.activation(y[0][:, c, :], y[0][:, c, :], ACT.Copy, scale=share[:, 0, c:c + 1]).then_inc(weighted, 1)

                @block.vector
                def _(dve):
                    dve.wait_ge(gain_turned, 1)
                    for h in range(2):
                        dve.tensor_scalar(gain[:, h * 512:(h + 1) * 512], ps[h][:, :], float(plus), None, ALU.add)
                    for c in range(TC):
                        dve.wait_ge(fetched[c][1], here)
                        dve.wait_ge(weighted, c + 1)
                        dve.scalar_tensor_tensor(out=y[1][:, c, :], in0=y[1][:, c, :], scalar=share[:, 1, c:c + 1], in1=y[0][:, c, :],
                                                 op0=ALU.mult, op1=ALU.add)
                        dve.drain()
                        dve.tensor_tensor(y[1][:, c, :], y[1][:, c, :], gain[:], ALU.mult)
                        dve.drain()
                        dve.scalar_tensor_tensor(out=k.x[:, c, :], in0=k.x[:, c, :], scalar=float(residual), in1=y[1][:, c, :],
                                                 op0=ALU.mult, op1=ALU.add)


def first_mix_end(k, ohT, onT, mergedT, first_slices):
    with ExitStack() as ctx:
        weights = OutWeights(k, ctx, "mix_out", k.i["w_out"])
        merge_branches(k, ohT, onT, mergedT, first_slices, weights.send)
        project_out(k, "mix_out", weights, mergedT, k.mod[:, 2 * KC:3 * KC], 1.0, ALPHA)


def affine_norm(k, tag):
    normalize(k, tag, 1e-5, gain=k.col(f"{tag}_g", 0, 8), shift=k.col(f"{tag}_b", 0, 8), out=k.x)


def first_experts(k):
    with ExitStack() as ctx:
        with ExitStack() as weights_ctx:
            layer = Experts(k, ctx, weights_ctx, "moe1", 0, F1, [k.i["exp_up"], k.i["exp_gate"]], k.i["exp_down"])
            layer.load_first()
            affine_norm(k, "ln1")
            normalize(k, "ln1h", 1e-5)
            transposed(k, "h2", k.scale_ffn, k.mod[:, 3 * KC:4 * KC])
            route(k, "route1", k.w_router, k.row("router_b"), layer.row_of[:], layer.share[:], layer.most)
            layer.run(k.xn, k.scale_ffn, k.mod[:, 3 * KC:4 * KC])
        second = Modulation(k, ctx, "mod2", k.i["ada_w_2"])
        layer.add(k.mod[:, 5 * KC:6 * KC], 1.0, ALPHA, second.load_first)
        affine_norm(k, "ln2")
        normalize(k, "rms0", 1e-6, root_mean_square=True)
        second.run(k.col("c_2", 0, 8), k.col("b_ada_2", 0, 48), k.mod, (k.col("norm_mix_g_2", 0, 8), k.col("norm_ffn_g_2", 0, 8)))


def second_experts(k):
    with ExitStack() as ctx:
        with ExitStack() as weights_ctx:
            layer = Experts(k, ctx, weights_ctx, "moe2", 1, F2, [k.i["exp_in_2"]], k.i["exp_down_2"])
            layer.load_first()
            normalize(k, "rms1", 1e-6, root_mean_square=True)
            transposed(k, "rms1T", k.scale_ffn, k.mod[:, 3 * KC:4 * KC])
            route(k, "route2", k.w_router_2, k.row("router_b_2"), layer.row_of[:], layer.share[:], layer.most)
            layer.run(k.xn, k.scale_ffn, k.mod[:, 3 * KC:4 * KC])
        layer.add(k.mod[:, 5 * KC:6 * KC], 0.0, 1.0)


def second_mix(k):
    with ExitStack() as outer:
        catT = k.sb(outer, "mx2_catT", [P, KC, SEQ])
        weights = OutWeights(k, outer, "mx2_out", k.i["w_out_2"])
        with ExitStack() as ctx:
            qk = k.sb(ctx, "mx2_qk", [P, 2, HEADS, SEQ])
            v_tok = k.sb(ctx, "mx2_v", [P, TC, 512])
            u = k.sb(ctx, "mx2_u", [P, 4, SEQ])
            with ExitStack() as early:
                slices = SlicesAhead(k, early, "p2", 2, lambda n: k.i["w_qku_2"][n])
                transposed(k, "rms0T", k.scale_mix, k.mod[:, 0:KC], slices.send)
                project_second(k, qk, v_tok, u, catT, slices)
            forgetting(k, qk, v_tok, catT, weights.send)
        project_out(k, "mx2_out", weights, catT, k.mod[:, 2 * KC:3 * KC], 0.0, 1.0)


def project_second(k, qk, v_tok, u, catT, first_slices):
    nc = k.nc
    G = len(POOL_WINDOWS)
    NV = 512 + HEADS
    with ExitStack() as ctx:
        w, w_loaded = first_slices.w, first_slices.loaded
        wv = k.sb(ctx, "p2_wv", [P, KC, NV])
        z = {n: k.sb(ctx, f"p2_{n}", [P, TC, HEADS]) for n in ("f", "low", "mag", "logf")}
        F = k.sb(ctx, "p2_F", [HEADS, SEQ])
        nF = k.sb(ctx, "p2_nF", [HEADS, SEQ])
        ps = k.banks(ctx, "p2_ps", 2)
        psv = k.banks(ctx, "p2_psv", 2)
        pool_ps = k.banks(ctx, "po_ps", 2)
        psf, = k.banks(ctx, "p2_psf", 1)
        psF, = k.banks(ctx, "p2_psF", 1)
        names = "wv_loaded projected kept v_projected v_kept f_projected mag_ready exp_ready ln_ready logf_ready summed F_ready cleared rows_set".split()
        S = {n: k.sem(ctx, "p2_" + n) for n in names}
        NCH = 12
        w_pool = k.sb(ctx, "po_w", [P, G, P])
        sums = k.sb(ctx, "po_sums", [P, G, SEQ])
        diff = k.sb(ctx, "po_diff", [P, G, SEQ])
        pool_loaded = k.sem(ctx, "po_loaded")
        diff_ready = k.sem(ctx, "po_diff_ready")
        pooled = k.sem(ctx, "po_pooled")
        pool_kept = k.sem(ctx, "po_kept")
        with nc.Block() as block:
            @block.sync
            def _(sp):
                sp.dma_start(wv[:], k.i["w_vf_2"].rearrange("(k p) n -> p k n", p=P)).then_inc(S["wv_loaded"], 16)
                with sp.Fori(1, NCH // 2) as it:
                    for s in range(2):
                        sp.wait_ge(S["projected"], it * 2 + (s - 1))
                        sp.dma_start(w[s], k.i["w_qku_2"][it * 2 + s]).then_inc(w_loaded[s], 16)
                sp.dma_start(w_pool[:], k.i["w_pool_2"].rearrange("g c d -> c g d")).then_inc(pool_loaded, 16)
                sp.wait_ge(S["F_ready"], 2)
                sp.wait_ge(S["kept"], NCH)
                for h in range(HEADS):
                    at = DH2 * (1 - h % 2)
                    ones = k.const("ones")[0:1, :].unsqueeze(1).broadcast_to([1, TC, P])
                    for side, row, other in ((0, F, 1), (1, nF, 0)):
                        sp.dma_start(qk[at + side:at + side + 1, side, h, :], row[h:h + 1, :]).then_inc(S["rows_set"], 16)
                        sp.dma_start(qk[at + other:at + other + 1, side, h, :], ones).then_inc(S["rows_set"], 16)
                sp.wait_ge(S["rows_set"], 16 * 4 * HEADS)

            @block.tensor
            def _(pe):
                def feature_major(it, s, first):
                    pe.wait_ge(w_loaded[s], it * 16 + 16)
                    if not first:
                        pe.wait_ge(S["kept"], it * 2 + (s - 1))
                    for kc in range(KC):
                        last = pe.matmul(ps[s][:, :], w[s][:, kc, :], k.hT[:, kc, :], start=(kc == 0), stop=(kc == KC - 1))
                    last.then_inc(S["projected"], 1)

                for s in range(2):
                    feature_major(0, s, True)
                pe.wait_ge(S["wv_loaded"], 16)
                for c in range(TC):
                    for kc in range(KC):
                        last = pe.matmul(psf[:, c * HEADS:(c + 1) * HEADS], k.hT[:, kc, c * P:(c + 1) * P], wv[:, kc, 512:NV],
                                         start=(kc == 0), stop=(kc == KC - 1))
                last.then_inc(S["f_projected"], 1)
                with pe.Fori(1, NCH // 2) as it:
                    for s in range(2):
                        feature_major(it, s, False)
                pe.wait_ge(S["logf_ready"], 1)
                for c in range(TC):
                    at = BT0 - c * P
                    last = pe.matmul(psF[0:HEADS, :], z["logf"][:, c, :], k.const("upto")[:, at:at + SEQ], start=(c == 0), stop=(c == TC - 1))
                last.then_inc(S["summed"], 1)
                for c in range(TC):
                    if c >= 2:
                        pe.wait_ge(S["v_kept"], c - 1)
                    for kc in range(KC):
                        last = pe.matmul(psv[c % 2][:, :], k.hT[:, kc, c * P:(c + 1) * P], wv[:, kc, 0:512],
                                         start=(kc == 0), stop=(kc == KC - 1))
                    last.then_inc(S["v_projected"], 1)
                pe.wait_ge(pool_loaded, 16)
                pe.wait_ge(diff_ready, 1)
                for g in range(G):
                    if g >= 2:
                        pe.wait_ge(pool_kept, g - 1)
                    pe.matmul(pool_ps[g % 2][:, :], w_pool[:, g, :], diff[:, g, :], start=True, stop=True).then_inc(pooled, 1)

            @block.scalar
            def _(act):
                act.wait_ge(S["mag_ready"], 1)
                act.activation(z["mag"][:], z["mag"][:], ACT.Exp, scale=-1.0).then_inc(S["exp_ready"], 1)
                act.wait_ge(S["exp_ready"], 1)
                act.activation(z["mag"][:], z["mag"][:], ACT.Ln, bias=1.0).then_inc(S["ln_ready"], 1)
                for c in range(TC):
                    act.wait_ge(S["v_projected"], c + 1)
                    act.activation(v_tok[:, c, :], psv[c % 2][:, :], ACT.Copy).then_inc(S["v_kept"], 1)

            @block.vector
            def _(dve):
                for j in range(NCH):
                    dve.wait_ge(S["projected"], j + 1)
                    if j < 8:
                        side, scale = (0, DH2 ** -0.5) if j < 4 else (1, 1.0)
                        for half in range(2):
                            last = dve.tensor_scalar(qk[:, side, 2 * (j % 4) + half, :], ps[j % 2][:, :],
                                                     k.const("half")[:, half:half + 1], scale, ALU.mult, ALU.mult)
                    else:
                        last = dve.tensor_copy(u[:, j - 8, :], ps[j % 2][:, :])
                    last.then_inc(S["kept"], 1)
                    if j == 1:
                        dve.wait_ge(S["f_projected"], 1)
                        dve.tensor_tensor(z["f"][:], psf[:, 0:TC * HEADS].rearrange("p (c h) -> p c h", h=HEADS),
                                          k.row("b_fgate_2").unsqueeze(1).broadcast_to([P, TC, HEADS]), ALU.add)
                        dve.drain()
                        dve.tensor_scalar(z["low"][:], z["f"][:], -1.0, None, ALU.mult)
                        dve.drain()
                        dve.tensor_tensor(z["mag"][:], z["f"][:], z["low"][:], ALU.max).then_inc(S["mag_ready"], 1)
                        dve.drain()
                        dve.tensor_scalar(z["low"][:], z["f"][:], 0.0, None, ALU.min)
                        dve.drain()
                        dve.wait_ge(S["ln_ready"], 1)
                        dve.tensor_tensor(z["logf"][:], z["low"][:], z["mag"][:], ALU.subtract).then_inc(S["logf_ready"], 1)
                dve.wait_ge(S["summed"], 1)
                dve.tensor_copy(F[:], psF[0:HEADS, :]).then_inc(S["F_ready"], 1)
                dve.tensor_scalar(nF[:], psF[0:HEADS, :], -1.0, None, ALU.mult).then_inc(S["F_ready"], 1)
                dve.drain()
                for g in range(G):
                    dve.tensor_tensor_scan(sums[:, g, :], k.const("ones", 0, 1).broadcast_to([P, SEQ]), u[:, g, :], 0.0, ALU.mult, ALU.add)
                dve.drain()
                for g, win in enumerate(POOL_WINDOWS):
                    dve.tensor_copy(diff[:, g, 0:win], sums[:, g, 0:win])
                    dve.tensor_tensor(diff[:, g, win:SEQ], sums[:, g, win:SEQ], sums[:, g, 0:SEQ - win], ALU.subtract)
                dve.drain()
                for g, win in enumerate(POOL_WINDOWS):
                    dve.tensor_tensor(diff[:, g, 0:16], diff[:, g, 0:16], k.const("pool_inv", 16 * g, 16 * g + 16), ALU.mult)
                    dve.tensor_scalar(diff[:, g, 16:SEQ], diff[:, g, 16:SEQ], 1.0 / win, None, ALU.mult)
                dve.drain()
                dve.tensor_tensor(diff[:], diff[:], u[:], ALU.subtract).then_inc(diff_ready, 1)
                for g in range(G):
                    dve.wait_ge(pooled, g + 1)
                    dve.tensor_scalar(catT[:, 4 + g, :], pool_ps[g % 2][:, :], k.col("pool_scale_2", g), None, ALU.mult).then_inc(pool_kept, 1)


def forgetting(k, qk, v_tok, catT, send_next):
    nc = k.nc
    units = [(m, c, e) for m in range(HEADS // 2) for c in range(TC) for e in range(2)]
    PER = 2 * TC
    with ExitStack() as ctx:
        NP = 4
        p = [k.sb(ctx, f"fa_p{s}", [P, SEQ]) for s in range(NP)]
        pT = [k.sb(ctx, f"fa_pT{s}", [P, SEQ]) for s in range(2)]
        top, ntop, total, factor = (k.sb(ctx, f"fa_{n}", [P, PER]) for n in ("top", "ntop", "total", "factor"))
        sc = k.banks(ctx, "fa_sc", 3)
        tr = k.banks(ctx, "fa_tr", 2)
        o_ps = k.banks(ctx, "fa_o", 2)
        names = "scored logits_ready exp_ready p_ready turned pT_ready mixed o_kept".split()
        S = {n: k.sem(ctx, "fa_" + n) for n in names}

        with nc.Block() as block:
            @block.sync
            def _(sp):
                send_next(sp)

            @block.tensor
            def _(pe):
                def scores(i):
                    m, c, e = units[i]
                    if i >= 3:
                        pe.wait_ge(S["logits_ready"], i - 2)
                    h = 2 * m + e
                    pe.matmul(sc[i % 3][:, 0:(c + 1) * P], qk[:, 0, h, c * P:(c + 1) * P], qk[:, 1, h, 0:(c + 1) * P],
                              start=True, stop=True).then_inc(S["scored"], 1)

                def turn(i):
                    pe.wait_ge(S["p_ready"], i + 1)
                    if i >= 2:
                        pe.wait_ge(S["pT_ready"], i - 1)
                    for kk in range(units[i][1] + 1):
                        last = pe.transpose(tr[i % 2][:, kk * P:(kk + 1) * P], p[i % NP][:, kk * P:(kk + 1) * P], k.const("ident"))
                    last.then_inc(S["turned"], 1)

                def mix(i):
                    m, c, e = units[i]
                    pe.wait_ge(S["pT_ready"], i + 1)
                    if i % PER == 0 and m >= 2:
                        pe.wait_ge(S["o_kept"], m - 1)
                    for kk in range(c + 1):
                        last = pe.matmul(o_ps[m % 2][e * DH2:(e + 1) * DH2, c * P:(c + 1) * P],
                                         v_tok[:, kk, (2 * m + e) * DH2:(2 * m + e + 1) * DH2],
                                         pT[i % 2][:, kk * P:(kk + 1) * P], start=(c == 0), stop=False, skip_group_check=True)
                    last.then_inc(S["mixed"], 1)

                for i in range(3):
                    scores(i)
                for i in range(len(units)):
                    turn(i)
                    if i + 3 < len(units):
                        scores(i + 3)
                    if i:
                        mix(i - 1)
                mix(len(units) - 1)

            @block.scalar
            def _(act):
                def weights(i):
                    n, u = (units[i][1] + 1) * P, i % PER
                    act.wait_ge(S["logits_ready"], i + 1)
                    act.activation(p[i % NP][:, 0:n], p[i % NP][:, 0:n], ACT.Exp, bias=ntop[:, u:u + 1],
                                   accum_out=total[:, u:u + 1]).then_inc(S["exp_ready"], 1)

                def keep_turned(i):
                    n = (units[i][1] + 1) * P
                    act.wait_ge(S["turned"], i + 1)
                    if i >= 2:
                        act.wait_ge(S["mixed"], i - 1)
                    act.activation(pT[i % 2][:, 0:n], tr[i % 2][:, 0:n], ACT.Copy).then_inc(S["pT_ready"], 1)

                for i in range(len(units) + 2):
                    if i < len(units):
                        weights(i)
                    if i >= 2:
                        keep_turned(i - 2)

            @block.vector
            def _(dve):
                def logits(i):
                    n, u = (units[i][1] + 1) * P, i % PER
                    dve.wait_ge(S["scored"], i + 1)
                    if i >= NP:
                        dve.wait_ge(S["turned"], i - NP + 1)
                    dve.tensor_tensor_reduce(p[i % NP][:, 0:n], sc[i % 3][:, 0:n], k.const("causal2", SEQ - n, SEQ), 1.0, NEG * 10,
                                             ALU.add, ALU.max, top[:, u:u + 1])
                    dve.drain()
                    dve.tensor_scalar(ntop[:, u:u + 1], top[:, u:u + 1], -1.0, None, ALU.mult).then_inc(S["logits_ready"], 1)

                def normalized(i):
                    n, u = (units[i][1] + 1) * P, i % PER
                    dve.wait_ge(S["exp_ready"], i + 1)
                    dve.reciprocal(factor[:, u:u + 1], total[:, u:u + 1])
                    dve.drain()
                    dve.tensor_scalar(p[i % NP][:, 0:n], p[i % NP][:, 0:n], factor[:, u:u + 1], None, ALU.mult).then_inc(S["p_ready"], 1)

                def keep_output(m):
                    dve.wait_ge(S["mixed"], (m + 1) * PER)
                    dve.tensor_copy(catT[:, m, :], o_ps[m % 2][:, :]).then_inc(S["o_kept"], 1)

                for i in range(len(units) + 1):
                    if i < len(units):
                        logits(i)
                    if i:
                        normalized(i - 1)
                    if i > PER and i % PER == 4:
                        keep_output(i // PER - 1)
                keep_output(HEADS // 2 - 1)


def program(nc, inputs, out):
    with ExitStack() as ctx:
        k = Kit(nc, inputs, out)
        persistent(k, ctx)

        first = ctx.enter_context(ExitStack())
        k.lb = k.sb(first, "hg_lb", [P, HEADS])
        k.hg_v_bias = k.sb(first, "hg_v_bias", [P, D])
        k.kv_v_bias = k.sb(first, "kv_v_bias", [P, 4 * P])
        with ExitStack() as early:
            modulation = Modulation(k, early, "mod1", inputs["ada_w"])
            load_constants(k, modulation)
            normalize(k, "ln0", 1e-5)
            lower_bound_layer(k, k.lb)
            broadcast_rows(k, "v_biases", [(k.col("b_in", 16, 8), k.hg_v_bias, 0.0), (k.col("b_in", 46, 2), k.kv_v_bias[:, 0:256], 0.0),
                                           (k.col("b_in", 50, 2), k.kv_v_bias[:, 256:512], 0.0)])
            modulation.run(k.col("c", 0, 8), k.col("ada_b", 0, 48), k.mod)
        with ExitStack() as mix:
            ohT = k.sb(mix, "ohT", [P, KC, SEQ])
            squares = k.sb(mix, "oh_squares", [P, HEADS, TC])
            onT = k.sb(mix, "onT", [P, KC, SEQ])
            first_merge = SlicesAhead(k, mix, "mg", 4, lambda n: k.i["w_merge"][0, n], inside=k.xn)
            with ExitStack() as mixers:
                ahead = KeyWeights(k, mixers)
                with ExitStack() as rec:
                    slices = SlicesAhead(k, rec, "hg", 4, lambda n: k.i["w_hg"][0, n])
                    transposed(k, "h1", k.scale_mix, k.mod[:, 0:KC], slices.send)
                    recurrence(k, ohT, squares, slices, ahead.slices.send)
                sparse_attention(k, onT, ahead, ohT, squares, first_merge.send)
            mergedT = k.sb(mix, "mergedT", [P, KC, SEQ])
            first_mix_end(k, ohT, onT, mergedT, first_merge)
        first.close()
        first_experts(k)

        second_mix(k)
        second_experts(k)
        normalize(k, "final", 1e-6, root_mean_square=True, gain=k.col("norm_final_g_2", 0, 8), out=k.x, store=out)


def _columns(v):
    return np.asarray(v, np.float32).reshape(-1, P).T


def arrange(x, c, ada_w, ada_b, w_in, b_in, hg_lb_logits, hg_norm_w, cmp_pos_k, cmp_w1_k, cmp_b1_k, cmp_w2_k,
            cmp_pos_v, cmp_w1_v, cmp_b1_v, cmp_w2_v, rel_bias, w_br_hg, w_br_nsa, w_out, ln1_g, ln1_b,
            router_grp_w, router_grp_b, router_exp_w, router_exp_b, exp_w1, exp_w3, exp_w2, ln2_g, ln2_b,
            c_2, norm_mix_g_2, norm_ffn_g_2, norm_final_g_2, w_ada_2, b_ada_2, w_in_2, b_fgate_2, w_pool_2,
            pool_scale_2, w_out_2, w_router_group_2, b_router_group_2, w_router_expert_2, b_router_expert_2,
            w_expert_gate_2, w_expert_up_2, w_expert_down_2):
    f = lambda a: np.ascontiguousarray(np.asarray(a))
    w_in, b_in = f(w_in)[0], f(b_in)[0]
    at = dict(hq=0, hf=1024, hv=2048, hg=3072, nq=4096, kc=5120, vc=5376, ks=5632, vs=5888, kw=6144, vw=6400,
              gate=6656, mgh=6680, mgn=7704)

    def chunks(w, a, n):
        return w[:, a:a + n * P].reshape(KC, P, n, P).transpose(2, 1, 0, 3)

    def by_row(w):
        n, rows, m = w.shape
        return w.reshape(n, rows // P, P, m).transpose(0, 2, 1, 3)

    def by_block(w):
        return w.reshape(KC, P, -1, 512).transpose(2, 1, 0, 3)

    vectors = dict(
        c=c, ada_b=ada_b, b_in=b_in[:at["gate"]], b_mg=b_in[at["mgh"]:], lb0=f(hg_lb_logits)[0],
        lb1=f(hg_lb_logits)[1], hg_norm_w=hg_norm_w, cmp_b1_k=cmp_b1_k, cmp_b1_v=cmp_b1_v, ln1_g=ln1_g, ln1_b=ln1_b, ln2_g=ln2_g, ln2_b=ln2_b, c_2=c_2, b_ada_2=b_ada_2,
        norm_mix_g_2=norm_mix_g_2, norm_ffn_g_2=norm_ffn_g_2, norm_final_g_2=norm_final_g_2,
        pool_scale_2=pool_scale_2)
    short = dict(b_gate=[b_in[at["gate"]:at["mgh"]]], router_b=[router_grp_b, router_exp_b],
                 router_b_2=[b_router_group_2, b_router_expert_2], b_fgate_2=[b_fgate_2])
    w2 = f(w_in_2)[0]
    out = dict(
        consts=np.concatenate([a for _, a in pack_consts()], 1),
        cols=np.concatenate([_columns(vectors[n]) for n, _ in pack_columns()], 1),
        rows=np.concatenate([f(v).reshape(-1) for n, _ in pack_rows() for v in short[n]]),
        buckets=bucket_rows(),
        x=f(x)[0], ada_w=by_block(f(ada_w)[0]),
        w_hg=np.stack([chunks(w_in, at[n], 8) for n in ("hq", "hf", "hg", "hv")], 1),
        w_nq=chunks(w_in, at["nq"], 8),
        w_kv=np.concatenate([chunks(w_in, at[n], 2) for n in ("kc", "vc", "ks", "kw")]),
        w_v=np.concatenate([w_in[:, at["vs"]:at["vs"] + 256], w_in[:, at["vw"]:at["vw"] + 256],
                            w_in[:, at["gate"]:at["mgh"]]], 1),
        w_cmp=np.stack([f(cmp_w1_k)[0], f(cmp_w1_v)[0]]), w_cmp2=np.stack([f(cmp_w2_k)[0], f(cmp_w2_v)[0]]),
        cmp_pos=np.stack([f(cmp_pos_k).reshape(CMP_BLOCK, P).T, f(cmp_pos_v).reshape(CMP_BLOCK, P).T]),
        rel_bias=f(rel_bias).T,
        w_merge=np.stack([chunks(w_in, at["mgh"], 8), chunks(w_in, at["mgn"], 8), chunks(f(w_br_hg)[0], 0, 8),
                          chunks(f(w_br_nsa)[0], 0, 8)], 1),
        w_out=by_block(f(w_out)[0]),
        w_router=np.concatenate([f(router_grp_w)[0], f(router_exp_w)[0]], 1),
        exp_up=by_row(f(exp_w1)[0]), exp_gate=by_row(f(exp_w3)[0]), exp_down=by_row(f(exp_w2)[0]),
        ada_w_2=by_block(f(w_ada_2)[0]),
        w_qku_2=np.concatenate([chunks(w2, 0, 8), chunks(w2, 1544, 4)]),
        w_vf_2=w2[:, 1024:1544],
        w_pool_2=f(w_pool_2)[0], w_out_2=by_block(f(w_out_2)[0]),
        w_router_2=np.concatenate([f(w_router_group_2)[0], f(w_router_expert_2)[0].transpose(1, 0, 2).reshape(D, N_EXP)], 1),
        exp_in_2=by_row(np.concatenate([f(w_expert_gate_2)[0].reshape(N_EXP, D, F2), f(w_expert_up_2)[0].reshape(N_EXP, D, F2)], 2)),
        exp_down_2=by_row(f(w_expert_down_2)[0].reshape(N_EXP, F2, D)),
    )
    return {n: np.ascontiguousarray(a) for n, a in out.items()}


def kernel(**inputs):
    from concourse import bacc
    from concourse.bass_utils import run_bass_kernel_spmd

    arrays = {f"in_{n}": a for n, a in arrange(**inputs).items()}
    nc = bacc.Bacc("TRN2", target_bir_lowering=False, num_devices=1)
    views = {n[3:]: nc.dram_tensor(n, a.shape, mybir.dt.from_np(a.dtype), kind="ExternalInput").ap() for n, a in arrays.items()}
    out = nc.dram_tensor("out_x", (SEQ, D), F32, kind="ExternalOutput").ap()
    program(nc, views, out)
    r = run_bass_kernel_spmd(nc, [arrays], core_ids=[0])
    return r.results[0]["out_x"].reshape(1, SEQ, D)
```
